# Optimizing a Trainium2 kernel written in Bass

```python
import jax, jax.numpy as jnp
from jax import lax
import numpy as np

D_MODEL = 1024
BATCH = 1
SEQ = 1024
DEPTH = 1
DEC_BATCH = 8
DEC_SEQ = 4
PAST_LEN = 2048
PAGE_SIZE = 128

H_A = 8
DH_A = 64
W_A = H_A * DH_A
Q_BLOCK = 128
H_B = 8
DH_B = 64
W_B = H_B * DH_B
DECAY_LORA = 64
AAA_LORA = 64
GATE_LORA = 128
GN_EPS = 64e-5
N_GROUPS = 4
EXPERTS_PER_GROUP = 8
N_EXPERTS = N_GROUPS * EXPERTS_PER_GROUP
TOP_K_IN_GROUP = 2
D_EXPERT = 256
ROUTE_BLOCK = 256
NORM_EPS = 1e-6

FOX_COLS = 3 * W_A + H_A
RW_COLS = 3 * W_B + DECAY_LORA + AAA_LORA + GATE_LORA
GATE_COLS = 2 * D_MODEL
IN_COLS = FOX_COLS + RW_COLS + GATE_COLS
FOX_SPLITS = (W_A, 2 * W_A, 3 * W_A)
RW_SPLITS = (W_B, 2 * W_B, 3 * W_B, 3 * W_B + DECAY_LORA, 3 * W_B + DECAY_LORA + AAA_LORA)

kernel_name = "fox_rwkv7_hier_moe_step"

def rmsnorm(x, g):
    x32 = x.astype(jnp.float32)
    y = x32 * lax.rsqrt(jnp.mean(x32 * x32, axis=-1, keepdims=True) + NORM_EPS)
    return (y * g).astype(x.dtype)

def fox_attend(q, k, v, c_q, c_k, q_pos, k_pos):
    s = jnp.einsum('bqhd,bkhd->bhqk', q, k).astype(jnp.float32) * (DH_A ** -0.5)
    s = s + jnp.transpose(c_q, (0, 2, 1))[..., :, None] - jnp.transpose(c_k, (0, 2, 1))[..., None, :]
    s = jnp.where(k_pos[None, :] <= q_pos[:, None], s, -jnp.inf)
    p = jax.nn.softmax(s, axis=-1)
    return jnp.einsum('bhqk,bkhd->bqhd', p.astype(v.dtype), v)

def fox_prompt(q, k, v, logf):
    B, T = q.shape[:2]
    nb = T // Q_BLOCK
    c = jnp.cumsum(logf, axis=1)
    k_pos = jnp.arange(T)
    qb = jnp.swapaxes(q.reshape(B, nb, Q_BLOCK, H_A, DH_A), 0, 1)
    cb = jnp.swapaxes(c.reshape(B, nb, Q_BLOCK, H_A), 0, 1)
    pb = k_pos.reshape(nb, Q_BLOCK)
    ob = lax.map(lambda a: fox_attend(a[0], k, v, a[1], c, a[2], k_pos), (qb, cb, pb))
    return jnp.swapaxes(ob, 0, 1).reshape(B, T, H_A, DH_A)

def fox_sample(q, k, v, logf, k_past, v_past, logf_past):
    past_len, T = k_past.shape[1], q.shape[1]
    k_all = jnp.concatenate([k_past.astype(k.dtype), k], axis=1)
    v_all = jnp.concatenate([v_past.astype(v.dtype), v], axis=1)
    c_all = jnp.cumsum(jnp.concatenate([logf_past.astype(jnp.float32), logf], axis=1), axis=1)
    q_pos = past_len + jnp.arange(T)
    k_pos = jnp.arange(past_len + T)
    return fox_attend(q, k_all, v_all, c_all[:, past_len:], c_all, q_pos, k_pos)

def gather_pages(pool, page_table):
    g = pool[page_table]
    return g.reshape(g.shape[0], g.shape[1] * g.shape[2], *g.shape[3:])

def _wkv_step(S, inp):
    r, d, k, v, kk, a = inp
    s_kk = jnp.einsum('bhvk,bhk->bhv', S, kk)
    S = S * d[:, :, None, :] - s_kk[..., None] * (kk * a)[:, :, None, :] + v[..., None] * k[:, :, None, :]
    return S, jnp.einsum('bhvk,bhk->bhv', S, r)

def rwkv_branch(u, shift_prev, wkv_prev, mu_rw, w0, w2, a0, a2, g2, k_k, k_a, r_k, lnx_w, lnx_b):
    B, T, _ = u.shape
    f32 = jnp.float32
    u_prev = jnp.concatenate([shift_prev[:, None, :].astype(u.dtype), u[:, :-1]], axis=1)
    us = u + mu_rw * (u_prev - u)
    r, k, v, wl, al, gl = jnp.split(us, RW_SPLITS, axis=-1)
    w = -jax.nn.softplus(-(w0 + jnp.tanh(wl) @ w2).astype(f32)) - 0.5
    decay = jnp.exp(-jnp.exp(w))
    a = jax.nn.sigmoid((a0 + al @ a2).astype(f32))
    g = jax.nn.sigmoid(gl) @ g2
    heads = lambda t: t.astype(f32).reshape(B, T, H_B, DH_B)
    kk = heads(k * k_k)
    kk = kk / jnp.maximum(jnp.sqrt(jnp.sum(kk * kk, axis=-1, keepdims=True)), 1e-12)
    k_mod = k.astype(f32) * (1.0 + (a - 1.0) * k_a)
    r_h, k_h, v_h, a_h, d_h = heads(r), heads(k_mod), heads(v), heads(a), heads(decay)
    xs = tuple(jnp.moveaxis(t, 1, 0) for t in (r_h, d_h, k_h, v_h, kk, a_h))
    wkv_new, o = lax.scan(_wkv_step, wkv_prev.astype(f32), xs)
    o = jnp.moveaxis(o, 0, 1)
    mean = jnp.mean(o, axis=-1, keepdims=True)
    var = jnp.mean(jnp.square(o - mean), axis=-1, keepdims=True)
    o = ((o - mean) * lax.rsqrt(var + GN_EPS)).reshape(B, T, W_B) * lnx_w + lnx_b
    bonus = (jnp.sum(r_h * k_h * r_k.reshape(H_B, DH_B), axis=-1, keepdims=True) * v_h).reshape(B, T, W_B)
    o = ((o + bonus) * g).astype(u.dtype)
    return o, u[:, -1], wkv_new

def hier_moe(h, w_grp, w_exp, we_gate, we_up, we_down):
    B, T, D = h.shape
    hf = h.reshape(-1, D)
    n = hf.shape[0]
    grp_logits = (hf @ w_grp).astype(jnp.float32)
    grp_prob = jax.nn.softmax(grp_logits, axis=-1)
    g_idx = jnp.argmax(grp_logits, axis=-1).astype(jnp.int32)
    p_grp = jnp.take_along_axis(grp_prob, g_idx[:, None], axis=-1)
    exp_logits = (hf @ w_exp).astype(jnp.float32).reshape(n, N_GROUPS, EXPERTS_PER_GROUP)
    in_grp = jnp.take_along_axis(exp_logits, g_idx[:, None, None], axis=1)[:, 0]
    top_v, top_i = lax.top_k(in_grp, TOP_K_IN_GROUP)
    weights = jax.nn.softmax(top_v, axis=-1) * p_grp
    eid = (g_idx[:, None] * EXPERTS_PER_GROUP + top_i).reshape(-1).astype(jnp.int32)
    tok = jnp.repeat(jnp.arange(n, dtype=jnp.int32), TOP_K_IN_GROUP)
    wts = weights.reshape(-1)
    n_assign = eid.shape[0]
    n_blocks = -(-n_assign // ROUTE_BLOCK) + N_EXPERTS
    rows = n_blocks * ROUTE_BLOCK
    counts = jnp.zeros((N_EXPERTS,), jnp.int32).at[eid].add(1)
    padded = (counts + ROUTE_BLOCK - 1) // ROUTE_BLOCK * ROUTE_BLOCK
    pad_end = jnp.cumsum(padded).astype(jnp.int32)
    pad_start = pad_end - padded
    start = jnp.cumsum(counts).astype(jnp.int32) - counts
    order = jnp.argsort(eid)
    e_sorted = eid[order]
    dest = pad_start[e_sorted] + jnp.arange(n_assign, dtype=jnp.int32) - start[e_sorted]
    row_tok = jnp.full((rows,), n, jnp.int32).at[dest].set(tok[order])
    row_w = jnp.zeros((rows,), jnp.float32).at[dest].set(wts[order])
    blk_start = jnp.arange(n_blocks, dtype=jnp.int32) * ROUTE_BLOCK
    blk_exp = jnp.minimum(jnp.searchsorted(pad_end, blk_start, side='right'), N_EXPERTS - 1)
    h_pad = jnp.concatenate([hf, jnp.zeros((1, D), hf.dtype)], axis=0)

    def run_block(args):
        tok_b, w_b, e = args
        xb = h_pad[tok_b]
        yb = (jax.nn.silu(xb @ we_gate[e]) * (xb @ we_up[e])) @ we_down[e]
        return yb * w_b[:, None].astype(yb.dtype)

    ys = lax.map(run_block, (row_tok.reshape(n_blocks, ROUTE_BLOCK), row_w.reshape(n_blocks, ROUTE_BLOCK), blk_exp))
    out = jnp.zeros((n + 1, D), h.dtype).at[row_tok].add(ys.reshape(rows, D).astype(h.dtype))
    return out[:n].reshape(B, T, D)

def hybrid_layer(x, past, shift_prev, wkv_prev, norm_mix, w_in, b_f, mu_rw, w0, w2, a0, a2, g2,
                 k_k, k_a, r_k, lnx_w, lnx_b, p_a, p_b, w_o, norm_ffn, w_grp, w_exp, we_gate, we_up, we_down):
    B, T, _ = x.shape
    xn = rmsnorm(x, norm_mix)
    u = xn @ w_in
    u_fox, u_rw, u_gate = jnp.split(u, (FOX_COLS, FOX_COLS + RW_COLS), axis=-1)
    q, k, v, fl = jnp.split(u_fox, FOX_SPLITS, axis=-1)
    q = q.reshape(B, T, H_A, DH_A)
    k = k.reshape(B, T, H_A, DH_A)
    v = v.reshape(B, T, H_A, DH_A)
    logf = jax.nn.log_sigmoid((fl + b_f).astype(jnp.float32))
    if past is None:
        o_a = fox_prompt(q, k, v, logf)
    else:
        o_a = fox_sample(q, k, v, logf, *past)
    o_b, shift_new, wkv_new = rwkv_branch(u_rw, shift_prev, wkv_prev, mu_rw, w0, w2, a0, a2, g2,
                                          k_k, k_a, r_k, lnx_w, lnx_b)
    g_a, g_b = jnp.split(jax.nn.sigmoid(u_gate), 2, axis=-1)
    mixed = (g_a * (o_a.reshape(B, T, W_A) @ p_a) + g_b * (o_b @ p_b)) @ w_o
    x = x + mixed
    x = x + hier_moe(rmsnorm(x, norm_ffn), w_grp, w_exp, we_gate, we_up, we_down)
    return x, (k, v, logf, wkv_new, shift_new)

def setup_inputs(seed: int = 0) -> dict:
    key = jax.random.key(seed)
    ks = iter(jax.random.split(key, 40))
    f32 = jnp.float32

    def nrm(shape, scale):
        return jax.random.normal(next(ks), shape, f32) * scale

    n_pages = PAST_LEN // PAGE_SIZE
    used = DEC_BATCH * n_pages
    n_phys = used + max(1, used // 4)
    L = DEPTH
    inp = {}
    inp['x_prompt'] = nrm((BATCH, SEQ, D_MODEL), 1.0)
    inp['x_sample'] = nrm((DEC_BATCH, DEC_SEQ, D_MODEL), 1.0)
    inp['cache_k'] = nrm((L, n_phys, PAGE_SIZE, H_A, DH_A), 1.0)
    inp['cache_v'] = nrm((L, n_phys, PAGE_SIZE, H_A, DH_A), 1.0)
    inp['cache_logf'] = jax.nn.log_sigmoid(3.0 + nrm((L, n_phys, PAGE_SIZE, H_A), 1.0))
    inp['page_table'] = jax.random.permutation(next(ks), n_phys)[:used].reshape(DEC_BATCH, n_pages).astype(jnp.int32)
    inp['state_wkv'] = nrm((L, DEC_BATCH, H_B, DH_B, DH_B), 0.5)
    inp['state_shift'] = nrm((L, DEC_BATCH, RW_COLS), 1.0)
    inp['norm_mix'] = 1.0 + nrm((L, D_MODEL), 0.02)
    inp['w_in'] = nrm((L, D_MODEL, IN_COLS), D_MODEL ** -0.5)
    inp['b_f'] = 3.0 + nrm((L, H_A), 0.1)
    inp['mu_rw'] = jax.random.uniform(next(ks), (L, RW_COLS), f32)
    inp['w0'] = nrm((L, W_B), 0.5)
    inp['w2'] = nrm((L, DECAY_LORA, W_B), 0.1)
    inp['a0'] = nrm((L, W_B), 0.1)
    inp['a2'] = nrm((L, AAA_LORA, W_B), AAA_LORA ** -0.5)
    inp['g2'] = nrm((L, GATE_LORA, W_B), 0.1)
    inp['k_k'] = 0.85 + nrm((L, W_B), 0.02)
    inp['k_a'] = 1.0 + nrm((L, W_B), 0.02)
    inp['r_k'] = nrm((L, H_B, DH_B), 0.1)
    inp['lnx_w'] = 1.0 + nrm((L, W_B), 0.02)
    inp['lnx_b'] = nrm((L, W_B), 0.02)
    inp['p_a'] = nrm((L, W_A, D_MODEL), W_A ** -0.5)
    inp['p_b'] = nrm((L, W_B, D_MODEL), W_B ** -0.5)
    inp['w_o'] = nrm((L, D_MODEL, D_MODEL), D_MODEL ** -0.5)
    inp['norm_ffn'] = 1.0 + nrm((L, D_MODEL), 0.02)
    inp['w_grp'] = nrm((L, D_MODEL, N_GROUPS), D_MODEL ** -0.5)
    inp['w_exp'] = nrm((L, D_MODEL, N_EXPERTS), D_MODEL ** -0.5)
    inp['we_gate'] = nrm((L, N_EXPERTS, D_MODEL, D_EXPERT), D_MODEL ** -0.5)
    inp['we_up'] = nrm((L, N_EXPERTS, D_MODEL, D_EXPERT), D_MODEL ** -0.5)
    inp['we_down'] = nrm((L, N_EXPERTS, D_EXPERT, D_MODEL), D_EXPERT ** -0.5)
    inp['norm_final'] = 1.0 + nrm((D_MODEL,), 0.02)
    return inp

def reference(x_prompt, x_sample, cache_k, cache_v, cache_logf, page_table, state_wkv, state_shift,
              norm_mix, w_in, b_f, mu_rw, w0, w2, a0, a2, g2, k_k, k_a, r_k, lnx_w, lnx_b,
              p_a, p_b, w_o, norm_ffn, w_grp, w_exp, we_gate, we_up, we_down, norm_final):
    xp, xs = x_prompt, x_sample
    new_p, new_s = [], []
    for l in range(DEPTH):
        lw = (norm_mix[l], w_in[l], b_f[l], mu_rw[l], w0[l], w2[l], a0[l], a2[l], g2[l], k_k[l], k_a[l],
              r_k[l], lnx_w[l], lnx_b[l], p_a[l], p_b[l], w_o[l], norm_ffn[l], w_grp[l], w_exp[l],
              we_gate[l], we_up[l], we_down[l])
        shift0 = jnp.zeros((xp.shape[0], RW_COLS), xp.dtype)
        wkv0 = jnp.zeros((xp.shape[0], H_B, DH_B, DH_B), jnp.float32)
        xp, st_p = hybrid_layer(xp, None, shift0, wkv0, *lw)
        past = (gather_pages(cache_k[l], page_table), gather_pages(cache_v[l], page_table),
                gather_pages(cache_logf[l], page_table))
        xs, st_s = hybrid_layer(xs, past, state_shift[l], state_wkv[l], *lw)
        new_p.append(st_p)
        new_s.append(st_s)
    y_prompt = rmsnorm(xp, norm_final)
    y_sample = rmsnorm(xs, norm_final)
    k_prompt = jnp.stack([s[0] for s in new_p])
    v_prompt = jnp.stack([s[1] for s in new_p])
    logf_prompt = jnp.stack([s[2] for s in new_p])
    wkv_prompt = jnp.stack([s[3] for s in new_p])
    shift_prompt = jnp.stack([s[4] for s in new_p])
    k_sample = jnp.stack([s[0] for s in new_s])
    v_sample = jnp.stack([s[1] for s in new_s])
    logf_sample = jnp.stack([s[2] for s in new_s])
    wkv_sample = jnp.stack([s[3] for s in new_s])
    shift_sample = jnp.stack([s[4] for s in new_s])
    return (y_prompt, y_sample, k_prompt, v_prompt, logf_prompt, wkv_prompt, shift_prompt,
            k_sample, v_sample, logf_sample, wkv_sample, shift_sample)


_drawn_inputs = setup_inputs


def setup_inputs(seed=0):
    import zlib

    import numpy as np

    out = dict(_drawn_inputs(seed))
    spreads = {}
    factors = {'k_k': 200.0,
     'k_a': 2.918,
     'lnx_b': 4.363,
     'norm_final': 24.114,
     'lnx_w': 3.306,
     'cache_logf': 2.999}
    for name, (base, spread) in spreads.items():
        noise = np.random.default_rng([zlib.crc32(name.encode()), seed]).standard_normal(out[name].shape)
        drawn = base * np.exp(spread * noise) if base else spread * noise
        out[name] = __import__('jax').numpy.asarray(drawn.astype(out[name].dtype))
    for name, factor in factors.items():
        out[name] = (out[name] * factor).astype(out[name].dtype)
    return out
```

```python
from contextlib import ExitStack, contextmanager

import numpy as np

import concourse.bass as bass
from concourse import mybir

P = 128
D = 1024
KD = D // P
SEQ, NB, TS = 1024, 8, 4
NS = NB * TS
NT = SEQ + NS
TT = SEQ // P
NTT = TT + 1
H, DH, W = 8, 64, 512
HP = H // 2
PAST, PAGE = 2048, 128
NPG = PAST // PAGE
NE, GR, EPG, DE = 32, 4, 8, 256
RW = 3 * W + 64 + 64 + 128
FOX = 3 * W + H
C = 64
NCH = SEQ // C
NORM_EPS, GN_EPS = 1e-6, 64e-5
NEG = -1.0e30
EXP_HALF = float(np.exp(-0.5))

F32, BF16, I32 = mybir.dt.float32, mybir.dt.bfloat16, mybir.dt.int32
ALU, ACT = mybir.AluOpType, mybir.ActivationFunctionType
X = mybir.AxisListType.X
ds = bass.ds

VEC_FIELDS = [("norm_mix", 8), ("norm_ffn", 8), ("mu", 14), ("w0", 4), ("a0", 4), ("k_k", 4), ("k_a", 4),
              ("r_k", 4), ("lnx_w", 4), ("lnx_b", 4), ("b_f", 1)]
VEC_AT, _n = {}, 0
for _name, _k in VEC_FIELDS:
    VEC_AT[_name] = (_n, _n + _k)
    _n += _k
NVEC = _n

LEVELS = [1, 2, 4, 8, 16, 32]


def shape_constants():
    out = {}
    out["ident"] = np.eye(P, dtype=np.float32)
    head = np.arange(P) // DH
    out["head_ones"] = (head[:, None] == head[None, :]).astype(np.float32)
    i, j = np.arange(P)[:, None], np.arange(P)[None, :]
    out["causal"] = np.where(j <= i, 0.0, NEG).astype(np.float32)
    t, s = (np.arange(P) % C)[:, None], np.arange(C)[None, :]
    out["lower_eye"] = (t == s).astype(np.float32)
    out["upper"] = (t < s).astype(np.float32)
    out["upper_diag"] = (t <= s).astype(np.float32)
    out["level0"] = -((t // 2 == s // 2) & (t % 2 == 1) & (s % 2 == 0)).astype(np.float32)
    lv = [((s // (2 * z) == t // (2 * z)) & ((s // z) % 2 == 1) & ((t // z) % 2 == 0)).astype(np.float32)
          for z in LEVELS]
    lv[0] = -lv[0]
    out["levels_t"] = np.concatenate(lv, 1)
    row, key = np.arange(P), np.arange(NS)
    own = [((row // NS)[:, None] + 4 * g == (key // TS)[None, :]) & ((row % TS)[:, None] >= (key % TS)[None, :])
           for g in range(2)]
    out["own_past"] = np.concatenate([np.where(o, 0.0, NEG) for o in own], 1).astype(np.float32)
    bh = np.arange(NB * H)
    sel = np.zeros((P, NB, H, TS), np.float32)
    for b in range(NB):
        sel[bh, b, :, :] = ((bh // H == b)[:, None] & (bh % H)[:, None] == np.arange(H)[None, :])[:, :, None] * 0.0
        for h in range(H):
            sel[b * H + h, b, h, :] = -8.0
            sel[64 + b * H + h, b, h, :] = 8.0
    out["row_sel"] = sel.reshape(P, NB * NS)
    out["before"] = (i < j).astype(np.float32)
    out["expert_id"] = np.broadcast_to(np.arange(NE, dtype=np.float32)[None, :], (P, NE))
    out["is_sample"] = (np.arange(P) < NS).astype(np.float32)[:, None]
    out["beyond"] = np.where(np.arange(P) < NS, 0.0, 1e7).astype(np.float32)[:, None]
    out["token"] = (np.arange(NTT)[None, :] * P + np.arange(P)[:, None]).astype(np.float32)
    return out


CONSTS = shape_constants()
CONST_AT, _n = {}, 0
for _name, _a in CONSTS.items():
    CONST_AT[_name] = (_n, _n + _a.shape[1])
    _n += _a.shape[1]
NCONST = _n


class Shared:
    pass


class Steps:

    def __init__(self, sem):
        self.sem, self.n = sem, 0

    def done(self, ins):
        ins.then_inc(self.sem, 1)
        self.n = self.n + 1

    def settle(self, eng):
        eng.wait_ge(self.sem, self.n)

    def then(self, eng, ins):
        self.done(ins)
        self.settle(eng)

    @contextmanager
    def loop(self, eng, count, per):
        base = self.n
        with eng.Fori(0, count) as i:
            self.n = base + i * per
            self.at = self.n
            self.count = 0
            yield i
        self.n = base + count * per


def build(nc, a, upto=99):
    with ExitStack() as ctx:
        e = Shared()
        e.nc, e.a, e.ctx = nc, a, ctx
        e.sems = {}

        def sem(name):
            if name not in e.sems:
                e.sems[name] = nc.alloc_semaphore(name=name)
            return e.sems[name]

        e.sem = sem
        e.sb = lambda name, shape, dt=F32: ctx.enter_context(nc.sbuf_tensor(name, shape, dt))
        e.steps = {n: Steps(ctx.enter_context(nc.semaphore(f"{n}_steps"))) for n in ("dve", "act", "pool", "pe")}
        e.vec = e.sb("vec", [P, NVEC])
        e.const = e.sb("const", [P, NCONST])
        e.identb = e.sb("identb", [P, P], BF16)
        e.causalb = e.sb("causalb", [P, 512], BF16)
        e.own_pastb = e.sb("own_pastb", [P, 2 * NS], BF16)
        e.ones = e.sb("ones", [P, SEQ])
        e.eps = e.sb("eps", [P, 2])
        e.v = lambda name: e.vec[:, VEC_AT[name][0]:VEC_AT[name][1]]
        e.c = lambda name: e.const[:, CONST_AT[name][0]:CONST_AT[name][1]]
        e.c_rows = nc.dram_tensor("c_rows", (H, 2, 2, SEQ), F32, kind="Internal").ap()
        dram = lambda name, shape, dt=F32: nc.dram_tensor(name, shape, dt, kind="Internal").ap()
        e.CAP = NTT * P
        e.sv_d, e.so_d = dram("sample_vectors", (6, NS, W)), dram("sample_out", (NS, W))
        e.table_d = dram("expert_table", (NE * e.CAP, 4), I32)
        e.h_d, e.y2_d = dram("h_rows", (NTT * P, D)), dram("y2", (2 * NT, D))
        rows = e.sb("rows", [P, (KD + HP) * NT])
        e.xnT = rows[:, 0:KD * NT].rearrange("p (k n) -> p k n", k=KD)
        e.oaT = rows[:, KD * NT:].rearrange("p (k n) -> p k n", k=HP)
        e.x1 = rows[:, 0:NTT * D].rearrange("p (t d) -> p t d", t=NTT)
        for n, stage in enumerate(STAGES):
            if n <= upto:
                stage(e)
            if len(e.sems) > 100:
                nc.clear_and_free_semaphores(list(e.sems.values()))
                nc.all_engine_barrier()
                e.sems.clear()


@contextmanager
def memory(e):
    with ExitStack() as ctx:
        sb = lambda name, shape, dt=F32: ctx.enter_context(e.nc.sbuf_tensor(name, shape, dt))
        ps = lambda name, shape, dt=F32: ctx.enter_context(e.nc.psum_tensor(name, shape, dt))
        yield sb, ps


def pairs(eng, count, body):
    with eng.Fori(0, count // 2) as i:
        for b in range(2):
            body(2 * i + b, i, b)
    if count % 2:
        body(count - 1, count // 2, 0)


def stage_norm(e):
    nc, a, sem = e.nc, e.a, e.sem
    loaded, const_loaded = [sem(f"x_loaded{b}") for b in range(2)], sem("const_loaded")
    xt_free, sq, std, rstd, xn_ready = sem("xt_free"), sem("x_sq"), sem("x_std"), sem("x_rstd"), sem("xn_ready")
    turned, xnT_ready, const_ready = sem("x_turned"), sem("xnT_ready"), sem("const_ready")
    with memory(e) as (sb, ps), nc.Block() as block:
        xt, xn, junk = sb("xt", [P, 2, D]), sb("xn", [P, 2, D]), sb("sq_junk", [P, D])
        stat = sb("x_stat", [P, 2, 4])
        pt = [ps(f"x_pt{b}", [P, KD, P]) for b in range(2)]

        @block.sync
        def _(sp):
            sp.dma_start(e.vec[:], a["vec"]).then_inc(const_loaded, 16)
            sp.dma_start(e.const[:], a["consts"]).then_inc(const_loaded, 16)

            def load(t, i, b):
                sp.wait_ge(xt_free, t + 1)
                sp.dma_start(xt[:, b, :], a["x"][ds(t * P, P), :]).then_inc(loaded[b], 16)
            pairs(sp, NTT, load)

        @block.scalar
        def _(act):
            act.wait_ge(const_ready, 5)

            def body(t, i, b):
                act.wait_ge(loaded[b], 16 * (i + 1))
                act.activation(junk[:], xt[:, b, :], ACT.Square, accum_out=stat[:, b, 0:1]).then_inc(sq, 1)
                act.wait_ge(sq, t + 1)
                act.activation(stat[:, b, 1:2], stat[:, b, 0:1], ACT.Sqrt, scale=1.0 / D,
                               bias=e.eps[:, 0:1]).then_inc(std, 1)
            pairs(act, NTT, body)

        @block.vector
        def _(dve):
            dve.memset(e.ones[:], 1.0).then_inc(const_ready, 1)
            dve.memset(e.eps[:, 0:1], NORM_EPS)
            dve.memset(e.eps[:, 1:2], GN_EPS).then_inc(const_ready, 1)
            dve.sem_inc(xt_free, 2)
            dve.wait_ge(const_loaded, 32)
            dve.tensor_copy(e.identb[:], e.c("ident")).then_inc(const_ready, 1)
            dve.memset(e.causalb[:, 0:384], 0.0)
            dve.tensor_copy(e.causalb[:, 384:512], e.c("causal")).then_inc(const_ready, 1)
            dve.tensor_copy(e.own_pastb[:], e.c("own_past")).then_inc(const_ready, 1)

            def body(t, i, b):
                dve.wait_ge(std, t + 1)
                dve.reciprocal(stat[:, b, 2:3], stat[:, b, 1:2]).then_inc(rstd, 1)
                dve.wait_ge(rstd, t + 1)
                dve.tensor_scalar(xn[:, b, :], xt[:, b, :], stat[:, b, 2:3], None, ALU.mult).then_inc(xn_ready, 1)
                dve.wait_ge(xn_ready, t + 1)
                dve.sem_inc(xt_free, 1)
                dve.wait_ge(turned, t + 1)
                n = P if not isinstance(t, int) else NS
                dve.tensor_tensor(e.xnT[:, :, ds(t * P, n)], pt[b][:, :, 0:n],
                                  e.v("norm_mix").unsqueeze(2).to_broadcast([P, KD, n]),
                                  ALU.mult).then_inc(xnT_ready, 1)
            pairs(dve, NTT, body)

        @block.tensor
        def _(pe):
            def body(t, i, b):
                pe.wait_ge(xn_ready, t + 1)
                if not isinstance(t, int) or t >= 2:
                    pass
                for k in range(KD):
                    mm = pe.transpose(pt[b][:, k, :], xn[:, b, k * P:(k + 1) * P], e.c("ident"))
                mm.then_inc(turned, 1)
            pairs(pe, NTT, body)


COLS = [(0, 512), (512, 512), (SEQ, NS)]


def project_tiles(e, name, sb, ps, block, j0, n, dest, extra_pe=None):
    a, sem = e.a, e.sem
    w_loaded = [sem(f"{name}_w_loaded{b}") for b in range(2)]
    made, act_out, dve_out = sem(f"{name}_made"), sem(f"{name}_act_out"), sem(f"{name}_dve_out")
    w = sb(f"{name}_w", [P, 2, KD, P])
    pp = [ps(f"{name}_pp{b}", [P, 3, 512]) for b in range(2)]

    @block.sync
    def _(sp):
        for b in range(2):
            sp.dma_start(w[:, b], a["w_in"][j0 + b]).then_inc(w_loaded[b], 16)
        with sp.Fori(0, n // 2 - 1) as i:
            for b in range(2):
                sp.wait_ge(made, 2 * i + b + 1)
                sp.dma_start(w[:, b], a["w_in"][ds(j0 + 2 + 2 * i + b, 1)].squeeze(0)).then_inc(w_loaded[b], 16)

    @block.tensor
    def _(pe):
        def body(j, i, b, first=False):
            pe.wait_ge(w_loaded[b], 16 * (i + 1))
            if not first:
                pe.wait_ge(act_out, j - 1)
                pe.wait_ge(dve_out, j - 1)
            for k in range(KD):
                for c, (at, m) in enumerate(COLS):
                    mm = pe.matmul(pp[b][:, c, 0:m], w[:, b, k, :], e.xnT[:, k, at:at + m],
                                   start=(k == 0), stop=(k == KD - 1))
            mm.then_inc(made, 1)
        body(0, 0, 0, True)
        body(1, 0, 1, True)
        with pe.Fori(1, n // 2) as i:
            for b in range(2):
                body(2 * i + b, i, b)
        if extra_pe:
            extra_pe(pe)

    def out(eng, copy, done, cols):
        def body(j, i, b):
            eng.wait_ge(made, j + 1)
            for c in cols:
                at, m = COLS[c]
                ins = copy(dest[:, ds(j, 1), at:at + m].squeeze(1), pp[b][:, c, 0:m])
            ins.then_inc(done, 1)
        pairs(eng, n, body)

    @block.scalar
    def _(act):
        out(act, act.copy, act_out, [0])

    @block.vector
    def _(dve):
        out(dve, dve.tensor_copy, dve_out, [1, 2])


def stage_fox_project(e):
    e.fox_mem = e.ctx.enter_context(ExitStack())
    e.qkv = e.fox_mem.enter_context(e.nc.sbuf_tensor("qkv", [P, 12, NT], F32))
    with memory(e) as (sb, ps), e.nc.Block() as block:
        project_tiles(e, "fox", sb, ps, block, 0, 12, e.qkv)


def stage_fox_prepare(e):
    nc, a, sem = e.nc, e.a, e.sem
    e.v_tok = e.fox_mem.enter_context(nc.sbuf_tensor("v_tok", [P, NTT, W], F32))
    e.logfT = e.fox_mem.enter_context(nc.sbuf_tensor("logfT", [H, NT], F32))
    wf_loaded, f_made, z_ready, m_ready = sem("wf_loaded"), sem("f_made"), sem("f_z"), sem("f_m")
    exp_ready, ln_ready, logf_ready, c_ready = sem("f_exp"), sem("f_ln"), sem("logf_ready"), sem("c_ready")
    turned, kept, logf_turned, logf_kept = sem("kv_turned"), sem("kv_kept"), sem("logf_turned"), sem("logf_kept")
    stored = sem("fox_stored")
    with memory(e) as (sb, ps), nc.Block() as block:
        wf, k_tok = sb("wf", [P, KD, H]), sb("k_tok", [P, NTT, W])
        z, m, ex = sb("f_z_t", [H, NT]), sb("f_m_t", [H, NT]), sb("f_ex", [H, NT])
        crow = sb("crow", [H, 2, SEQ])
        logf_tok = sb("logf_tok", [P, NTT, H])
        fp = ps("fp", [P, 3, 512])
        kv = [ps(f"kv_t{b}", [P, 512]) for b in range(3)]
        lp = ps("logf_t", [P, NTT, H])
        tiles = [(t, src, min(P, NT - t * P)) for t in range(NTT) for src in (4, 8)]

        @block.sync
        def _(sp):
            sp.dma_start(wf[:], a["w_f"]).then_inc(wf_loaded, 16)
            n = 0
            for x, (t, src, m_) in enumerate(tiles):
                sp.wait_ge(kept, x + 1)
                tok, dst = (k_tok, a["k_out"]) if src == 4 else (e.v_tok, a["v_out"])
                sp.dma_start(dst[t * P:t * P + m_, :], tok[0:m_, t, :]).then_inc(stored, 16)
                n += 1
            sp.wait_ge(c_ready, 2)
            sp.dma_start(e.c_rows[:, 0, 0, :], crow[:, 0, :]).then_inc(stored, 16)
            sp.dma_start(e.c_rows[:, 0, 1, :], e.ones[0:H, 0:SEQ]).then_inc(stored, 16)
            sp.dma_start(e.c_rows[:, 1, 0, :], e.ones[0:H, 0:SEQ]).then_inc(stored, 16)
            sp.dma_start(e.c_rows[:, 1, 1, :], crow[:, 1, :]).then_inc(stored, 16)
            sp.wait_ge(logf_kept, 1)
            sp.dma_start(a["logf_out"][0:SEQ, :].rearrange("(t p) h -> p t h", p=P), logf_tok[:, 0:TT, :]).then_inc(stored, 16)
            sp.dma_start(a["logf_out"][SEQ:NT, :], logf_tok[0:NS, TT, :]).then_inc(stored, 16)
            sp.wait_ge(stored, 16 * (n + 6))

        @block.tensor
        def _(pe):
            pe.wait_ge(wf_loaded, 16)
            for k in range(KD):
                for c, (at, n) in enumerate(COLS):
                    mm = pe.matmul(fp[0:H, c, 0:n], wf[:, k, :], e.xnT[:, k, at:at + n],
                                   start=(k == 0), stop=(k == KD - 1))
            mm.then_inc(f_made, 1)
            for x, (t, src, n) in enumerate(tiles):
                if x >= 3:
                    pe.wait_ge(kept, x - 2)
                for j in range(HP):
                    mm = pe.transpose(kv[x % 3][0:n, j * P:(j + 1) * P], e.qkv[:, src + j, t * P:t * P + n], e.c("ident"))
                mm.then_inc(turned, 1)
            pe.wait_ge(logf_ready, 1)
            for t in range(NTT):
                n = min(P, NT - t * P)
                mm = pe.transpose(lp[0:n, t, :], e.logfT[:, t * P:t * P + n], e.c("ident")[0:H, 0:H])
            mm.then_inc(logf_turned, 1)

        @block.scalar
        def _(act):
            act.wait_ge(m_ready, 1)
            act.activation(ex[:], m[:], ACT.Exp).then_inc(exp_ready, 1)
            act.wait_ge(exp_ready, 1)
            act.activation(ex[:], ex[:], ACT.Ln, bias=e.ones[0:H, 0:1]).then_inc(ln_ready, 1)

        @block.vector
        def _(dve):
            dve.wait_ge(f_made, 1)
            for c, (at, n) in enumerate(COLS):
                ins = dve.tensor_scalar(z[:, at:at + n], fp[0:H, c, 0:n], e.v("b_f")[0:H, :], None, ALU.add)
            ins.then_inc(z_ready, 1)
            dve.wait_ge(z_ready, 1)
            dve.scalar_tensor_tensor(m[:], z[:], -1.0, z[:], ALU.mult, ALU.min).then_inc(m_ready, 1)
            for x, (t, src, n) in enumerate(tiles):
                dve.wait_ge(turned, x + 1)
                tok = k_tok if src == 4 else e.v_tok
                dve.tensor_copy(tok[0:n, t, :], kv[x % 3][0:n, :]).then_inc(kept, 1)
            dve.wait_ge(ln_ready, 1)
            dve.scalar_tensor_tensor(e.logfT[:], z[:], 0.0, ex[:], ALU.min, ALU.subtract).then_inc(logf_ready, 1)
            dve.wait_ge(logf_ready, 1)
            dve.tensor_tensor_scan(m[:, 0:SEQ], e.ones[0:H, 0:SEQ], e.logfT[:, 0:SEQ], 0.0, ALU.mult, ALU.add).then_inc(z_ready, 1)
            dve.wait_ge(z_ready, 2)
            dve.tensor_scalar(crow[:, 0, :], m[:, 0:SEQ], 8.0, None, ALU.mult).then_inc(c_ready, 1)
            dve.tensor_scalar(crow[:, 1, :], m[:, 0:SEQ], -8.0, None, ALU.mult).then_inc(c_ready, 1)
            dve.wait_ge(logf_turned, 1)
            dve.tensor_copy(logf_tok[:, 0:TT, :], lp[:, 0:TT, :])
            dve.tensor_copy(logf_tok[0:NS, TT, :], lp[0:NS, TT, :]).then_inc(logf_kept, 1)


def stage_fox_prompt(e):
    nc, a, sem = e.nc, e.a, e.sem
    rows_loaded = [sem(f"c_rows_loaded{s}") for s in range(2)]
    staged, head_done = sem("fox_staged"), sem("fox_head_done")
    scored, maxed, bias_ready, exped = sem("fox_scored"), sem("fox_maxed"), sem("fox_bias"), sem("fox_exped")
    turned, pt_dve, pt_act = sem("fox_turned"), sem("fox_pt_dve"), sem("fox_pt_act")
    mixed, recip, out_done, o_turned, o_kept = (sem("fox_mixed"), sem("fox_recip"), sem("fox_out"),
                                                sem("fox_o_turned"), sem("fox_o_kept"))
    with memory(e) as (sb, ps), nc.Block() as block:
        q_head, k_head = sb("q_head", [66, 2, SEQ]), sb("k_head", [66, 2, SEQ])
        prob, probT = sb("prob", [P, 2, SEQ]), sb("probT", [P, TT, P])
        o_tok = sb("o_tok", [P, TT, W])
        stat = sb("fox_stat", [P, 2, 4])
        score = [ps(f"score{b}", [P, 1024]) for b in range(2)]
        pt = ps("prob_t", [P, TT, P])
        op = [ps(f"fox_o{b}", [P, 512]) for b in range(2)]
        items = [(s, t) for s in range(2) for t in range(TT)]
        M = len(items)
        act_copies = lambda i, s, t: (TT - 4) * (2 * i + s) + max(t - 3, 0)

        @block.sync
        def _(sp):
            with sp.Fori(0, HP) as i:
                for s in range(2):
                    sp.wait_ge(head_done, 2 * i + s + 1)
                    sp.dma_start(q_head[64:66, s, :], e.c_rows[ds(2 * i + s, 1), 0].squeeze(0)).then_inc(rows_loaded[s], 16)
                    sp.dma_start(k_head[64:66, s, :], e.c_rows[ds(2 * i + s, 1), 1].squeeze(0)).then_inc(rows_loaded[s], 16)

        @block.tensor
        def _(pe):
            pe.sem_inc(head_done, 2)

            def scores(i, m):
                s, t = items[m]
                g = i * M + m
                if t == 0:
                    pe.wait_ge(staged, 4 * (i + 1))
                    pe.wait_ge(rows_loaded[s], 32 * (i + 1))
                pe.wait_ge(exped, g + 1)
                for c in range(0, (t + 1) * P, 512):
                    n = min(512, (t + 1) * P - c)
                    last = c + n == (t + 1) * P
                    pe.matmul(score[m % 2][:, c:c + n], q_head[:, s, t * P:(t + 1) * P], k_head[:, s, c:c + n],
                              start=True, stop=not last)
                pe.matmul(score[m % 2][:, c:c + n], e.identb[:], e.causalb[:, 512 - n:512],
                          start=False, stop=True).then_inc(scored, 1)

            def turn(i, m):
                s, t = items[m]
                g = i * M + m
                pe.wait_ge(exped, g + 3)
                for k in range(t + 1):
                    mm = pe.transpose(pt[:, k, :], prob[:, m % 2, k * P:(k + 1) * P], e.c("ident"))
                mm.then_inc(turned, 1)

            def times_v(i, m):
                s, t = items[m]
                g = i * M + m
                pe.wait_ge(pt_dve, g + 1)
                if t >= 4:
                    pe.wait_ge(pt_act, act_copies(i, s, t))
                pe.wait_ge(out_done, g + 1)
                for k in range(t + 1):
                    mm = pe.matmul(op[m % 2][:, 0:DH], probT[:, k, :], e.v_tok[:, k, ds((2 * i + s) * DH, DH)],
                                   start=(k == 0), stop=(k == t))
                mm.then_inc(mixed, 1)
                if t == TT - 1:
                    pe.wait_ge(mixed, g + 1)
                    pe.sem_inc(head_done, 1)

            with pe.Fori(0, HP) as i:
                scores(i, 0)
                for m in range(M):
                    turn(i, m)
                    if m + 1 < M:
                        scores(i, m + 1)
                    times_v(i, m)
            pe.wait_ge(out_done, 2 + HP * M)
            for t in range(TT):
                if t >= 2:
                    pe.wait_ge(o_kept, t - 1)
                for j in range(HP):
                    mm = pe.transpose(op[t % 2][:, j * P:(j + 1) * P], o_tok[:, t, j * P:(j + 1) * P], e.c("ident"))
                mm.then_inc(o_turned, 1)

        @block.scalar
        def _(act):
            act.sem_inc(exped, 2)
            with act.Fori(0, HP) as i:
                for m, (s, t) in enumerate(items):
                    g = i * M + m
                    if m == 0:
                        for z in range(2):
                            act.wait_ge(head_done, 2 * i + z + 1)
                            act.copy(q_head[0:64, z, :], e.qkv[64 * z:64 * z + 64, ds(i, 1), 0:SEQ].squeeze(1)).then_inc(staged, 1)
                    act.wait_ge(bias_ready, g + 1)
                    act.activation(prob[:, m % 2, 0:(t + 1) * P], score[m % 2][:, 0:(t + 1) * P], ACT.Exp, scale=0.125,
                                   bias=stat[:, m % 2, 1:2], accum_out=stat[:, m % 2, 2:3]).then_inc(exped, 1)
                    act.wait_ge(turned, g + 1)
                    if t >= 4:
                        act.wait_ge(mixed, g)
                        act.copy(probT[:, 4:t + 1, :], pt[:, 4:t + 1, :]).then_inc(pt_act, 1)

        @block.vector
        def _(dve):
            dve.sem_inc(out_done, 2)
            with dve.Fori(0, HP) as i:
                for m, (s, t) in enumerate(items):
                    g = i * M + m
                    if m == 0:
                        for z in range(2):
                            dve.wait_ge(head_done, 2 * i + z + 1)
                            dve.tensor_copy(k_head[0:64, z, :], e.qkv[64 * z:64 * z + 64, ds(i + HP, 1), 0:SEQ].squeeze(1)).then_inc(staged, 1)
                    dve.wait_ge(scored, g + 1)
                    dve.reduce_max(stat[:, m % 2, 0:1], score[m % 2][:, 0:(t + 1) * P], X).then_inc(maxed, 1)
                    dve.wait_ge(maxed, g + 1)
                    dve.tensor_scalar(stat[:, m % 2, 1:2], stat[:, m % 2, 0:1], -0.125, None, ALU.mult).then_inc(bias_ready, 1)
                    dve.wait_ge(turned, g + 1)
                    h = min(t + 1, 4)
                    dve.tensor_copy(probT[:, 0:h, :], pt[:, 0:h, :]).then_inc(pt_dve, 1)
                    dve.wait_ge(exped, g + 3)
                    dve.reciprocal(stat[:, m % 2, 3:4], stat[:, m % 2, 2:3]).then_inc(recip, 1)
                    dve.wait_ge(recip, g + 1)
                    dve.wait_ge(mixed, g + 1)
                    dve.tensor_scalar(o_tok[:, t, ds((2 * i + s) * DH, DH)], op[m % 2][:, 0:DH], stat[:, m % 2, 3:4],
                                      None, ALU.mult).then_inc(out_done, 1)
            for t in range(TT):
                dve.wait_ge(o_turned, t + 1)
                dve.tensor_copy(e.oaT[:, :, t * P:(t + 1) * P],
                                op[t % 2][:].rearrange("p (j n) -> p j n", j=HP)).then_inc(o_kept, 1)


RING = 8


def stage_fox_sample(e):
    nc, a, sem = e.nc, e.a, e.sem
    table_loaded, lf_loaded, new_loaded = sem("table_loaded"), sem("lf_loaded"), sem("new_loaded")
    lf_turned, steps = sem("lf_turned"), e.steps["dve"]
    prepared, zeroed, ones_set = sem("dec_prepared"), sem("dec_zeroed"), sem("dec_ones_set")
    page_loaded = [sem(f"page_loaded{u}") for u in range(RING)]
    page_used, k_turned, kt_out, page_scored = sem("page_used"), sem("k_turned"), sem("kt_out"), sem("page_scored")
    scored, maxed, biased, exped, recip, prob_ready = (sem("dec_scored"), sem("dec_maxed"), sem("dec_biased"),
                                                       sem("dec_exped"), sem("dec_recip"), sem("dec_prob"))
    p_turned, p_kept, mixed, o_kept = sem("dec_p_turned"), sem("dec_p_kept"), sem("dec_mixed"), sem("dec_o_kept")
    NG, BG = 2, 4
    NP2 = NPG // RING
    KEYS = PAST + NS
    with memory(e) as (sb, ps), nc.Block() as block:
        table = sb("table", [1, NB * NPG], I32)
        lf = sb("lf", [P, NPG, NB, H])
        ck = sb("ck", [P, PAST + TS])
        ck_new = sb("ck_new", [P, NB, TS])
        lf_new = sb("lf_new", [NB * H, TS])
        row = sb("row_gate", [P, NB, H, TS])
        qs = sb("qs", [P, NB, HP, P])
        page = sb("page", [P, RING, W])
        kt = sb("kt", [P, 2, HP, P])
        prob = sb("dec_prob_t", [P, KEYS])
        probT = sb("dec_probT", [P, NPG + 1, P])
        zero = sb("zero", [P, 512], BF16)
        stat = sb("dec_stat", [P, 4])
        score = ps("dec_score", [P, 2560])
        ktp = [ps(f"ktp{b}", [P, HP, P]) for b in range(2)]
        ov = ps("dec_o", [P, 512])

        @block.sync
        def _(sp):
            sp.dma_start(table[:], a["page_table"]).then_inc(table_loaded, 16)
            for b in range(NB):
                sp.dma_start(lf_new[b * H:(b + 1) * H, :],
                             a["logf_out"][SEQ + b * TS:SEQ + (b + 1) * TS, :].rearrange("t h -> h t"), allow_slow_non_contiguous=True).then_inc(new_loaded, 16)
            sp.wait_ge(table_loaded, 16)
            with sp.Fori(0, NPG) as j:
                for b in range(NB):
                    n = sp.value_load(table[0:1, ds(j + b * NPG, 1)], min_val=0, max_val=a["cache_k"].shape[0] - 1)
                    sp.dma_start(lf[:, ds(j, 1), b, :].squeeze(1), a["cache_logf"][ds(n, 1)].squeeze(0)).then_inc(lf_loaded, 16)
            for g in range(NG):
                for kv, cache in enumerate((a["cache_k"], a["cache_v"])):
                    with sp.Fori(0, BG * NP2) as r:
                        for u in range(RING):
                            n = sp.value_load(table[0:1, ds(r * RING + (g * BG * NPG + u), 1)],
                                              min_val=0, max_val=a["cache_k"].shape[0] - 1)
                            sp.wait_ge(page_used, r * RING + (2 * g + kv) * BG * NPG + u + 1)
                            sp.dma_start(page[:, u, :], cache[ds(n, 1)].rearrange("n p h d -> p (n h d)")
                                         ).then_inc(page_loaded[u], 16)

        @block.gpsimd
        def _(pool):
            pool.memset(qs[:], 0.0).then_inc(zeroed, 1)
            pool.memset(zero[:], 0.0).then_inc(zeroed, 1)
            pool.wait_ge(zeroed, 2)
            pool.memset(ck[64:P, :], 1.0).then_inc(ones_set, 1)
            pool.memset(ck_new[64:P, :, :], 1.0).then_inc(ones_set, 1)

        def rounds(eng, body):
            with eng.Fori(0, NP2) as r:
                for u in range(RING):
                    body(r, u, r * RING + u)

        @block.tensor
        def _(pe):
            pe.sem_inc(page_used, RING)
            pe.sem_inc(page_scored, 2)
            pe.wait_ge(lf_loaded, 16 * NB * NPG)
            for j in range(NPG):
                mm = pe.transpose(score[0:NB * H, j * P:(j + 1) * P], lf[:, j].rearrange("p b h -> p (b h)"), e.c("ident"))
            mm.then_inc(lf_turned, 1)
            pe.wait_ge(prepared, 1)
            for g in range(NG):
                if g:
                    pe.wait_ge(exped, g)
                for c in range(4):
                    pe.matmul(score[:, c * 512:(c + 1) * 512], e.identb[:], zero[:], start=True, stop=False)
                pe.matmul(score[:, PAST:KEYS], e.identb[:], e.own_pastb[:, g * NS:(g + 1) * NS], start=True, stop=False)
                for b in range(BG):
                    for p in range(HP):
                        pe.matmul(score[:, PAST:KEYS], qs[:, g * BG + b, p, :], e.qkv[:, HP + p, SEQ:NT], start=False, stop=False)
                for b in range(BG):
                    base = (g * BG + b) * NPG

                    def keys(r, u, n):
                        pe.wait_ge(page_loaded[u], 16 * (r + 1 + 2 * g * BG * NP2 + b * NP2))
                        for p in range(HP):
                            mm = pe.transpose(ktp[u % 2][:, p, :], page[:, u, p * P:(p + 1) * P], e.c("ident"))
                        mm.then_inc(k_turned, 1)
                        pe.wait_ge(k_turned, base + n + 1)
                        pe.sem_inc(page_used, 1)
                        pe.wait_ge(kt_out, base + n + 1)
                        for p in range(HP):
                            mm = pe.matmul(score[:, ds(n * P, P)], qs[:, g * BG + b, p, :], kt[:, u % 2, p, :],
                                           start=False, stop=False)
                        mm.then_inc(page_scored, 1)
                    rounds(pe, keys)
                for c in range(4):
                    pe.matmul(score[:, c * 512:(c + 1) * 512], row[:, g * BG:(g + 1) * BG].rearrange("p b h t -> p (b h t)"),
                              ck[:, c * 512:(c + 1) * 512], start=False, stop=True)
                pe.matmul(score[:, PAST:KEYS], row[:, g * BG:(g + 1) * BG].rearrange("p b h t -> p (b h t)"),
                          ck_new[:].rearrange("p b t -> p (b t)"), start=False, stop=True).then_inc(scored, 1)
                pe.wait_ge(prob_ready, g + 1)
                for x in range(5):
                    m = 5 * g + x
                    if x >= 2:
                        pe.wait_ge(p_kept, m - 1)
                    for y in range(4 if x < 4 else 1):
                        j = 4 * x + y
                        n = P if x < 4 else NS
                        mm = pe.transpose(ktp[x % 2][0:n, y, :], prob[:, j * P:j * P + n], e.c("ident"))
                    mm.then_inc(p_turned, 1)
                pe.wait_ge(p_kept, 5 * g + 5)
                for b in range(BG):
                    s = g * BG + b
                    if s:
                        pe.wait_ge(o_kept, s)
                    pe.matmul(ov[:, 0:NS], e.identb[:], zero[:, 0:NS], start=True, stop=False)

                    def values(r, u, n):
                        pe.wait_ge(page_loaded[u], 16 * (r + 1 + (2 * g + 1) * BG * NP2 + b * NP2))
                        for p in range(HP):
                            mm = pe.matmul(ov[:, p * 8:p * 8 + 8], page[:, u, p * P:(p + 1) * P],
                                           probT[:, ds(n, 1), b * NS + p * 8:b * NS + p * 8 + 8].squeeze(1),
                                           start=False, stop=False)
                        mm.then_inc(page_used, 1)
                    rounds(pe, values)
                    for p in range(HP):
                        pe.matmul(ov[:, p * 8:p * 8 + 8], e.v_tok[0:NS, TT, p * P:(p + 1) * P],
                                  probT[0:NS, NPG, b * NS + p * 8:b * NS + p * 8 + 8], start=False, stop=False)
                    pe.matmul(ov[:, 0:NS], e.identb[:], zero[:, 0:NS], start=False, stop=True).then_inc(mixed, 1)

        @block.scalar
        def _(act):
            for g in range(NG):
                for b in range(BG):
                    base = (g * BG + b) * NPG

                    def out(r, u, n):
                        if u % 2:
                            return
                        act.wait_ge(k_turned, base + n + 1)
                        act.wait_ge(page_scored, base + n + 1)
                        act.copy(kt[:, 0], ktp[0][:]).then_inc(kt_out, 1)
                    rounds(act, out)
                act.wait_ge(biased, g + 1)
                if g:
                    act.wait_ge(p_turned, 5 * g)
                act.activation(prob[:], score[:, 0:KEYS], ACT.Exp, scale=0.125, bias=stat[:, 1:2],
                               accum_out=stat[:, 2:3]).then_inc(exped, 1)

        @block.vector
        def _(dve):
            dve.wait_ge(lf_turned, 1)
            dve.wait_ge(new_loaded, 16 * NB)
            dve.wait_ge(ones_set, 2)
            for c in range(4):
                steps.then(dve, dve.tensor_tensor_scan(
                    ck[0:64, c * 512:(c + 1) * 512], e.ones[0:64, 0:512], score[0:64, c * 512:(c + 1) * 512],
                    0.0 if c == 0 else ck[0:64, c * 512 - 1:c * 512], ALU.mult, ALU.add))
            steps.then(dve, dve.tensor_tensor_scan(ck[0:64, PAST:PAST + TS], e.ones[0:64, 0:TS], lf_new[:],
                                                   ck[0:64, PAST - 1:PAST], ALU.mult, ALU.add))
            cq = ck[0:64, PAST:PAST + TS]
            steps.done(dve.tensor_copy(ck_new[0:64], cq.unsqueeze(1).to_broadcast([64, NB, TS])))
            steps.done(dve.tensor_copy(stat[64:P, 0:4], cq))
            steps.done(dve.tensor_copy(row[:].rearrange("p b h t -> p (b h t)"), e.c("row_sel")))
            dve.wait_ge(zeroed, 2)
            for p in range(HP):
                for s in range(2):
                    half = slice(64 * s, 64 * s + 64)
                    for g in range(NG):
                        for b in range(BG):
                            col = b * NS + (2 * p + s) * TS
                            steps.done(dve.tensor_copy(qs[half, g * BG + b, p, col:col + TS],
                                                       e.qkv[half, p, SEQ + (g * BG + b) * TS:SEQ + (g * BG + b + 1) * TS]))
            steps.settle(dve)
            rows = row[64:P].rearrange("p b h t -> p (b h) t")
            dve.tensor_tensor(rows, rows, stat[64:P, 0:4].unsqueeze(1).to_broadcast([64, NB * H, TS]),
                              ALU.mult).then_inc(prepared, 1)
            for g in range(NG):
                for b in range(BG):
                    base = (g * BG + b) * NPG

                    def out(r, u, n):
                        if u % 2 == 0:
                            return
                        dve.wait_ge(k_turned, base + n + 1)
                        dve.wait_ge(page_scored, base + n + 1)
                        dve.tensor_copy(kt[:, 1], ktp[1][:]).then_inc(kt_out, 1)
                    rounds(dve, out)
                dve.wait_ge(scored, g + 1)
                dve.wait_ge(prepared, 1)
                dve.reduce_max(stat[:, 0:1], score[:, 0:KEYS], X).then_inc(maxed, 1)
                dve.wait_ge(maxed, g + 1)
                dve.tensor_scalar(stat[:, 1:2], stat[:, 0:1], -0.125, None, ALU.mult).then_inc(biased, 1)
                dve.wait_ge(exped, g + 1)
                dve.reciprocal(stat[:, 3:4], stat[:, 2:3]).then_inc(recip, 1)
                dve.wait_ge(recip, g + 1)
                dve.tensor_scalar(prob[:], prob[:], stat[:, 3:4], None, ALU.mult).then_inc(prob_ready, 1)
                for x in range(5):
                    dve.wait_ge(p_turned, 5 * g + x + 1)
                    if g:
                        dve.wait_ge(mixed, g * BG)
                    if x < 4:
                        dve.tensor_copy(probT[:, 4 * x:4 * x + 4, :], ktp[x % 2][:]).then_inc(p_kept, 1)
                    else:
                        dve.tensor_copy(probT[0:NS, NPG, :], ktp[x % 2][0:NS, 0, :]).then_inc(p_kept, 1)
                for b in range(BG):
                    s = g * BG + b
                    dve.wait_ge(mixed, s + 1)
                    for z in range(2):
                        half = slice(64 * z, 64 * z + 64)
                        ins = dve.tensor_copy(e.oaT[half, :, SEQ + s * TS:SEQ + (s + 1) * TS],
                                              ov[half, 0:NS].rearrange("p (j z t) -> p j z t", j=HP, z=2)[:, :, z, :])
                    ins.then_inc(o_kept, 1)


def stage_rwkv_project(e):
    e.fox_mem.close()
    e.obT = e.sb("obT", [P, HP, NT])
    e.rw_mem = e.ctx.enter_context(ExitStack())
    e.u = e.rw_mem.enter_context(e.nc.sbuf_tensor("u_rw", [P, 14, NT], F32))
    with memory(e) as (sb, ps), e.nc.Block() as block:
        project_tiles(e, "rw", sb, ps, block, 12, 14, e.u)


def stage_rwkv_prepare(e):
    nc, a, sem = e.nc, e.a, e.sem
    rw = lambda name, shape: e.rw_mem.enter_context(nc.sbuf_tensor(name, shape, F32))
    e.alpha, e.beta = rw("alpha", [P, HP, NT]), rw("beta", [P, HP, NT])
    e.rho, e.gamma, e.val = e.u[:, 0:4], e.u[:, 4:8], e.u[:, 8:12]
    e.chunk_decay = rw("chunk_decay", [P, HP, NCH])
    e.dec_s = rw("dec_s", [P, HP, NS])
    loaded, shifted, stored = sem("lora_loaded"), sem("rw_shifted"), sem("shift_stored")
    shift_kept = sem("shift_kept")
    tanh_done, sg, sa = sem("rw_tanh"), sem("rw_sig_z"), sem("rw_sig_a")
    made_z, made_a, sq_done, made_s = sem("rw_made_z"), sem("rw_made_a"), sem("rw_sq"), sem("rw_made_s")
    ss_max, rt, exps, rk_ready, made_b, bonus_done = (sem("rw_ss_max"), sem("rw_root"), sem("rw_exps"),
                                                      sem("rw_rk"), sem("rw_made_b"), sem("rw_bonus"))
    cum_ready, pair_done = sem("rw_cum"), sem("rw_pair_done")
    st = e.steps["dve"]
    with memory(e) as (sb, ps), nc.Block() as block:
        lora, lg = sb("lora_w", [P, W]), None
        old = sb("shift_old", [P, 14, NB])
        last = sb("shift_last", [P, 14, NB + 1])
        t0, t1, t2, t3, t4 = (sb(f"rw_t{n}", [P, NT]) for n in range(5))
        keep = sb("keep", [P, SEQ])
        zp, ap_ = ps("rw_zp", [P, 3, 512]), ps("rw_ap", [P, 3, 512])

        @block.sync
        def _(sp):
            sp.dma_start(old[:], a["shiftT"]).then_inc(loaded, 16)
            sp.dma_start(lora[0:64, :], a["w2"]).then_inc(loaded, 16)
            sp.dma_start(lora[64:P, :], a["a2"]).then_inc(loaded, 16)
            sp.wait_ge(shift_kept, 1)
            sp.dma_start(a["shift_out"], last[:]).then_inc(stored, 16)
            sp.wait_ge(stored, 16)

        @block.tensor
        def _(pe):
            pe.wait_ge(tanh_done, 1)
            for p in range(HP):
                if p:
                    pe.wait_ge(pair_done, p)
                for c, (at, n) in enumerate(COLS):
                    mm = pe.matmul(zp[:, c, 0:n], lora[0:64, p * P:(p + 1) * P], e.u[0:64, 12, at:at + n],
                                   start=True, stop=True)
                mm.then_inc(made_z, 1)
                for c, (at, n) in enumerate(COLS):
                    mm = pe.matmul(ap_[:, c, 0:n], lora[64:P, p * P:(p + 1) * P], e.u[64:P, 12, at:at + n],
                                   start=True, stop=True)
                mm.then_inc(made_a, 1)
                pe.wait_ge(sq_done, p + 1)
                pe.wait_ge(sg, p + 1)
                for c, (at, n) in enumerate(COLS):
                    mm = pe.matmul(zp[:, c, 0:n], e.c("head_ones"), t2[:, at:at + n], start=True, stop=True)
                mm.then_inc(made_s, 1)
                pe.wait_ge(rk_ready, p + 1)
                pe.wait_ge(sa, p + 1)
                for c, (at, n) in enumerate(COLS):
                    mm = pe.matmul(ap_[:, c, 0:n], e.c("head_ones"), t4[:, at:at + n], start=True, stop=True)
                mm.then_inc(made_b, 1)

        def cols(out, banks):
            yield out[:, 0:SEQ].rearrange("p (c n) -> p c n", c=2), banks[:, 0:2, :]
            yield out[:, SEQ:NT], banks[:, 2, 0:NS]

        @block.scalar
        def _(act):
            act.wait_ge(shifted, 14)
            act.activation(e.u[0:64, 12, :], e.u[0:64, 12, :], ACT.Tanh).then_inc(tanh_done, 1)
            act.activation(e.u[:, 13, :], e.u[:, 13, :], ACT.Sigmoid)
            for p in range(HP):
                if p:
                    act.wait_ge(pair_done, p)
                act.wait_ge(made_z, p + 1)
                for out, banks in cols(t0[:], zp):
                    ins = act.activation(out, banks, ACT.Sigmoid, bias=e.v("w0")[:, p:p + 1])
                ins.then_inc(sg, 1)
                act.wait_ge(made_a, p + 1)
                for out, banks in cols(t1[:], ap_):
                    ins = act.activation(out, banks, ACT.Sigmoid, bias=e.v("a0")[:, p:p + 1])
                ins.then_inc(sa, 1)
                act.activation(t2[:], e.gamma[:, p], ACT.Square, scale=e.v("k_k")[:, p:p + 1]).then_inc(sq_done, 1)
                act.wait_ge(ss_max, p + 1)
                act.activation(t2[:], t2[:], ACT.Sqrt).then_inc(rt, 1)
                act.wait_ge(cum_ready, p + 1)
                act.activation(t3[:, 0:SEQ], t3[:, 0:SEQ], ACT.Exp)
                act.activation(e.dec_s[:, p], t0[:, SEQ:NT], ACT.Exp)
                act.activation(t2[:, 0:SEQ], t0[:, 0:SEQ], ACT.Exp, scale=-1.0).then_inc(exps, 1)
                act.wait_ge(exps, 2 * p + 1)
                act.activation(t0[:, 0:SEQ], t0[:, 0:SEQ], ACT.Exp).then_inc(exps, 1)

        @block.vector
        def _(dve):
            st.then(dve, dve.memset(keep[:], 1.0))
            st.then(dve, dve.memset(keep[:, 0:SEQ:C], 0.0))
            dve.wait_ge(loaded, 48)
            dve.tensor_copy(last[:, :, 0:1], e.u[:, :, SEQ - 1:SEQ])
            dve.tensor_copy(last[:, :, 1:], e.u[:, :, SEQ + TS - 1:NT:TS]).then_inc(shift_kept, 1)
            samples = lambda x: x.rearrange("p (b t) -> p b t", t=TS)
            for j in range(14):
                d, u = (t0, t1)[j % 2], e.u[:, j]
                dve.tensor_tensor(d[:, 1:SEQ], u[:, 0:SEQ - 1], u[:, 1:SEQ], ALU.subtract)
                dve.tensor_scalar(d[:, 0:1], u[:, 0:1], -1.0, None, ALU.mult)
                ds_, us = samples(d[:, SEQ:NT]), samples(u[:, SEQ:NT])
                dve.tensor_tensor(ds_[:, :, 1:], us[:, :, 0:TS - 1], us[:, :, 1:], ALU.subtract)
                st.then(dve, dve.tensor_tensor(ds_[:, :, 0], old[:, j], us[:, :, 0], ALU.subtract))
                dve.scalar_tensor_tensor(u, d[:], e.v("mu")[:, j:j + 1], u, ALU.mult, ALU.add).then_inc(shifted, 1)
            dve.wait_ge(shifted, 14)
            for p in range(HP):
                r, k, v = e.rho[:, p], e.gamma[:, p], e.val[:, p]
                dve.wait_ge(sg, p + 1)
                st.then(dve, dve.tensor_scalar(t0[:], t0[:], -EXP_HALF, None, ALU.mult))
                st.then(dve, dve.tensor_tensor_scan(t3[:, 0:SEQ], keep[:], t0[:, 0:SEQ], 0.0, ALU.mult, ALU.add))
                dve.wait_ge(made_s, p + 1)
                for out, banks in cols(t2[:], zp):
                    ins = dve.tensor_scalar(out, banks, 1e-24, None, ALU.max)
                ins.then_inc(ss_max, 1)
                dve.wait_ge(rt, p + 1)
                st.then(dve, dve.reciprocal(t2[:], t2[:]))
                st.then(dve, dve.scalar_tensor_tensor(e.alpha[:, p], k, e.v("k_k")[:, p:p + 1], t2[:], ALU.mult, ALU.mult))
                st.then(dve, dve.tensor_tensor(e.beta[:, p], e.alpha[:, p], t1[:], ALU.mult))
                st.then(dve, dve.tensor_scalar(t1[:], t1[:], 1.0, e.v("k_a")[:, p:p + 1], ALU.subtract, ALU.mult))
                st.then(dve, dve.scalar_tensor_tensor(k, t1[:], 1.0, k, ALU.add, ALU.mult))
                dve.scalar_tensor_tensor(t4[:], r, e.v("r_k")[:, p:p + 1], k, ALU.mult, ALU.mult).then_inc(rk_ready, 1)
                st.then(dve, dve.tensor_tensor(t1[:, 0:SEQ], t3[:, 0:SEQ], t0[:, 0:SEQ], ALU.subtract))
                st.then(dve, dve.tensor_copy(t0[:, 0:SEQ], t3[:, 0:SEQ]))
                dve.tensor_copy(t3[:, 0:SEQ], t1[:, 0:SEQ]).then_inc(cum_ready, 1)
                dve.wait_ge(made_b, p + 1)
                vb = dict(zip("ab", [v[:, 0:SEQ].rearrange("p (c n) -> p c n", c=2), v[:, SEQ:NT]]))
                for (out, banks), vv in zip(cols(e.obT[:, p], ap_), vb.values()):
                    dve.tensor_tensor(out, banks, vv, ALU.mult)
                dve.wait_ge(exps, 2 * p + 1)
                m = slice(0, SEQ)
                dve.tensor_tensor(e.alpha[:, p, m], e.alpha[:, p, m], t3[:, m], ALU.mult)
                dve.tensor_tensor(e.beta[:, p, m], e.beta[:, p, m], t2[:, m], ALU.mult)
                dve.tensor_tensor(k[:, m], k[:, m], t2[:, m], ALU.mult)
                dve.wait_ge(exps, 2 * p + 2)
                dve.tensor_copy(e.chunk_decay[:, p], t0[:, C - 1:SEQ:C])
                dve.tensor_tensor(r[:, m], r[:, m], t0[:, m], ALU.mult).then_inc(pair_done, 1)


def stage_rwkv_scan(e):
    nc, a, sem = e.nc, e.a, e.sem
    stored = sem("scan_stored")
    names = ("staged made_g kept_g l_masked lt_ready masked t_ready made_tok kept_tok kept_v made_y kept_y made_z "
             "t_upd made_x kept_x made_u kept_u made_o made_s state_add state_ready gn_sum gn_cent gn_sq gn_var "
             "gn_root gn_rec gn_out o_turned o_stored go").split()
    q = {n: sem(f"scan_{n}") for n in names}
    NL = len(LEVELS) - 1
    with memory(e) as (sb, ps), nc.Block() as block:
        two = lambda name: sb(name, [P, 2, HP, C])
        ar = sb("ar", [P, 2, HP, 2, C])
        be, ga, va = two("be"), two("ga"), two("va")
        rbt, mt, rgt = two("rbt"), two("mt"), two("rgt")
        btok, gtok, vtok = two("btok"), two("gtok"), two("vtok")
        tt = two("tt")
        lt, ltm = sb("lt", [P, HP, C]), sb("ltm", [P, NL, HP, C])
        tl, ys = sb("tl", [P, HP, C]), sb("ys", [P, HP, C])
        xs, un = sb("xs", [P, HP, C]), sb("un", [P, HP, C])
        state, grown = sb("state_t", [P, HP, C]), sb("state_grown", [P, HP, C])
        cent, sqr = sb("gn_cent_t", [P, HP, C]), sb("gn_sqr", [P, HP, C])
        stat = sb("gn_stat", [P, 4, HP])
        g1, g2 = ps("g1", [P, HP, 2, C]), ps("g2", [P, HP, 2, C])
        g3, tk = ps("g3", [P, 2, HP, C]), ps("tk", [P, 2, HP, C])
        yp, zp = ps("yp", [P, 512]), ps("zp", [P, HP, 2, C])
        xp, op = ps("xp", [P, 2, HP, C]), ps("scan_op", [P, 2, HP, C])

        heads = [(p, slice(64 * s, 64 * s + 64)) for p in range(HP) for s in range(2)]
        bc = lambda x: x.unsqueeze(1).to_broadcast([P, HP, C])
        flat = lambda x: x.rearrange("p a n -> p (a n)")
        ypv = yp[:, 0:HP * C].rearrange("p (h n) -> p h n", h=HP)

        def schedule(eng, body):
            body(0, 0, True, False)
            with eng.Fori(0, NCH // 2 - 1) as i:
                body(2 * i + 1, 1, True, True)
                body(2 * i + 2, 0, True, True)
            body(NCH - 1, 1, True, True)
            body(NCH, 0, False, True)

        @block.gpsimd
        def _(pool):
            def stage(c, b):
                at = ds(c * C, C)
                pool.tensor_copy(ar[:, b, :, 0, :], e.alpha[:, :, at]).then_inc(q["staged"], 1)
                pool.tensor_copy(ar[:, b, :, 1, :], e.rho[:, :, at]).then_inc(q["staged"], 1)
                pool.tensor_copy(be[:, b], e.beta[:, :, at]).then_inc(q["staged"], 1)
                pool.tensor_copy(ga[:, b], e.gamma[:, :, at]).then_inc(q["staged"], 1)
                pool.tensor_copy(va[:, b], e.val[:, :, at]).then_inc(q["staged"], 1)
            stage(0, 0)
            stage(1, 1)
            with pool.Fori(1, NCH // 2) as i:
                for b in range(2):
                    pool.wait_ge(q["made_o"], 2 * i + b - 1)
                    stage(2 * i + b, b)

        @block.tensor
        def _(pe):
            ident = e.c("ident")

            def each(out, lhsT, rhs, start=True, stop=True):
                for p, hs in heads:
                    mm = pe.matmul(out(p, hs), lhsT(p, hs), rhs(p, hs), start=start, stop=stop)
                return mm

            def go():
                pe.sem_inc(q["go"], 1)

            def grams(c, b):
                pe.wait_ge(q["staged"], 5 * c + 5)
                pe.wait_ge(q["kept_g"], 3 * c)
                pe.wait_ge(q["kept_v"], c)
                pe.wait_ge(q["kept_tok"], 2 * c)
                go()
                both = lambda p, hs: flat(ar[hs, b, p])
                each(lambda p, hs: flat(g1[hs, p]), lambda p, hs: be[hs, b, p], both)
                each(lambda p, hs: flat(g2[hs, p]), lambda p, hs: ga[hs, b, p], both)
                each(lambda p, hs: g3[hs, 0, p], lambda p, hs: ar[hs, b, p, 0], lambda p, hs: be[hs, b, p])
                each(lambda p, hs: g3[hs, 1, p], lambda p, hs: va[hs, b, p], lambda p, hs: ident[hs, hs]).then_inc(q["made_g"], 1)
                each(lambda p, hs: tk[hs, 0, p], lambda p, hs: be[hs, b, p], lambda p, hs: ident[hs, hs])
                each(lambda p, hs: tk[hs, 1, p], lambda p, hs: ga[hs, b, p], lambda p, hs: ident[hs, hs]).then_inc(q["made_tok"], 1)

            def level_y(c, b, l):
                if l == 0:
                    pe.wait_ge(q["t_ready"], 2 * c + 2)
                    pe.wait_ge(q["masked"], c + 1)
                pe.wait_ge(q["t_upd"], c * NL + l)
                go()
                each(lambda p, hs: ypv[hs, p], lambda p, hs: ltm[hs, l, p], lambda p, hs: tl[hs, p]).then_inc(q["made_y"], 1)

            def level_z(c, b, l):
                pe.wait_ge(q["kept_y"], c * NL + l + 1)
                go()
                if l < NL - 1:
                    each(lambda p, hs: zp[hs, p, 0], lambda p, hs: tt[hs, b, p], lambda p, hs: ys[hs, p])
                each(lambda p, hs: zp[hs, p, 1], lambda p, hs: ys[hs, p], lambda p, hs: tt[hs, b, p]).then_inc(q["made_z"], 1)

            def x(c, b):
                pe.wait_ge(q["kept_tok"], 2 * c + 2)
                pe.wait_ge(q["kept_v"], c + 1)
                pe.wait_ge(q["kept_g"], 3 * c + 3)
                pe.wait_ge(q["state_ready"], c + 1)
                go()
                for p, hs in heads:
                    pe.matmul(xp[hs, 0, p], ar[hs, b, p, 0], state[hs, p], start=True, stop=False)
                    mm = pe.matmul(xp[hs, 0, p], mt[hs, b, p], vtok[hs, b, p], start=False, stop=True)
                mm.then_inc(q["made_x"], 1)

            def u(c, b):
                pe.wait_ge(q["kept_x"], c + 1)
                pe.wait_ge(q["t_upd"], NL * (c + 1))
                pe.wait_ge(q["o_stored"], c + 1)
                go()
                each(lambda p, hs: op[hs, 1, p], lambda p, hs: tt[hs, b, p], lambda p, hs: xs[hs, p]).then_inc(q["made_u"], 1)

            def s_and_o(c, b):
                pe.wait_ge(q["kept_u"], c + 1)
                go()
                for p, hs in heads:
                    pe.matmul(xp[hs, 1, p], btok[hs, b, p], un[hs, p], start=True, stop=False)
                    mm = pe.matmul(xp[hs, 1, p], gtok[hs, b, p], vtok[hs, b, p], start=False, stop=True)
                mm.then_inc(q["made_s"], 1)
                for p, hs in heads:
                    pe.matmul(op[hs, 0, p], ar[hs, b, p, 1], state[hs, p], start=True, stop=False)
                    pe.matmul(op[hs, 0, p], rbt[hs, b, p], un[hs, p], start=False, stop=False)
                    mm = pe.matmul(op[hs, 0, p], rgt[hs, b, p], vtok[hs, b, p], start=False, stop=True)
                mm.then_inc(q["made_o"], 1)

            def turn(c):
                pe.wait_ge(q["gn_out"], c + 1)
                go()
                each(lambda p, hs: op[hs, 1, p], lambda p, hs: sqr[hs, p], lambda p, hs: ident[hs, hs]).then_inc(q["o_turned"], 1)

            def body(c, b, A, B):
                d = 1 - b
                if B:
                    x(c - 1, d)
                if A:
                    grams(c, b)
                if B:
                    u(c - 1, d)
                if A:
                    level_y(c, b, 0)
                if B:
                    s_and_o(c - 1, d)
                if A:
                    level_z(c, b, 0)
                    for l in (1, 2):
                        level_y(c, b, l)
                        level_z(c, b, l)
                if B:
                    turn(c - 1)
                if A:
                    for l in range(3, NL):
                        level_y(c, b, l)
                        level_z(c, b, l)
            schedule(pe, body)

        @block.scalar
        def _(act):
            def body(c, b, A, B):
                m = c - 1

                def keep_y(l):
                    act.wait_ge(q["made_y"], c * NL + l + 1)
                    act.copy(ys[:], ypv).then_inc(q["kept_y"], 1)
                if B:
                    act.wait_ge(q["made_x"], m + 1)
                    act.copy(xs[:], xp[:, 0]).then_inc(q["kept_x"], 1)
                if A:
                    act.wait_ge(q["made_tok"], c + 1)
                    act.copy(btok[:, b], tk[:, 0]).then_inc(q["kept_tok"], 1)
                    act.copy(gtok[:, b], tk[:, 1]).then_inc(q["kept_tok"], 1)
                if B:
                    act.wait_ge(q["made_u"], m + 1)
                    act.mul(un[:], op[:, 1], -1.0).then_inc(q["kept_u"], 1)
                if A:
                    act.wait_ge(q["l_masked"], c + 1)
                    act.copy(vtok[:, b], g3[:, 1]).then_inc(q["kept_v"], 1)
                    keep_y(0)
                    keep_y(1)
                if B:
                    act.wait_ge(q["gn_var"], m + 1)
                    act.activation(stat[:, 2], stat[:, 1], ACT.Sqrt, scale=1.0 / DH, bias=e.eps[:, 1:2]).then_inc(q["gn_root"], 1)
                if A:
                    keep_y(2)
                if B:
                    act.wait_ge(q["o_turned"], m + 1)
                    act.copy(e.alpha[:, :, ds(m * C, C)], op[:, 1]).then_inc(q["o_stored"], 1)
                if A:
                    for l in range(3, NL):
                        keep_y(l)
            act.sem_inc(q["o_stored"], 1)
            schedule(act, body)

        @block.vector
        def _(dve):
            dve.memset(state[:], 0.0).then_inc(q["state_ready"], 1)

            def prepare(c, b):
                dve.wait_ge(q["made_g"], c + 1)
                dve.tensor_copy(lt[:], g1[:, :, 0, :]).then_inc(q["lt_ready"], 1)
                dve.tensor_tensor(tl[:], g3[:, 0], bc(e.c("level0")), ALU.mult).then_inc(q["l_masked"], 1)
                dve.wait_ge(q["lt_ready"], 2 * c + 1)
                dve.tensor_tensor(tt[:, b], lt[:], bc(e.c("levels_t")[:, 0:C]), ALU.mult).then_inc(q["lt_ready"], 1)
                dve.wait_ge(q["l_masked"], c + 1)
                dve.tensor_tensor(tl[:], tl[:], bc(e.c("lower_eye")), ALU.add).then_inc(q["t_ready"], 1)
                dve.wait_ge(q["lt_ready"], 2 * c + 2)
                dve.tensor_tensor(tt[:, b], tt[:, b], bc(e.c("lower_eye")), ALU.add).then_inc(q["t_ready"], 1)
                for l in range(NL):
                    ins = dve.tensor_tensor(ltm[:, l], lt[:], bc(e.c("levels_t")[:, (l + 1) * C:(l + 2) * C]), ALU.mult)
                ins.then_inc(q["masked"], 1)
                dve.tensor_tensor(rbt[:, b], g1[:, :, 1, :], bc(e.c("upper_diag")), ALU.mult).then_inc(q["kept_g"], 1)
                dve.tensor_tensor(mt[:, b], g2[:, :, 0, :], bc(e.c("upper")), ALU.mult).then_inc(q["kept_g"], 1)
                dve.tensor_tensor(rgt[:, b], g2[:, :, 1, :], bc(e.c("upper_diag")), ALU.mult).then_inc(q["kept_g"], 1)

            def update(c, b, l):
                n = c * NL + l
                dve.wait_ge(q["made_z"], n + 1)
                dve.wait_ge(q["t_ready"], 2 * c + 2)
                dve.wait_ge(q["t_upd"], n)
                if l < NL - 1:
                    dve.tensor_tensor(tl[:], tl[:], zp[:, :, 0, :], ALU.subtract)
                dve.tensor_tensor(tt[:, b], tt[:, b], zp[:, :, 1, :], ALU.subtract).then_inc(q["t_upd"], 1)

            def new_state(c):
                dve.wait_ge(q["made_o"], c + 1)
                dve.tensor_tensor(grown[:], state[:], xp[:, 1], ALU.add).then_inc(q["state_add"], 1)
                dve.wait_ge(q["state_add"], c + 1)
                dve.tensor_tensor(state[:], grown[:], e.chunk_decay[:, :, ds(c, 1)].to_broadcast([P, HP, C]),
                                  ALU.mult).then_inc(q["state_ready"], 1)

            def centre(c):
                dve.reduce_sum(stat[:, 0], op[:, 0], X).then_inc(q["gn_sum"], 1)
                dve.wait_ge(q["gn_sum"], c + 1)
                dve.scalar_tensor_tensor(cent[:], stat[:, 0].unsqueeze(2).to_broadcast([P, HP, C]), -1.0 / DH, op[:, 0],
                                         ALU.mult, ALU.add).then_inc(q["gn_cent"], 1)
                dve.wait_ge(q["gn_cent"], c + 1)
                dve.tensor_tensor(sqr[:], cent[:], cent[:], ALU.mult).then_inc(q["gn_sq"], 1)
                dve.wait_ge(q["gn_sq"], c + 1)
                dve.reduce_sum(stat[:, 1], sqr[:], X).then_inc(q["gn_var"], 1)

            def normalise(c):
                dve.wait_ge(q["gn_root"], c + 1)
                dve.reciprocal(stat[:, 3], stat[:, 2]).then_inc(q["gn_rec"], 1)
                dve.wait_ge(q["gn_rec"], c + 1)
                dve.tensor_tensor(sqr[:], cent[:], stat[:, 3].unsqueeze(2).to_broadcast([P, HP, C]),
                                  ALU.mult).then_inc(q["gn_out"], 1)

            def body(c, b, A, B):
                if A:
                    prepare(c, b)
                if B:
                    new_state(c - 1)
                if A:
                    update(c, b, 0)
                if B:
                    centre(c - 1)
                if A:
                    update(c, b, 1)
                if B:
                    normalise(c - 1)
                if A:
                    for l in range(2, NL):
                        update(c, b, l)
            schedule(dve, body)

        @block.sync
        def _(sp):
            sp.wait_ge(q["state_ready"], NCH + 1)
            sp.dma_start(a["wkv_prompt"], state[:]).then_inc(stored, 16)
            sp.wait_ge(stored, 16)


def stage_rwkv_sample(e):
    nc, a, sem = e.nc, e.a, e.sem
    st = e.steps["dve"]
    turned, kept, sent, back, loaded = sem("rs_turned"), sem("rs_kept"), sem("rs_sent"), sem("rs_back"), sem("rs_loaded")
    outer, o_ready, o_sent, o_back = sem("rs_outer"), sem("rs_o_ready"), sem("rs_o_sent"), sem("rs_o_back")
    var, root, oh_ready, o_turned = sem("rs_var"), sem("rs_root"), sem("rs_oh"), sem("rs_o_turned")
    gate_made, gate_used, ready = sem("rs_gate_made"), sem("rs_gate_used"), sem("rs_v_ready")
    state_done, stored, used = sem("rs_state_done"), sem("rs_stored"), sem("rs_outer_used")
    NV = 6
    with memory(e) as (sb, ps), nc.Block() as block:
        g2w = sb("g2w", [P, W])
        vec = sb("rs_vec", [P, NV, TS, DH])
        vz = sb("rs_vz", [P, TS, DH // 2])
        o = sb("rs_o", [P, TS, DH // 2])
        nsk = sb("rs_nsk", [P, DH // 2])
        stat = sb("rs_stat", [NS, 4, H])
        ot, cent, sq = (sb(f"rs_tok{n}", [NS, H, DH]) for n in range(3))
        flat = lambda x: x.rearrange("p h n -> p (h n)")
        cube = lambda x: flat(x)[:, 0:2048].rearrange("p (v k) -> p v k", k=DH)
        vt = flat(e.gamma)[0:NS, 0:NV * W].rearrange("p (v c) -> p v c", v=NV)
        state, tmp = cube(e.beta), flat(e.beta)[:, 2048:4096].rearrange("p (v k) -> p v k", k=DH)
        prod = cube(e.gamma)
        scr = sb("rs_scr", [P, NT])
        tp = ps("rs_t", [NS, NV, W])
        gp = ps("rs_g", [P, 2, 512])

        @block.sync
        def _(sp):
            sp.dma_start(g2w[:], a["g2"]).then_inc(loaded, 16)
            sp.wait_ge(kept, 1)
            sp.dma_start(e.sv_d.rearrange("v t c -> t v c"), vt).then_inc(sent, 16)
            for z in range(2):
                sp.dma_start(flat(e.beta)[64 * z:64 * z + 64, 0:2048],
                             a["state"].rearrange("b h (z v) k -> z (b h) (v k)", z=2)[z]).then_inc(back, 16)
            sp.wait_ge(sent, 16)
            for z in range(2):
                for b in range(NB):
                    for v in range(NV):
                        sp.dma_start(vec[64 * z + 8 * b:64 * z + 8 * b + 8, v],
                                     e.sv_d[v, b * TS:(b + 1) * TS, :].rearrange("t (h d) -> h t d", h=H)).then_inc(back, 16)
            sp.wait_ge(o_ready, TS)
            for z in range(2):
                for b in range(NB):
                    sp.dma_start(e.so_d[b * TS:(b + 1) * TS, :].rearrange("t (h z v) -> z h t v", h=H, z=2)[z],
                                 o[64 * z + 8 * b:64 * z + 8 * b + 8]).then_inc(o_sent, 16)
            sp.wait_ge(o_sent, 16 * 2 * NB)
            sp.dma_start(ot[:].rearrange("p h d -> p (h d)"), e.so_d).then_inc(o_back, 16)
            for z in range(2):
                sp.dma_start(a["wkv_sample"].rearrange("b h (z v) k -> z (b h) (v k)", z=2)[z],
                             flat(e.beta)[64 * z:64 * z + 64, 0:2048]).then_inc(stored, 16)
            sp.wait_ge(stored, 32)

        @block.tensor
        def _(pe):
            for v, src in enumerate((e.alpha, e.beta, e.gamma, e.rho, e.val, e.dec_s)):
                for p in range(HP):
                    col = src[:, p, SEQ:NT] if v < 5 else src[:, p]
                    mm = pe.transpose(tp[:, v, p * P:(p + 1) * P], col, e.c("ident"))
            mm.then_inc(turned, 1)
            pe.wait_ge(loaded, 16)
            pe.wait_ge(oh_ready, 1)
            pe.wait_ge(kept, 1)
            for p in range(HP):
                mm = pe.transpose(gp[:, 0, p * NS:(p + 1) * NS], sq[:].rearrange("p h d -> p (h d)")[:, p * P:(p + 1) * P],
                                  e.c("ident")[0:NS, 0:NS])
            mm.then_inc(o_turned, 1)
            n = 0
            for p in range(HP):
                for at, m in COLS:
                    pe.wait_ge(gate_used, max(1, n))
                    pe.wait_ge(ready, 1)
                    pe.matmul(gp[:, n % 2, 0:m], g2w[:, p * P:(p + 1) * P], e.u[:, 13, at:at + m],
                              start=True, stop=True).then_inc(gate_made, 1)
                    n += 1

        @block.gpsimd
        def _(pool):
            pool.wait_ge(ready, 1)
            for t in range(TS):
                if t:
                    pool.wait_ge(used, t)
                pool.tensor_tensor(prod, vz[:, t].unsqueeze(2).to_broadcast([P, DH // 2, DH]),
                                   vec[:, 2, t].unsqueeze(1).to_broadcast([P, DH // 2, DH]), ALU.mult).then_inc(outer, 1)

        @block.scalar
        def _(act):
            act.wait_ge(var, 1)
            act.activation(stat[:, 2], stat[:, 1], ACT.Sqrt, scale=1.0 / DH, bias=e.eps[0:NS, 1:2]).then_inc(root, 1)

        @block.vector
        def _(dve):
            dve.wait_ge(turned, 1)
            dve.tensor_copy(vt, tp[:]).then_inc(kept, 1)
            dve.wait_ge(back, 16 * (2 + 2 * NB * NV))
            for z in range(2):
                h = slice(64 * z, 64 * z + 64)
                ins = dve.tensor_copy(vz[h], vec[h, 4, :, 32 * z:32 * z + 32])
                st.done(ins)
            st.settle(dve)
            dve.sem_inc(ready, 1)
            row = lambda v, t: vec[:, v, t].unsqueeze(1).to_broadcast([P, DH // 2, DH])
            for t in range(TS):
                if t:
                    dve.wait_ge(o_ready, t)
                st.then(dve, dve.tensor_tensor(tmp, state, row(0, t), ALU.mult))
                st.done(dve.tensor_reduce(nsk[:], tmp, X, ALU.add, negate=True))
                st.then(dve, dve.tensor_tensor(state, state, row(5, t), ALU.mult))
                st.then(dve, dve.tensor_tensor(tmp, nsk[:].unsqueeze(2).to_broadcast([P, DH // 2, DH]), row(1, t), ALU.mult))
                st.then(dve, dve.tensor_tensor(state, state, tmp, ALU.add))
                dve.wait_ge(outer, t + 1)
                dve.tensor_tensor(state, state, prod, ALU.add).then_inc(used, 1)
                dve.wait_ge(used, t + 1)
                st.then(dve, dve.tensor_tensor(tmp, state, row(3, t), ALU.mult))
                dve.tensor_reduce(o[:, t], tmp, X, ALU.add).then_inc(o_ready, 1)
            dve.wait_ge(o_back, 16)
            st.then(dve, dve.reduce_sum(stat[:, 0], ot[:], X))
            wide = lambda x: x.unsqueeze(2).to_broadcast([NS, H, DH])
            st.then(dve, dve.scalar_tensor_tensor(cent[:], wide(stat[:, 0]), -1.0 / DH, ot[:], ALU.mult, ALU.add))
            st.then(dve, dve.tensor_tensor(sq[:], cent[:], cent[:], ALU.mult))
            dve.reduce_sum(stat[:, 1], sq[:], X).then_inc(var, 1)
            dve.wait_ge(root, 1)
            st.then(dve, dve.reciprocal(stat[:, 3], stat[:, 2]))
            dve.tensor_tensor(sq[:], cent[:], wide(stat[:, 3]), ALU.mult).then_inc(oh_ready, 1)
            dve.wait_ge(o_turned, 1)
            st.then(dve, dve.tensor_copy(e.alpha[:, :, SEQ:NT], gp[:, 0, 0:HP * NS].rearrange("p (h n) -> p h n", h=HP)))
            dve.sem_inc(gate_used, 1)
            n = 0
            for p in range(HP):
                st.then(dve, dve.tensor_scalar(scr[:], e.alpha[:, p], e.v("lnx_w")[:, p:p + 1], e.v("lnx_b")[:, p:p + 1],
                                               ALU.mult, ALU.add))
                st.then(dve, dve.tensor_tensor(e.obT[:, p], e.obT[:, p], scr[:], ALU.add))
                for at, m in COLS:
                    dve.wait_ge(gate_made, n + 1)
                    dve.tensor_tensor(e.obT[:, p, at:at + m], e.obT[:, p, at:at + m], gp[:, n % 2, 0:m],
                                      ALU.mult).then_inc(gate_used, 1)
                    n += 1


def stage_mix(e):
    nc, a, sem = e.nc, e.a, e.sem
    e.rw_mem.close()
    e.mixedT = e.sb("mixedT", [P, KD, NT])
    loaded = [sem(f"mix_w_loaded{b}") for b in range(2)]
    made, gated, summed, prods = sem("mix_made"), sem("mix_gated"), sem("mix_summed"), sem("mix_prods")
    with memory(e) as (sb, ps), nc.Block() as block:
        w = sb("mix_w", [P, 2, 24, P])
        banks = [ps(f"mix_b{b}", [P, 4, 512]) for b in range(2)]
        gate = sb("mix_gate", [P, 2, 2, 512])
        part = sb("mix_part", [P, 2, 512])
        items = [(c, at, m) for c, (at, m) in enumerate(COLS)]

        @block.sync
        def _(sp):
            def load(j, b):
                sp.dma_start(w[:, b, 0:8], a["w_in"][ds(j + 26, 1)].squeeze(0)).then_inc(loaded[b], 16)
                sp.dma_start(w[:, b, 8:16], a["w_in"][ds(j + 34, 1)].squeeze(0)).then_inc(loaded[b], 16)
                sp.dma_start(w[:, b, 16:24], a["p_ab"][ds(j, 1)].squeeze(0)).then_inc(loaded[b], 16)
            load(0, 0)
            load(1, 1)
            with sp.Fori(0, KD // 2 - 1) as i:
                for b in range(2):
                    sp.wait_ge(made, 3 * (2 * i + b + 1))
                    load(2 * i + b + 2, b)

        def loop(eng, body):
            with eng.Fori(0, KD // 2) as i:
                for b in range(2):
                    for c, at, m in items:
                        body(2 * i + b, b, i, (3 * b + c) % 2, c, at, m, 6 * i + 3 * b + c)

        @block.tensor
        def _(pe):
            pe.sem_inc(summed, 2)

            def body(j, b, i, x, c, at, m, n):
                if c == 0:
                    pe.wait_ge(loaded[b], 48 * (i + 1))
                pe.wait_ge(summed, n + 1)
                for g in range(2):
                    for k in range(KD):
                        pe.matmul(banks[x][:, g, 0:m], w[:, b, 8 * g + k, :], e.xnT[:, k, at:at + m], start=(k == 0), stop=(k == KD - 1))
                for g, src in enumerate((e.oaT, e.obT)):
                    for k in range(HP):
                        mm = pe.matmul(banks[x][:, 2 + g, 0:m], w[:, b, 16 + 4 * g + k, :], src[:, k, at:at + m],
                                       start=(k == 0), stop=(k == HP - 1))
                mm.then_inc(made, 1)
            loop(pe, body)

        @block.scalar
        def _(act):
            def body(j, b, i, x, c, at, m, n):
                act.wait_ge(made, n + 1)
                act.wait_ge(summed, n + 1)
                act.activation(gate[:, x, :, 0:m], banks[x][:, 0:2, 0:m], ACT.Sigmoid).then_inc(gated, 1)
            loop(act, body)

        @block.vector
        def _(dve):
            def body(j, b, i, x, c, at, m, n):
                dve.wait_ge(gated, n + 1)
                dve.wait_ge(made, n + 1)
                dve.wait_ge(summed, n + 2)
                dve.tensor_tensor(part[:, :, 0:m], gate[:, x, :, 0:m], banks[x][:, 2:4, 0:m], ALU.mult).then_inc(prods, 1)
                dve.wait_ge(prods, n + 1)
                dve.tensor_tensor(e.mixedT[:, ds(j, 1), at:at + m].squeeze(1), part[:, 0, 0:m], part[:, 1, 0:m],
                                  ALU.add).then_inc(summed, 1)
            loop(dve, body)


def stage_out_and_route(e):
    nc, a, sem = e.nc, e.a, e.sem
    st = e.steps["dve"]
    e.count = e.sb("count", [1, NE + 1], I32)
    w_loaded = sem("wo_loaded")
    x_loaded, made, added, sq, std, rstd = sem("xr_loaded"), sem("wo_made"), sem("x1_added"), sem("x1_sq"), sem("x1_std"), sem("x1_rstd")
    h_ready, h_stored, h_turned, hT_ready, logits_made, logits_kept = (
        sem("h_ready"), [sem(f"h_stored{b}") for b in range(2)], sem("h_turned"), sem("hT_ready"), sem("logits_made"), sem("logits_kept"))
    r_exp_in, r_exped, r_exp2_in, r_exped2, m_ready, ranked = (sem("r_exp_in"), sem("r_exped"), sem("r_exp2_in"),
                                                              sem("r_exped2"), sem("r_m_ready"), sem("r_ranked"))
    ent_ready, table_set, scattered, table_zero = sem("ent_ready"), sem("table_set"), sem("scattered"), sem("table_zero")
    with memory(e) as (sb, ps), nc.Block() as block:
        wo, wr = sb("wo", [P, KD, D]), sb("wr", [P, KD, GR + NE])
        xt = e.x1
        hx = sb("hx_t", [P, 2, D])
        hT = sb("hT", [P, 2, KD, P])
        junk = sb("h_junk", [P, D])
        stat = sb("h_stat", [P, 3, NTT])
        lg = sb("logits", [P, NTT, GR + NE])
        n9 = lambda name, k=NE: sb(f"r_{name}", [P, NTT, k])
        gd, eq, ohg, bias4 = n9("gd", GR), n9("eq", GR), n9("ohg", GR), n9("bias4", GR)
        el, cand, o1, o2, both, prev, tmp = (n9(x) for x in "el cand o1 o2 both prev tmp".split())
        s = sb("r_small", [P, 16, NTT])
        slot = sb("slot", [P, NTT, 2], I32)
        ent = sb("ent", [P, NTT, 2, 4], I32)
        total = sb("r_total", [P, NE + 1])
        empty = sb("empty", [P, NE * e.CAP // P * 4], I32)
        xp = [ps(f"x1_p{b}", [P, 2, 512]) for b in range(2)]
        hp = ps("h_p", [P, KD, P])
        lp = ps("lg_p", [P, 512])
        rp = ps("rank_p", [P, 512])

        @block.sync
        def _(sp):
            sp.dma_start(wo[:], a["w_o"].rearrange("(k p) n -> p k n", p=P)).then_inc(w_loaded, 16)
            sp.dma_start(wr[:], a["w_route"]).then_inc(w_loaded, 16)
            sp.dma_start(xt[:], a["x"].rearrange("(t p) d -> p t d", p=P)).then_inc(x_loaded, 16)
            sp.wait_ge(table_zero, 1)
            sp.dma_start(e.table_d.rearrange("(p n) c -> p (n c)", p=P), empty[:]).then_inc(table_set, 16)
            for t in range(NTT):
                sp.wait_ge(h_ready, t + 1)
                sp.dma_start(e.h_d[t * P:(t + 1) * P, :], hx[:, t % 2]).then_inc(h_stored[t % 2], 16)

        @block.tensor
        def _(pe):
            pe.wait_ge(w_loaded, 32)

            def out(t):
                n = min(P, NT - t * P)
                if t >= 2:
                    pe.wait_ge(added, t - 1)
                for k in range(KD):
                    for c in range(2):
                        mm = pe.matmul(xp[t % 2][0:n, c], e.mixedT[:, k, t * P:t * P + n], wo[:, k, c * 512:(c + 1) * 512],
                                       start=(k == 0), stop=(k == KD - 1))
                mm.then_inc(made, 1)

            def route(t):
                pe.wait_ge(h_ready, t + 1)
                if t:
                    pe.wait_ge(hT_ready, t)
                for k in range(KD):
                    mm = pe.transpose(hp[:, k], hx[:, t % 2, k * P:(k + 1) * P], e.c("ident"))
                mm.then_inc(h_turned, 1)
                pe.wait_ge(hT_ready, t + 1)
                if t:
                    pe.wait_ge(logits_kept, t)
                for k in range(KD):
                    mm = pe.matmul(lp[:, 0:GR + NE], hT[:, t % 2, k], wr[:, k], start=(k == 0), stop=(k == KD - 1))
                mm.then_inc(logits_made, 1)
            out(0)
            for t in range(NTT):
                if t + 1 < NTT:
                    out(t + 1)
                route(t)
            pe.wait_ge(m_ready, 1)
            pe.matmul(rp[:, 0:NTT * NE], e.c("before"), both[:].rearrange("p t e -> p (t e)"), start=True, stop=False)
            pe.matmul(rp[:, 0:NTT * NE], e.ones[:, 0:P], prev[:].rearrange("p t e -> p (t e)"), start=False, stop=True)
            pe.matmul(rp[:, 480:480 + NE], e.ones[:, 0:P], total[:, 0:NE], start=True, stop=True).then_inc(ranked, 1)

        @block.scalar
        def _(act):
            for t in range(NTT):
                act.wait_ge(added, t + 1)
                act.activation(junk[:], e.x1[:, t], ACT.Square, accum_out=stat[:, 0, t:t + 1]).then_inc(sq, 1)
                act.wait_ge(sq, t + 1)
                act.activation(stat[:, 1, t:t + 1], stat[:, 0, t:t + 1], ACT.Sqrt, scale=1.0 / D,
                               bias=e.eps[:, 0:1]).then_inc(std, 1)
            act.wait_ge(r_exp_in, 1)
            act.activation(gd[:], gd[:], ACT.Exp).then_inc(r_exped, 1)
            act.wait_ge(r_exp2_in, 1)
            act.activation(s[:, 8], s[:, 7], ACT.Exp).then_inc(r_exped2, 1)

        @block.gpsimd
        def _(pool):
            pool.memset(empty[:], 1 << 24).then_inc(table_zero, 1)
            pool.wait_ge(ent_ready, 1)
            pool.wait_ge(table_set, 16)
            for t in range(NTT):
                for j in range(2):
                    pool.indirect_dma_start(out=e.table_d, out_offset=bass.IndirectOffsetOnAxis(ap=slot[:, t, j:j + 1], axis=0),
                                            in_=ent[:, t, j], in_offset=None, bounds_check=NE * e.CAP - 1,
                                            oob_is_err=False).then_inc(scattered, 16)
            pool.wait_ge(scattered, 16 * 2 * NTT)
            for b in range(2):
                pool.wait_ge(h_stored[b], 16 * ((NTT + 1 - b) // 2))

        @block.vector
        def _(dve):
            dve.wait_ge(x_loaded, 16)

            def add(t):
                n = min(P, NT - t * P)
                dve.wait_ge(made, t + 1)
                dve.tensor_tensor(e.x1[0:n, t], e.x1[0:n, t], xp[t % 2][0:n].rearrange("p c n -> p (c n)"),
                                  ALU.add).then_inc(added, 1)

            def norm(t):
                dve.wait_ge(std, t + 1)
                dve.reciprocal(stat[:, 2, t:t + 1], stat[:, 1, t:t + 1]).then_inc(rstd, 1)
                dve.wait_ge(rstd, t + 1)
                if t >= 2:
                    dve.wait_ge(h_stored[t % 2], 16 * (t // 2))
                dve.tensor_scalar(hx[:, t % 2], e.x1[:, t], stat[:, 2, t:t + 1], None, ALU.mult).then_inc(h_ready, 1)
                dve.wait_ge(h_turned, t + 1)
                dve.tensor_tensor(hT[:, t % 2], hp[:], e.v("norm_ffn").unsqueeze(2).to_broadcast([P, KD, P]),
                                  ALU.mult).then_inc(hT_ready, 1)
                dve.wait_ge(logits_made, t + 1)
                dve.tensor_copy(lg[:, t], lp[:, 0:GR + NE]).then_inc(logits_kept, 1)
            add(0)
            for t in range(NTT):
                if t + 1 < NTT:
                    add(t + 1)
                norm(t)
            dve.wait_ge(logits_kept, NTT)
            G, E = lg[:, :, 0:GR], lg[:, :, GR:]
            w4 = lambda x: x.unsqueeze(2).to_broadcast([P, NTT, GR])
            w32 = lambda x: x.unsqueeze(2).to_broadcast([P, NTT, NE])
            iota = lambda k: e.c("expert_id")[:, 0:k].unsqueeze(1).to_broadcast([P, NTT, k])
            by_group = lambda x: x.rearrange("p t (g k) -> p (t g) k", g=GR)
            do = lambda ins: st.then(dve, ins)
            do(dve.reduce_max(s[:, 0], G, X))
            dve.tensor_tensor(gd[:], G, w4(s[:, 0]), ALU.subtract).then_inc(r_exp_in, 1)
            do(dve.tensor_tensor(eq[:], G, w4(s[:, 0]), ALU.is_equal))
            do(dve.scalar_tensor_tensor(eq[:], eq[:], -99.0, iota(GR), ALU.mult, ALU.add))
            do(dve.tensor_reduce(s[:, 1], eq[:], X, ALU.min))
            do(dve.tensor_tensor(ohg[:], eq[:], w4(s[:, 1]), ALU.is_equal))
            dve.wait_ge(r_exped, 1)
            do(dve.reduce_sum(s[:, 2], gd[:], X))
            do(dve.reciprocal(s[:, 2], s[:, 2]))
            do(dve.tensor_scalar(bias4[:], ohg[:], -NEG, NEG, ALU.mult, ALU.add))
            wide = lambda x: x.rearrange("p t g -> p (t g)").unsqueeze(2).to_broadcast([P, NTT * GR, EPG])
            do(dve.tensor_copy(el[:], E))
            do(dve.tensor_tensor(by_group(el[:]), by_group(el[:]), wide(ohg[:]), ALU.mult))
            do(dve.tensor_tensor(by_group(el[:]), by_group(el[:]), wide(bias4[:]), ALU.add))

            def first_largest(at, onehot):
                do(dve.reduce_max(s[:, at], el[:], X))
                do(dve.tensor_tensor(cand[:], el[:], w32(s[:, at]), ALU.is_equal))
                do(dve.scalar_tensor_tensor(cand[:], cand[:], -99.0, iota(NE), ALU.mult, ALU.add))
                do(dve.tensor_reduce(s[:, at + 1], cand[:], X, ALU.min))
                do(dve.tensor_tensor(onehot[:], cand[:], w32(s[:, at + 1]), ALU.is_equal))
            first_largest(3, o1)
            do(dve.scalar_tensor_tensor(el[:], o1[:], 3 * NEG, el[:], ALU.mult, ALU.add))
            first_largest(5, o2)
            dve.tensor_tensor(s[:, 7], s[:, 5], s[:, 3], ALU.subtract).then_inc(r_exp2_in, 1)
            dve.wait_ge(r_exped2, 1)
            do(dve.tensor_scalar(s[:, 9], s[:, 8], 1.0, None, ALU.add))
            do(dve.reciprocal(s[:, 9], s[:, 9]))
            do(dve.tensor_tensor(s[:, 9], s[:, 9], s[:, 2], ALU.mult))
            do(dve.tensor_tensor(s[:, 10], s[:, 9], s[:, 8], ALU.mult))
            last = slice(NTT - 1, NTT)
            for o in (o1, o2):
                do(dve.tensor_scalar(o[:, NTT - 1], o[:, NTT - 1], e.c("is_sample"), None, ALU.mult))
            do(dve.tensor_tensor(both[:], o1[:], o2[:], ALU.add))
            do(dve.memset(prev[:, 0], 0.0))
            for t in range(NTT - 1):
                do(dve.tensor_tensor(prev[:, t + 1], prev[:, t], both[:, t], ALU.add))
            dve.tensor_tensor(total[:, 0:NE], prev[:, NTT - 1], both[:, NTT - 1], ALU.add).then_inc(m_ready, 1)
            dve.wait_ge(ranked, 1)
            rank = rp[:, 0:NTT * NE].rearrange("p (t e) -> p t e", t=NTT)
            for j, (o, at) in enumerate(((o1, 4), (o2, 6))):
                do(dve.tensor_tensor(tmp[:], o[:], rank, ALU.mult))
                do(dve.reduce_sum(s[:, 11 + j], tmp[:], X))
                do(dve.tensor_scalar(s[:, at], s[:, at], 99.0, float(e.CAP), ALU.add, ALU.mult))
                do(dve.tensor_tensor(s[:, 11 + j], s[:, 11 + j], s[:, at], ALU.add))
                do(dve.scalar_tensor_tensor(s[:, 11 + j, last], s[:, 11 + j, last], e.c("is_sample"), e.c("beyond"), ALU.mult, ALU.add))
                do(dve.tensor_copy(slot[:, :, j], s[:, 11 + j]))
                do(dve.tensor_copy(ent[:, :, j, 0], e.c("token")))
                do(dve.tensor_scalar(s[:, 13], e.c("token"), 2.0, float(j), ALU.mult, ALU.add))
                do(dve.tensor_copy(ent[:, :, j, 1], s[:, 13]))
                do(dve.tensor_copy(ent[:, :, j, 2].bitcast(F32), s[:, 9 + j]))
                do(dve.tensor_copy(ent[:, :, j, 3], e.c("token")))
            do(dve.tensor_copy(total[:, 0:NE], rp[:, 480:480 + NE]))
            do(dve.reduce_max(total[:, NE:NE + 1], total[:, 0:NE], X))
            dve.tensor_copy(e.count[:], total[0:1, :]).then_inc(ent_ready, 1)


def stage_moe(e):
    nc, a, sem = e.nc, e.a, e.sem
    NW = 3
    w_loaded = [sem(f"we_loaded{b}") for b in range(NW)]
    names = "ent_loaded gathered turned hT_ready made_gu silu acted a_turned aT_ready made_y y_dve y_act scattered zero go"
    q = {n: sem(f"moe_{n}") for n in names.split()}
    with memory(e) as (sb, ps), nc.Block() as block:
        wgu, wd = sb("wgu", [P, NW, KD, 2 * DE]), sb("wd", [P, NW, 2, D])
        ent = sb("moe_ent", [P, 2, 4], I32)
        hx, hT = sb("moe_hx", [P, 2, D]), sb("moe_hT", [P, KD, P])
        act_g, act_u, aT = sb("moe_g", [P, DE]), sb("moe_a", [P, DE]), sb("moe_aT", [P, 2, P])
        y = sb("moe_y", [P, 2, D])
        hp = ps("moe_hp", [P, KD, P])
        gu, ap_ = ps("moe_gu", [P, 2 * DE]), ps("moe_ap", [P, 2, P])
        yp = [ps(f"moe_yp{b}", [P, 2, 512]) for b in range(2)]
        weight = lambda b: ent[:, b, 2:3].bitcast(F32)

        def rows_of(ex, r):
            return ds(ex * e.CAP + r * P, P)

        def load_weights(sp, wb, ex):
            sp.dma_start(wgu[:, wb], a["we_gu"][ds(ex, 1)].squeeze(0)).then_inc(w_loaded[wb], 16)
            sp.dma_start(wd[:, wb], a["we_down"][ds(ex, 1)].squeeze(0)).then_inc(w_loaded[wb], 16)

        def go(pool):
            pool.sem_inc(q["go"], 1)

        def gather(pool, n, ex, r, b):
            pool.dma_start(ent[:, b], e.table_d[rows_of(ex, r), :]).then_inc(q["ent_loaded"], 16)
            pool.wait_ge(q["ent_loaded"], 16 * (n + 1))
            go(pool)
            pool.indirect_dma_start(out=hx[:, b], out_offset=None, in_=e.h_d,
                                    in_offset=bass.IndirectOffsetOnAxis(ap=ent[:, b, 0:1], axis=0),
                                    bounds_check=NT - 1, oob_is_err=False).then_inc(q["gathered"], 16)

        def scatter(pool, n, b):
            pool.wait_ge(q["y_dve"], n + 1)
            pool.wait_ge(q["y_act"], n + 1)
            go(pool)
            pool.indirect_dma_start(out=e.y2_d, out_offset=bass.IndirectOffsetOnAxis(ap=ent[:, b, 1:2], axis=0),
                                    in_=y[:, b], in_offset=None, bounds_check=2 * NT - 1,
                                    oob_is_err=False).then_inc(q["scattered"], 16)

        def pe_turn(pe, n, b):
            pe.wait_ge(q["gathered"], 16 * (n + 1))
            pe.wait_ge(q["hT_ready"], n)
            for k in range(KD):
                mm = pe.transpose(hp[:, k], hx[:, b, k * P:(k + 1) * P], e.c("ident"))
            mm.then_inc(q["turned"], 1)

        def pe_gate_up(pe, n, wb):
            pe.wait_ge(q["hT_ready"], n + 1)
            for k in range(KD):
                mm = pe.matmul(gu[:], hT[:, k], wgu[:, wb, k], start=(k == 0), stop=(k == KD - 1))
            mm.then_inc(q["made_gu"], 1)

        def pe_down(pe, n, b, wb):
            pe.wait_ge(q["acted"], n + 1)
            for k in range(2):
                mm = pe.transpose(ap_[:, k], act_u[:, k * P:(k + 1) * P], e.c("ident"))
            mm.then_inc(q["a_turned"], 1)
            pe.wait_ge(q["aT_ready"], n + 1)
            for c in range(2):
                for k in range(2):
                    mm = pe.matmul(yp[b][:, c], aT[:, k], wd[:, wb, k, c * 512:(c + 1) * 512], start=(k == 0), stop=(k == 1))
            mm.then_inc(q["made_y"], 1)

        def act_silu(act, n):
            act.wait_ge(q["made_gu"], n + 1)
            act.activation(act_g[:], gu[:, 0:DE], ACT.Silu).then_inc(q["silu"], 1)

        def act_y(act, n, b):
            act.wait_ge(q["made_y"], n + 1)
            act.activation(y[:, b, 0:512], yp[b][:, 0], ACT.Copy, scale=weight(b)).then_inc(q["y_act"], 1)

        def dve_hT(dve, n):
            dve.wait_ge(q["turned"], n + 1)
            dve.wait_ge(q["made_gu"], n)
            dve.tensor_tensor(hT[:], hp[:], e.v("norm_ffn").unsqueeze(2).to_broadcast([P, KD, P]),
                              ALU.mult).then_inc(q["hT_ready"], 1)

        def dve_act(dve, n):
            dve.wait_ge(q["silu"], n + 1)
            dve.tensor_tensor(act_u[:], act_g[:], gu[:, DE:], ALU.mult).then_inc(q["acted"], 1)
            dve.wait_ge(q["a_turned"], n + 1)
            dve.tensor_copy(aT[:], ap_[:]).then_inc(q["aT_ready"], 1)

        def dve_y(dve, n, b):
            dve.wait_ge(q["made_y"], n + 1)
            dve.tensor_scalar(y[:, b, 512:D], yp[b][:, 1], weight(b), None, ALU.mult).then_inc(q["y_dve"], 1)

        UN = 2 * NW
        NI = NE // UN

        def first_round(eng, body):
            with eng.Fori(0, NI) as it:
                for u in range(UN):
                    body(it * UN + u, it * 2 + u // NW, u % 2, u % NW)
            for n in range(NI * UN, NE):
                body(n, n // NW, n % 2, n % NW)

        def more_rounds(eng, body):
            longest = eng.value_load(e.count[0:1, NE:NE + 1], min_val=0, max_val=NT)
            with eng.Fori(1, NTT) as r:
                with eng.If(longest > r * P):
                    with eng.Fori(0, NE) as ex:
                        body(r * NE + ex, ex, r)

        @block.sync
        def _(sp):
            for b in range(NW):
                load_weights(sp, b, b)

            with sp.Fori(0, NE // NW - 1) as it:
                for u in range(NW):
                    sp.wait_ge(q["made_y"], it * NW + u + 1)
                    load_weights(sp, u, it * NW + u + NW)
            for ex in range(NE // NW * NW, NE):
                sp.wait_ge(q["made_y"], ex - NW + 1)
                load_weights(sp, ex % NW, ex)

            def more(n, ex, r):
                sp.wait_ge(q["made_y"], n)
                load_weights(sp, 0, ex)
            more_rounds(sp, more)

        @block.gpsimd
        def _(pool):
            pool.memset(hx[:], 0.0).then_inc(q["zero"], 1)
            pool.wait_ge(q["zero"], 1)
            gather(pool, 0, 0, 0, 0)
            gather(pool, 1, 1, 0, 1)

            def first(n, i, b, wb):
                scatter(pool, n, b)
                if not (isinstance(n, int) and n + 2 >= NE):
                    pool.wait_ge(q["scattered"], 16 * (n + 1))
                    go(pool)
                    gather(pool, n + 2, n + 2, 0, b)
            first_round(pool, first)
            pool.wait_ge(q["scattered"], 16 * NE)

            def more(n, ex, r):
                pool.wait_ge(q["scattered"], 16 * n)
                go(pool)
                gather(pool, n, ex, r, 0)
                scatter(pool, n, 0)
                pool.wait_ge(q["scattered"], 16 * (n + 1))
                go(pool)
            more_rounds(pool, more)

        w_more = lambda n: 32 * (n - NE + (NE + NW - 1) // NW + 1)

        @block.tensor
        def _(pe):
            pe_turn(pe, 0, 0)

            def first(n, i, b, wb):
                pe.wait_ge(w_loaded[wb], 32 * (i + 1))
                pe_gate_up(pe, n, wb)
                if not (isinstance(n, int) and n + 1 >= NE):
                    pe_turn(pe, n + 1, 1 - b)
                pe_down(pe, n, b, wb)
            first_round(pe, first)

            def more(n, ex, r):
                pe.wait_ge(w_loaded[0], w_more(n))
                pe_turn(pe, n, 0)
                pe_gate_up(pe, n, 0)
                pe_down(pe, n, 0, 0)
            more_rounds(pe, more)

        @block.scalar
        def _(act):
            def first(n, i, b, wb):
                act_silu(act, n)
                act_y(act, n, b)
            first_round(act, first)

            def more(n, ex, r):
                act_silu(act, n)
                act_y(act, n, 0)
            more_rounds(act, more)

        @block.vector
        def _(dve):
            dve_hT(dve, 0)

            def first(n, i, b, wb):
                dve_act_then_turn(dve, n)
                dve_y(dve, n, b)

            def dve_act_then_turn(dve, n):
                last = isinstance(n, int) and n + 1 >= NE
                if not last:
                    dve_hT(dve, n + 1)
                dve_act(dve, n)
            first_round(dve, first)

            def more(n, ex, r):
                dve_hT(dve, n)
                dve_act(dve, n)
                dve_y(dve, n, 0)
            more_rounds(dve, more)


def stage_final(e):
    nc, a, sem = e.nc, e.a, e.sem
    loaded = [sem(f"y2_loaded{b}") for b in range(2)]
    stored = [sem(f"y_stored{b}") for b in range(2)]
    gain_loaded, sum1, sum2, sq, std, rstd, out_ready = (
        sem("gain_loaded"), sem("f_sum1"), sem("f_sum2"), sem("f_sq"), sem("f_std"), sem("f_rstd"), sem("f_out"))
    with memory(e) as (sb, ps), nc.Block() as block:
        y2 = sb("y2_tile", [P, 2, 2 * D])
        gain, junk = sb("gain", [P, D]), sb("f_junk", [P, D])
        out = sb("y_out", [P, 2, D])
        stat = sb("f_stat", [P, 3, NTT])

        @block.sync
        def _(sp):
            sp.dma_start(gain[:], a["norm_final"].to_broadcast([P, D])).then_inc(gain_loaded, 16)
            for t in range(NTT):
                n = min(P, NT - t * P)
                if t >= 2:
                    sp.wait_ge(sum2, t - 1)
                sp.dma_start(y2[0:n, t % 2, :], e.y2_d.rearrange("(t j) d -> t (j d)", j=2)[t * P:t * P + n, :]).then_inc(loaded[t % 2], 16)
                if t >= 1:
                    sp.wait_ge(out_ready, t)
                    sp.dma_start(a["y"][(t - 1) * P:t * P, :], out[:, (t - 1) % 2]).then_inc(stored[(t - 1) % 2], 16)
            sp.wait_ge(out_ready, NTT)
            sp.dma_start(a["y"][TT * P:TT * P + NS, :], out[0:NS, TT % 2]).then_inc(stored[TT % 2], 16)
            for b in range(2):
                sp.wait_ge(stored[b], 16 * ((NTT + 1 - b) // 2))

        @block.scalar
        def _(act):
            for t in range(NTT):
                n = min(P, NT - t * P)
                act.wait_ge(sum2, t + 1)
                act.activation(junk[0:n], e.x1[0:n, t], ACT.Square, accum_out=stat[0:n, 0, t:t + 1]).then_inc(sq, 1)
                act.wait_ge(sq, t + 1)
                act.activation(stat[0:n, 1, t:t + 1], stat[0:n, 0, t:t + 1], ACT.Sqrt, scale=1.0 / D,
                               bias=e.eps[0:n, 0:1]).then_inc(std, 1)

        @block.vector
        def _(dve):
            dve.wait_ge(gain_loaded, 16)

            def add(t):
                n = min(P, NT - t * P)
                dve.wait_ge(loaded[t % 2], 16 * (t // 2 + 1))
                dve.tensor_tensor(e.x1[0:n, t], e.x1[0:n, t], y2[0:n, t % 2, 0:D], ALU.add).then_inc(sum1, 1)
                dve.wait_ge(sum1, t + 1)
                dve.tensor_tensor(e.x1[0:n, t], e.x1[0:n, t], y2[0:n, t % 2, D:], ALU.add).then_inc(sum2, 1)

            add(0)
            for t in range(NTT):
                n = min(P, NT - t * P)
                if t + 1 < NTT:
                    add(t + 1)
                dve.wait_ge(std, t + 1)
                dve.reciprocal(stat[0:n, 2, t:t + 1], stat[0:n, 1, t:t + 1]).then_inc(rstd, 1)
                dve.wait_ge(rstd, t + 1)
                if t >= 2:
                    dve.wait_ge(stored[t % 2], 16 * (t // 2))
                dve.scalar_tensor_tensor(out[0:n, t % 2], e.x1[0:n, t], stat[0:n, 2, t:t + 1], gain[0:n], ALU.mult,
                                         ALU.mult).then_inc(out_ready, 1)


STAGES = [stage_norm, stage_fox_project, stage_fox_prepare, stage_fox_prompt, stage_fox_sample,
          stage_rwkv_project, stage_rwkv_prepare, stage_rwkv_scan, stage_rwkv_sample,
          stage_mix, stage_out_and_route, stage_moe, stage_final]


def layout(inputs):
    f = {n: np.asarray(v) for n, v in inputs.items()}
    a = {}
    a["x"] = np.concatenate([f["x_prompt"].reshape(SEQ, D), f["x_sample"].reshape(NS, D),
                             np.zeros((P - NS, D), np.float32)])
    w = f["w_in"][0]
    order = np.concatenate([w[:, 0:3 * W], w[:, FOX:]], 1)
    a["w_in"] = np.ascontiguousarray(order.reshape(KD, P, -1, P).transpose(2, 1, 0, 3))
    a["w_f"] = np.ascontiguousarray(w[:, 3 * W:FOX].reshape(KD, P, H).transpose(1, 0, 2))
    vec = np.zeros((P, NVEC), np.float32)
    for name, n in VEC_FIELDS:
        src = f[{"mu": "mu_rw"}.get(name, name)].reshape(-1)
        at = VEC_AT[name][0]
        if name == "b_f":
            vec[:H, at] = src
        else:
            vec[:, at:at + n] = src.reshape(n, P).T
    a["vec"] = vec
    a["consts"] = np.ascontiguousarray(np.concatenate([CONSTS[n] for n in CONST_AT], 1))
    for name in ("cache_k", "cache_v", "cache_logf", "w2", "a2", "g2", "w_o"):
        a[name] = f[name][0]
    pab = np.stack([f["p_a"][0], f["p_b"][0]]).reshape(2, HP, P, KD, P)
    a["p_ab"] = np.ascontiguousarray(pab.transpose(3, 2, 0, 1, 4).reshape(KD, P, 2 * HP, P))
    a["page_table"] = f["page_table"].reshape(1, NB * NPG)
    a["state"] = f["state_wkv"][0]
    a["shiftT"] = np.ascontiguousarray(f["state_shift"][0].reshape(NB, RW // P, P).transpose(2, 1, 0))
    a["norm_final"] = f["norm_final"].reshape(1, D)
    a["w_route"] = np.ascontiguousarray(np.concatenate([f["w_grp"][0], f["w_exp"][0]], 1)
                                        .reshape(KD, P, GR + NE).transpose(1, 0, 2))
    gu = np.concatenate([f["we_gate"][0], f["we_up"][0]], 2)
    a["we_gu"] = np.ascontiguousarray(gu.reshape(NE, KD, P, 2 * DE).transpose(0, 2, 1, 3))
    a["we_down"] = np.ascontiguousarray(f["we_down"][0].reshape(NE, 2, P, D).transpose(0, 2, 1, 3))
    return a


OUTS = {
    "y": [NTT * P, D], "k_out": [NT, W], "v_out": [NT, W], "logf_out": [NT, H],
    "wkv_prompt": [P, HP, DH], "wkv_sample": [NB, H, DH, DH],
    "shift_out": [P, RW // P, NB + 1],
}


def program(nc, arrays, upto=99):
    a = {}
    for n, v in arrays.items():
        a[n] = nc.dram_tensor(f"in_{n}", v.shape, mybir.dt.from_np(v.dtype), kind="ExternalInput").ap()
    for n, shape in OUTS.items():
        a[n] = nc.dram_tensor(f"out_{n}", shape, F32, kind="ExternalOutput").ap()
    build(nc, a, upto)


def kernel(**inputs):
    import concourse.bacc as bacc
    from concourse.bass_utils import run_bass_kernel_spmd

    arrays = layout(inputs)
    nc = bacc.Bacc("TRN2", target_bir_lowering=False, num_devices=1)
    program(nc, arrays)
    r = run_bass_kernel_spmd(nc, [{f"in_{n}": v for n, v in arrays.items()}], core_ids=[0]).results[0]
    o = {n: r[f"out_{n}"] for n in OUTS}
    split = lambda x, *tail: (x[:SEQ].reshape(1, 1, SEQ, *tail), x[SEQ:NT].reshape(1, NB, TS, *tail))
    kp, ks = split(o["k_out"], H, DH)
    vp, vs = split(o["v_out"], H, DH)
    fp, fs = split(o["logf_out"], H)
    y = o["y"]
    state = o["wkv_prompt"].reshape(2, DH, HP, DH).transpose(2, 0, 3, 1).reshape(1, 1, H, DH, DH)
    shift = o["shift_out"].transpose(2, 1, 0).reshape(NB + 1, RW)
    return (y[:SEQ].reshape(1, SEQ, D), y[SEQ:NT].reshape(NB, TS, D), kp, vp, fp,
            state, shift[0].reshape(1, 1, RW), ks, vs, fs,
            o["wkv_sample"].reshape(1, NB, H, DH, DH), shift[1:].reshape(1, NB, RW))
```

```python
from contextlib import ExitStack, contextmanager

import numpy as np

import concourse.bass as bass
from concourse import mybir

P = 128
D = 1024
KD = D // P
SEQ, NB, TS = 1024, 8, 4
NS = NB * TS
NT = SEQ + NS
TT = SEQ // P
NTT = TT + 1
H, DH, W = 8, 64, 512
HP = H // 2
PAST, PAGE = 2048, 128
NPG = PAST // PAGE
NE, GR, EPG, DE = 32, 4, 8, 256
R = 96
RW = 3 * W + 64 + 64 + 128
FOX = 3 * W + H
C = 64
NCH = SEQ // C
NORM_EPS, GN_EPS = 1e-6, 64e-5
NEG = -1.0e30
EXP_HALF = float(np.exp(-0.5))

F32, BF16, I32 = mybir.dt.float32, mybir.dt.bfloat16, mybir.dt.int32
ALU, ACT = mybir.AluOpType, mybir.ActivationFunctionType
X = mybir.AxisListType.X
ds = bass.ds

VEC_FIELDS = [("norm_mix", 8), ("norm_ffn", 8), ("mu", 14), ("w0", 4), ("a0", 4), ("k_k", 4), ("k_a", 4),
              ("r_k", 4), ("lnx_w", 4), ("lnx_b", 4), ("b_f", 1)]
VEC_AT, _n = {}, 0
for _name, _k in VEC_FIELDS:
    VEC_AT[_name] = (_n, _n + _k)
    _n += _k
NVEC = _n

LEVELS = [1, 2, 4, 8, 16, 32]


def shape_constants():
    out = {}
    out["ident"] = np.eye(P, dtype=np.float32)
    head = np.arange(P) // DH
    out["head_ones"] = (head[:, None] == head[None, :]).astype(np.float32)
    i, j = np.arange(P)[:, None], np.arange(P)[None, :]
    out["causal"] = np.where(j <= i, 0.0, NEG).astype(np.float32)
    t, s = (np.arange(P) % C)[:, None], np.arange(C)[None, :]
    out["lower_eye"] = (t == s).astype(np.float32)
    out["upper"] = (t < s).astype(np.float32)
    out["upper_diag"] = (t <= s).astype(np.float32)
    out["level0"] = -((t // 2 == s // 2) & (t % 2 == 1) & (s % 2 == 0)).astype(np.float32)
    lv = [((s // (2 * z) == t // (2 * z)) & ((s // z) % 2 == 1) & ((t // z) % 2 == 0)).astype(np.float32)
          for z in LEVELS]
    lv[0] = -lv[0]
    out["levels_t"] = np.concatenate(lv, 1)
    row, key = np.arange(P), np.arange(NS)
    own = [((row // NS)[:, None] + 4 * g == (key // TS)[None, :]) & ((row % TS)[:, None] >= (key % TS)[None, :])
           for g in range(2)]
    out["own_past"] = np.concatenate([np.where(o, 0.0, NEG) for o in own], 1).astype(np.float32)
    bh = np.arange(NB * H)
    sel = np.zeros((P, NB, H, TS), np.float32)
    for b in range(NB):
        sel[bh, b, :, :] = ((bh // H == b)[:, None] & (bh % H)[:, None] == np.arange(H)[None, :])[:, :, None] * 0.0
        for h in range(H):
            sel[b * H + h, b, h, :] = -8.0
            sel[64 + b * H + h, b, h, :] = 8.0
    out["row_sel"] = sel.reshape(P, NB * NS)
    out["before"] = (i < j).astype(np.float32)
    out["expert_id"] = np.broadcast_to(np.arange(NE, dtype=np.float32)[None, :], (P, NE))
    out["is_sample"] = (np.arange(P) < NS).astype(np.float32)[:, None]
    out["beyond"] = np.where(np.arange(P) < NS, 0.0, 1e7).astype(np.float32)[:, None]
    out["token"] = (np.arange(NTT)[None, :] * P + np.arange(P)[:, None]).astype(np.float32)
    return out


CONSTS = shape_constants()
CONST_AT, _n = {}, 0
for _name, _a in CONSTS.items():
    CONST_AT[_name] = (_n, _n + _a.shape[1])
    _n += _a.shape[1]
NCONST = _n


class Shared:
    pass


class Steps:

    def __init__(self, sem):
        self.sem, self.n = sem, 0

    def done(self, ins):
        ins.then_inc(self.sem, 1)
        self.n = self.n + 1

    def settle(self, eng):
        eng.wait_ge(self.sem, self.n)

    def then(self, eng, ins):
        self.done(ins)
        self.settle(eng)


def build(nc, a, upto=99):
    with ExitStack() as ctx:
        e = Shared()
        e.nc, e.a, e.ctx = nc, a, ctx
        e.sems = {}

        def sem(name):
            if name not in e.sems:
                e.sems[name] = nc.alloc_semaphore(name=name)
            return e.sems[name]

        e.sem = sem
        e.sb = lambda name, shape, dt=F32: ctx.enter_context(nc.sbuf_tensor(name, shape, dt))
        e.steps = {n: Steps(ctx.enter_context(nc.semaphore(f"{n}_steps"))) for n in ("dve", "act", "pool", "pe")}
        e.vec = e.sb("vec", [P, NVEC])
        e.const = e.sb("const", [P, NCONST])
        e.identb = e.sb("identb", [P, P], BF16)
        e.causalb = e.sb("causalb", [P, 512], BF16)
        e.own_pastb = e.sb("own_pastb", [P, 2 * NS], BF16)
        e.ones = e.sb("ones", [P, SEQ])
        e.eps = e.sb("eps", [P, 2])
        e.v = lambda name: e.vec[:, VEC_AT[name][0]:VEC_AT[name][1]]
        e.c = lambda name: e.const[:, CONST_AT[name][0]:CONST_AT[name][1]]
        e.c_rows = nc.dram_tensor("c_rows", (H, 2, 2, SEQ), F32, kind="Internal").ap()
        dram = lambda name, shape, dt=F32: nc.dram_tensor(name, shape, dt, kind="Internal").ap()
        e.CAP = NT
        e.sv_d, e.so_d = dram("sample_vectors", (6, NB, H, TS, DH)), dram("sample_out", (NS, W))
        e.table_d = dram("expert_table", (NE * e.CAP, 4), I32)
        e.h_d, e.y2_d = dram("h_rows", (NTT * P, D)), dram("y2", (2 * NT, D))
        rows = e.sb("rows", [P, (KD + HP) * NT])
        e.xnT = rows[:, 0:KD * NT].rearrange("p (k n) -> p k n", k=KD)
        e.oaT = rows[:, KD * NT:].rearrange("p (k n) -> p k n", k=HP)
        e.x1 = rows[:, 0:NTT * D].rearrange("p (t d) -> p t d", t=NTT)
        e.beside_x1 = rows[:, NTT * D:]
        for n, stage in enumerate(STAGES):
            if n <= upto:
                stage(e)
            if len(e.sems) > 100:
                nc.clear_and_free_semaphores(list(e.sems.values()))
                nc.all_engine_barrier()
                e.sems.clear()


@contextmanager
def memory(e):
    with ExitStack() as ctx:
        sb = lambda name, shape, dt=F32: ctx.enter_context(e.nc.sbuf_tensor(name, shape, dt))
        ps = lambda name, shape, dt=F32: ctx.enter_context(e.nc.psum_tensor(name, shape, dt))
        yield sb, ps


def pairs(eng, count, body):
    with eng.Fori(0, count // 2) as i:
        for b in range(2):
            body(2 * i + b, i, b)
    if count % 2:
        body(count - 1, count // 2, 0)


def stage_norm(e):
    nc, a, sem = e.nc, e.a, e.sem
    loaded, const_loaded = [sem(f"x_loaded{b}") for b in range(2)], sem("const_loaded")
    xt_free, sq, std, rstd, xn_ready = sem("xt_free"), sem("x_sq"), sem("x_std"), sem("x_rstd"), sem("xn_ready")
    turned, xnT_ready, const_ready = sem("x_turned"), sem("xnT_ready"), sem("const_ready")
    with memory(e) as (sb, ps), nc.Block() as block:
        xt, xn, junk = sb("xt", [P, 2, D]), sb("xn", [P, 2, D]), sb("sq_junk", [P, D])
        stat = sb("x_stat", [P, 2, 4])
        pt = [ps(f"x_pt{b}", [P, KD, P]) for b in range(2)]

        @block.sync
        def _(sp):
            sp.dma_start(e.vec[:], a["vec"]).then_inc(const_loaded, 16)
            sp.dma_start(e.const[:], a["consts"]).then_inc(const_loaded, 16)

            def load(t, i, b):
                sp.wait_ge(xt_free, t + 1)
                sp.dma_start(xt[:, b, :], a["x"][ds(t * P, P), :]).then_inc(loaded[b], 16)
            pairs(sp, NTT, load)

        @block.scalar
        def _(act):
            act.wait_ge(const_ready, 5)

            def body(t, i, b):
                act.wait_ge(loaded[b], 16 * (i + 1))
                act.activation(junk[:], xt[:, b, :], ACT.Square, accum_out=stat[:, b, 0:1]).then_inc(sq, 1)
                act.wait_ge(sq, t + 1)
                act.activation(stat[:, b, 1:2], stat[:, b, 0:1], ACT.Sqrt, scale=1.0 / D,
                               bias=e.eps[:, 0:1]).then_inc(std, 1)
            pairs(act, NTT, body)

        @block.vector
        def _(dve):
            dve.memset(e.ones[:], 1.0).then_inc(const_ready, 1)
            dve.memset(e.eps[:, 0:1], NORM_EPS)
            dve.memset(e.eps[:, 1:2], GN_EPS).then_inc(const_ready, 1)
            dve.sem_inc(xt_free, 2)
            dve.wait_ge(const_loaded, 32)
            dve.tensor_copy(e.identb[:], e.c("ident")).then_inc(const_ready, 1)
            dve.memset(e.causalb[:, 0:384], 0.0)
            dve.tensor_copy(e.causalb[:, 384:512], e.c("causal")).then_inc(const_ready, 1)
            dve.tensor_copy(e.own_pastb[:], e.c("own_past")).then_inc(const_ready, 1)

            def body(t, i, b):
                dve.wait_ge(std, t + 1)
                dve.reciprocal(stat[:, b, 2:3], stat[:, b, 1:2]).then_inc(rstd, 1)
                dve.wait_ge(rstd, t + 1)
                dve.tensor_scalar(xn[:, b, :], xt[:, b, :], stat[:, b, 2:3], None, ALU.mult).then_inc(xn_ready, 1)
                dve.wait_ge(xn_ready, t + 1)
                dve.sem_inc(xt_free, 1)
                dve.wait_ge(turned, t + 1)
                n = P if not isinstance(t, int) else NS
                dve.tensor_tensor(e.xnT[:, :, ds(t * P, n)], pt[b][:, :, 0:n],
                                  e.v("norm_mix").unsqueeze(2).to_broadcast([P, KD, n]),
                                  ALU.mult).then_inc(xnT_ready, 1)
            pairs(dve, NTT, body)

        @block.tensor
        def _(pe):
            def body(t, i, b):
                pe.wait_ge(xn_ready, t + 1)
                for k in range(KD):
                    mm = pe.transpose(pt[b][:, k, :], xn[:, b, k * P:(k + 1) * P], e.c("ident"))
                mm.then_inc(turned, 1)
            pairs(pe, NTT, body)


COLS = [(0, 512), (512, 512), (SEQ, NS)]


def project_tiles(e, name, sb, ps, block, j0, n, dest, extra_pe=None):
    a, sem = e.a, e.sem
    w_loaded = [sem(f"{name}_w_loaded{b}") for b in range(2)]
    made, act_out, dve_out = sem(f"{name}_made"), sem(f"{name}_act_out"), sem(f"{name}_dve_out")
    w = sb(f"{name}_w", [P, 2, KD, P])
    pp = [ps(f"{name}_pp{b}", [P, 3, 512]) for b in range(2)]

    @block.sync
    def _(sp):
        for b in range(2):
            sp.dma_start(w[:, b], a["w_in"][j0 + b]).then_inc(w_loaded[b], 16)
        with sp.Fori(0, n // 2 - 1) as i:
            for b in range(2):
                sp.wait_ge(made, 2 * i + b + 1)
                sp.dma_start(w[:, b], a["w_in"][ds(j0 + 2 + 2 * i + b, 1)].squeeze(0)).then_inc(w_loaded[b], 16)

    @block.tensor
    def _(pe):
        def body(j, i, b, first=False):
            pe.wait_ge(w_loaded[b], 16 * (i + 1))
            if not first:
                pe.wait_ge(act_out, j - 1)
                pe.wait_ge(dve_out, j - 1)
            for k in range(KD):
                for c, (at, m) in enumerate(COLS):
                    mm = pe.matmul(pp[b][:, c, 0:m], w[:, b, k, :], e.xnT[:, k, at:at + m],
                                   start=(k == 0), stop=(k == KD - 1))
            mm.then_inc(made, 1)
        body(0, 0, 0, True)
        body(1, 0, 1, True)
        with pe.Fori(1, n // 2) as i:
            for b in range(2):
                body(2 * i + b, i, b)
        if extra_pe:
            extra_pe(pe)

    def out(eng, copy, done, cols):
        def body(j, i, b):
            eng.wait_ge(made, j + 1)
            for c in cols:
                at, m = COLS[c]
                ins = copy(dest[:, ds(j, 1), at:at + m].squeeze(1), pp[b][:, c, 0:m])
            ins.then_inc(done, 1)
        pairs(eng, n, body)

    @block.scalar
    def _(act):
        out(act, act.copy, act_out, [0])

    @block.vector
    def _(dve):
        out(dve, dve.tensor_copy, dve_out, [1, 2])


def stage_fox_project(e):
    e.fox_mem = e.ctx.enter_context(ExitStack())
    e.qkv = e.fox_mem.enter_context(e.nc.sbuf_tensor("qkv", [P, 12, NT], F32))
    with memory(e) as (sb, ps), e.nc.Block() as block:
        project_tiles(e, "fox", sb, ps, block, 0, 12, e.qkv)


def stage_fox_prepare(e):
    nc, a, sem = e.nc, e.a, e.sem
    e.v_tok = e.fox_mem.enter_context(nc.sbuf_tensor("v_tok", [P, NTT, W], F32))
    e.logfT = e.fox_mem.enter_context(nc.sbuf_tensor("logfT", [H, NT], F32))
    wf_loaded, f_made, z_ready, m_ready = sem("wf_loaded"), sem("f_made"), sem("f_z"), sem("f_m")
    exp_ready, ln_ready, logf_ready, c_ready = sem("f_exp"), sem("f_ln"), sem("logf_ready"), sem("c_ready")
    turned, kept, logf_turned, logf_kept = sem("kv_turned"), sem("kv_kept"), sem("logf_turned"), sem("logf_kept")
    stored = sem("fox_stored")
    with memory(e) as (sb, ps), nc.Block() as block:
        wf, k_tok = sb("wf", [P, KD, H]), sb("k_tok", [P, NTT, W])
        z, m, ex = sb("f_z_t", [H, NT]), sb("f_m_t", [H, NT]), sb("f_ex", [H, NT])
        crow = sb("crow", [H, 2, SEQ])
        logf_tok = sb("logf_tok", [P, NTT, H])
        fp = ps("fp", [P, 3, 512])
        kv = [ps(f"kv_t{b}", [P, 512]) for b in range(3)]
        lp = ps("logf_t", [P, NTT, H])
        tiles = [(t, src, min(P, NT - t * P)) for t in range(NTT) for src in (4, 8)]

        @block.sync
        def _(sp):
            sp.dma_start(wf[:], a["w_f"]).then_inc(wf_loaded, 16)
            n = 0
            for x, (t, src, m_) in enumerate(tiles):
                sp.wait_ge(kept, x + 1)
                tok, dst = (k_tok, a["k_out"]) if src == 4 else (e.v_tok, a["v_out"])
                sp.dma_start(dst[t * P:t * P + m_, :], tok[0:m_, t, :]).then_inc(stored, 16)
                n += 1
            sp.wait_ge(c_ready, 2)
            sp.dma_start(e.c_rows[:, 0, 0, :], crow[:, 0, :]).then_inc(stored, 16)
            sp.dma_start(e.c_rows[:, 0, 1, :], e.ones[0:H, 0:SEQ]).then_inc(stored, 16)
            sp.dma_start(e.c_rows[:, 1, 0, :], e.ones[0:H, 0:SEQ]).then_inc(stored, 16)
            sp.dma_start(e.c_rows[:, 1, 1, :], crow[:, 1, :]).then_inc(stored, 16)
            sp.wait_ge(logf_kept, 1)
            sp.dma_start(a["logf_out"][0:SEQ, :].rearrange("(t p) h -> p t h", p=P), logf_tok[:, 0:TT, :]).then_inc(stored, 16)
            sp.dma_start(a["logf_out"][SEQ:NT, :], logf_tok[0:NS, TT, :]).then_inc(stored, 16)
            sp.wait_ge(stored, 16 * (n + 6))

        @block.tensor
        def _(pe):
            pe.wait_ge(wf_loaded, 16)
            for k in range(KD):
                for c, (at, n) in enumerate(COLS):
                    mm = pe.matmul(fp[0:H, c, 0:n], wf[:, k, :], e.xnT[:, k, at:at + n],
                                   start=(k == 0), stop=(k == KD - 1))
            mm.then_inc(f_made, 1)
            for x, (t, src, n) in enumerate(tiles):
                if x >= 3:
                    pe.wait_ge(kept, x - 2)
                for j in range(HP):
                    mm = pe.transpose(kv[x % 3][0:n, j * P:(j + 1) * P], e.qkv[:, src + j, t * P:t * P + n], e.c("ident"))
                mm.then_inc(turned, 1)
            pe.wait_ge(logf_ready, 1)
            for t in range(NTT):
                n = min(P, NT - t * P)
                mm = pe.transpose(lp[0:n, t, :], e.logfT[:, t * P:t * P + n], e.c("ident")[0:H, 0:H])
            mm.then_inc(logf_turned, 1)

        @block.scalar
        def _(act):
            act.wait_ge(m_ready, 1)
            act.activation(ex[:], m[:], ACT.Exp).then_inc(exp_ready, 1)
            act.wait_ge(exp_ready, 1)
            act.activation(ex[:], ex[:], ACT.Ln, bias=e.ones[0:H, 0:1]).then_inc(ln_ready, 1)

        @block.vector
        def _(dve):
            dve.wait_ge(f_made, 1)
            for c, (at, n) in enumerate(COLS):
                ins = dve.tensor_scalar(z[:, at:at + n], fp[0:H, c, 0:n], e.v("b_f")[0:H, :], None, ALU.add)
            ins.then_inc(z_ready, 1)
            dve.wait_ge(z_ready, 1)
            dve.scalar_tensor_tensor(m[:], z[:], -1.0, z[:], ALU.mult, ALU.min).then_inc(m_ready, 1)
            for x, (t, src, n) in enumerate(tiles):
                dve.wait_ge(turned, x + 1)
                tok = k_tok if src == 4 else e.v_tok
                dve.tensor_copy(tok[0:n, t, :], kv[x % 3][0:n, :]).then_inc(kept, 1)
            dve.wait_ge(ln_ready, 1)
            dve.scalar_tensor_tensor(e.logfT[:], z[:], 0.0, ex[:], ALU.min, ALU.subtract).then_inc(logf_ready, 1)
            dve.wait_ge(logf_ready, 1)
            dve.tensor_tensor_scan(m[:, 0:SEQ], e.ones[0:H, 0:SEQ], e.logfT[:, 0:SEQ], 0.0, ALU.mult, ALU.add).then_inc(z_ready, 1)
            dve.wait_ge(z_ready, 2)
            dve.tensor_scalar(crow[:, 0, :], m[:, 0:SEQ], 8.0, None, ALU.mult).then_inc(c_ready, 1)
            dve.tensor_scalar(crow[:, 1, :], m[:, 0:SEQ], -8.0, None, ALU.mult).then_inc(c_ready, 1)
            dve.wait_ge(logf_turned, 1)
            dve.tensor_copy(logf_tok[:, 0:TT, :], lp[:, 0:TT, :])
            dve.tensor_copy(logf_tok[0:NS, TT, :], lp[0:NS, TT, :]).then_inc(logf_kept, 1)


def stage_fox_prompt(e):
    nc, a, sem = e.nc, e.a, e.sem
    rows_loaded = [sem(f"c_rows_loaded{s}") for s in range(2)]
    q_staged, k_staged, zeroed = sem("fox_q_staged"), sem("fox_k_staged"), sem("qs_zeroed")
    e.table_loaded, e.lf_loaded, e.qs_ready = sem("table_loaded"), sem("lf_loaded"), sem("qs_ready")
    e.table, e.lf, e.qs = (e.fox_mem.enter_context(nc.sbuf_tensor(*x)) for x in (
        ("table", [1, NB * NPG], I32), ("lf", [P, NPG, NB, H], F32), ("qs", [P, NB, HP, P], F32)))
    scored, maxed, bias_ready, exped = sem("fox_scored"), sem("fox_maxed"), sem("fox_bias"), sem("fox_exped")
    turned, pt_dve, pt_act = sem("fox_turned"), sem("fox_pt_dve"), sem("fox_pt_act")
    mixed, recip, out_done, o_turned, o_kept = (sem("fox_mixed"), sem("fox_recip"), sem("fox_out"),
                                                sem("fox_o_turned"), sem("fox_o_kept"))
    with memory(e) as (sb, ps), nc.Block() as block:
        q_head, k_head = sb("q_head", [66, 2, SEQ]), sb("k_head", [66, 2, SEQ])
        prob, probT = sb("prob", [P, 2, SEQ]), sb("probT", [P, TT, P])
        o_tok = sb("o_tok", [P, TT, W])
        stat = sb("fox_stat", [P, 2, 4])
        score = [ps(f"score{b}", [P, 1024]) for b in range(2)]
        pt = ps("prob_t", [P, TT, P])
        op = [ps(f"fox_o{b}", [P, 512]) for b in range(2)]
        items = [(s, t) for s in range(2) for t in range(TT)]
        M = len(items)
        act_copies = lambda i, s, t: (TT - 4) * (2 * i + s) + max(t - 3, 0)

        def ahead(i, m):
            return (i, m + 2) if m + 2 < M else (i + 1, m + 2 - M)

        def all_pairs(eng, body):
            with eng.Fori(0, HP - 1) as i:
                for m in range(M):
                    body(i, m, True)
            for m in range(M):
                body(HP - 1, m, m + 2 < M)

        @block.sync
        def _(sp):
            def rows(i, s):
                sp.dma_start(q_head[64:66, s, :], e.c_rows[ds(2 * i + s, 1), 0].squeeze(0)).then_inc(rows_loaded[s], 16)
                sp.dma_start(k_head[64:66, s, :], e.c_rows[ds(2 * i + s, 1), 1].squeeze(0)).then_inc(rows_loaded[s], 16)
            rows(0, 0)
            rows(0, 1)
            with sp.Fori(0, HP - 1) as i:
                for s in range(2):
                    sp.wait_ge(scored, M * i + TT * (s + 1))
                    rows(i + 1, s)

        @block.gpsimd
        def _(pool):
            pool.dma_start(e.table[:], a["page_table"]).then_inc(e.table_loaded, 16)
            pool.memset(e.qs[:], 0.0).then_inc(zeroed, 1)
            pool.wait_ge(zeroed, 1)
            pool.wait_ge(e.table_loaded, 16)
            with pool.Fori(0, NPG) as j:
                for b in range(NB):
                    n = pool.value_load(e.table[0:1, ds(j + b * NPG, 1)], min_val=0, max_val=a["cache_k"].shape[0] - 1)
                    pool.dma_start(e.lf[:, ds(j, 1), b, :].squeeze(1), a["cache_logf"][ds(n, 1)].squeeze(0)).then_inc(e.lf_loaded, 16)
            for s in range(2):
                half = slice(64 * s, 64 * s + 64)
                for b in range(NB):
                    for p in range(HP):
                        col = b % (NB // 2) * NS + (2 * p + s) * TS
                        ins = pool.tensor_copy(e.qs[half, b, p, col:col + TS], e.qkv[half, p, SEQ + b * TS:SEQ + (b + 1) * TS])
                        ins.then_inc(e.qs_ready, 1)

        @block.tensor
        def _(pe):
            def scores(i, m):
                s, t = items[m]
                g = i * M + m
                if t == 0:
                    pe.wait_ge(q_staged, 2 * i + s + 1)
                    pe.wait_ge(k_staged, 2 * i + s + 1)
                    pe.wait_ge(rows_loaded[s], 32 * (i + 1))
                pe.wait_ge(exped, g + 1)
                for c in range(0, (t + 1) * P, 512):
                    n = min(512, (t + 1) * P - c)
                    last = c + n == (t + 1) * P
                    pe.matmul(score[m % 2][:, c:c + n], q_head[:, s, t * P:(t + 1) * P], k_head[:, s, c:c + n],
                              start=True, stop=not last)
                pe.matmul(score[m % 2][:, c:c + n], e.identb[:], e.causalb[:, 512 - n:512],
                          start=False, stop=True).then_inc(scored, 1)

            def body(i, m, more):
                s, t = items[m]
                g = i * M + m
                pe.wait_ge(exped, g + 3)
                for k in range(t + 1):
                    mm = pe.transpose(pt[:, k, :], prob[:, m % 2, k * P:(k + 1) * P], e.c("ident"))
                mm.then_inc(turned, 1)
                if more:
                    scores(*ahead(i, m))
                pe.wait_ge(pt_dve, g + 1)
                if t >= 4:
                    pe.wait_ge(pt_act, act_copies(i, s, t))
                pe.wait_ge(out_done, g + 1)
                for k in range(t + 1):
                    mm = pe.matmul(op[m % 2][:, 0:DH], probT[:, k, :], e.v_tok[:, k, ds((2 * i + s) * DH, DH)],
                                   start=(k == 0), stop=(k == t))
                mm.then_inc(mixed, 1)
            scores(0, 0)
            scores(0, 1)
            all_pairs(pe, body)
            pe.wait_ge(out_done, 2 + HP * M)
            for t in range(TT):
                if t >= 2:
                    pe.wait_ge(o_kept, t - 1)
                for j in range(HP):
                    mm = pe.transpose(op[t % 2][:, j * P:(j + 1) * P], o_tok[:, t, j * P:(j + 1) * P], e.c("ident"))
                mm.then_inc(o_turned, 1)

        @block.scalar
        def _(act):
            def stage_q(i, s):
                act.copy(q_head[0:64, s, :], e.qkv[64 * s:64 * s + 64, ds(i, 1), 0:SEQ].squeeze(1)).then_inc(q_staged, 1)

            def exp(i, m):
                t, g = items[m][1], i * M + m
                act.wait_ge(bias_ready, g + 1)
                act.activation(prob[:, m % 2, 0:(t + 1) * P], score[m % 2][:, 0:(t + 1) * P], ACT.Exp, scale=0.125,
                               bias=stat[:, m % 2, 1:2], accum_out=stat[:, m % 2, 2:3]).then_inc(exped, 1)

            def body(i, m, more):
                t, g = items[m][1], i * M + m
                act.wait_ge(turned, g + 1)
                if t >= 4:
                    act.wait_ge(mixed, g)
                    act.copy(probT[:, 4:t + 1, :], pt[:, 4:t + 1, :]).then_inc(pt_act, 1)
                if more:
                    exp(*ahead(i, m))
                    if m == TT + 1:
                        if not isinstance(i, int):
                            stage_q(i + 1, 0)
                    if m == 1:
                        stage_q(i, 1)
            act.sem_inc(exped, 2)
            stage_q(0, 0)
            exp(0, 0)
            exp(0, 1)
            all_pairs(act, body)

        @block.vector
        def _(dve):
            def stage_k(i, s):
                dve.tensor_copy(k_head[0:64, s, :], e.qkv[64 * s:64 * s + 64, ds(i + HP, 1), 0:SEQ].squeeze(1)).then_inc(k_staged, 1)

            def maximum(i, m):
                t, g = items[m][1], i * M + m
                dve.wait_ge(scored, g + 1)
                dve.reduce_max(stat[:, m % 2, 0:1], score[m % 2][:, 0:(t + 1) * P], X).then_inc(maxed, 1)
                dve.wait_ge(maxed, g + 1)
                dve.tensor_scalar(stat[:, m % 2, 1:2], stat[:, m % 2, 0:1], -0.125, None, ALU.mult).then_inc(bias_ready, 1)

            def body(i, m, more):
                s, t = items[m]
                g = i * M + m
                h = min(t + 1, 4)
                dve.wait_ge(turned, g + 1)
                dve.tensor_copy(probT[:, 0:h, :], pt[:, 0:h, :]).then_inc(pt_dve, 1)
                dve.wait_ge(exped, g + 3)
                dve.wait_ge(out_done, g + 1)
                dve.reciprocal(stat[:, m % 2, 3:4], stat[:, m % 2, 2:3]).then_inc(recip, 1)
                dve.wait_ge(recip, g + 1)
                if more:
                    maximum(*ahead(i, m))
                    if m == TT + 1 and not isinstance(i, int):
                        stage_k(i + 1, 0)
                    if m == 1:
                        stage_k(i, 1)
                dve.wait_ge(mixed, g + 1)
                dve.tensor_scalar(o_tok[:, t, ds((2 * i + s) * DH, DH)], op[m % 2][:, 0:DH], stat[:, m % 2, 3:4],
                                  None, ALU.mult).then_inc(out_done, 1)
            dve.sem_inc(out_done, 2)
            stage_k(0, 0)
            maximum(0, 0)
            maximum(0, 1)
            all_pairs(dve, body)
            for t in range(TT):
                dve.wait_ge(o_turned, t + 1)
                dve.tensor_copy(e.oaT[:, :, t * P:(t + 1) * P],
                                op[t % 2][:].rearrange("p (j n) -> p j n", j=HP)).then_inc(o_kept, 1)


RING = 8


def stage_fox_sample(e):
    nc, a, sem = e.nc, e.a, e.sem
    new_loaded = sem("new_loaded")
    lf_turned, summed, steps = sem("lf_turned"), sem("lf_summed"), e.steps["dve"]
    prepared, zeroed, ones_set = sem("dec_prepared"), sem("dec_zeroed"), sem("dec_ones_set")
    page_loaded = [sem(f"page_loaded{u}") for u in range(RING)]
    page_used, quad_scored = sem("page_used"), sem("quad_scored")
    kt_out = [sem(f"kt_out{b}") for b in range(2)]
    scored, maxed, biased, exped, recip, prob_ready = (sem("dec_scored"), sem("dec_maxed"), sem("dec_biased"),
                                                       sem("dec_exped"), sem("dec_recip"), sem("dec_prob"))
    p_turned, p_kept, mixed = sem("dec_p_turned"), sem("dec_p_kept"), sem("dec_mixed")
    o_out, o_turned, o_kept = sem("dec_o_out"), sem("dec_o_turned"), sem("dec_o_kept")
    NG, BG = 2, 4
    NP2 = NPG // RING
    used_before = lambda g, phase, b, n: RING + ((2 * g + phase) * BG + b) * NPG + n
    KEYS = PAST + NS
    with memory(e) as (sb, ps), nc.Block() as block:
        table, lf, qs = e.table, e.lf, e.qs
        ck = sb("ck", [P, PAST + TS])
        ck_new = sb("ck_new", [P, NB, TS])
        lf_new = sb("lf_new", [NB * H, TS])
        row = sb("row_gate", [P, NB, H, TS])
        page = sb("page", [P, RING, W])
        kt = e.qkv[:, 2 * HP:3 * HP, 0:SEQ].rearrange("p h (w n) -> p w h n", w=2)
        o_rows = sb("dec_o_rows", [NS, 2, W])
        prob = sb("dec_prob_t", [P, KEYS])
        probT = sb("dec_probT", [P, NPG + 1, P])
        zero = sb("zero", [P, 512], BF16)
        stat = sb("dec_stat", [P, 4])
        score = ps("dec_score", [P, 2560])
        ktp = [ps(f"ktp{b}", [P, HP, P]) for b in range(2)]
        ov = [ps("dec_o", [P, 512])[:], ktp[1][:].rearrange("p j n -> p (j n)")]
        o_cols = ktp[0][:].rearrange("p j n -> p (j n)")

        @block.sync
        def _(sp):
            for b in range(NB):
                sp.dma_start(lf_new[b * H:(b + 1) * H, :],
                             a["logf_out"][SEQ + b * TS:SEQ + (b + 1) * TS, :].rearrange("t h -> h t"), allow_slow_non_contiguous=True).then_inc(new_loaded, 16)
            for g in range(NG):
                for kv, cache in enumerate((a["cache_k"], a["cache_v"])):
                    with sp.Fori(0, BG * NP2) as r:
                        for u in range(RING):
                            n = sp.value_load(table[0:1, ds(r * RING + (g * BG * NPG + u), 1)],
                                              min_val=0, max_val=a["cache_k"].shape[0] - 1)
                            sp.wait_ge(page_used, r * RING + (2 * g + kv) * BG * NPG + u + 1)
                            sp.dma_start(page[:, u, :], cache[ds(n, 1)].rearrange("n p h d -> p (n h d)")
                                         ).then_inc(page_loaded[u], 16)

        @block.gpsimd
        def _(pool):
            pool.memset(zero[:], 0.0).then_inc(zeroed, 1)
            pool.wait_ge(zeroed, 1)
            pool.memset(ck[64:P, :], 1.0).then_inc(ones_set, 1)
            pool.memset(ck_new[64:P, :, :], 1.0).then_inc(ones_set, 1)

        def key_pages(eng, b, body):
            if b < BG - 1:
                with eng.Fori(0, NP2) as r:
                    for w in range(2):
                        body(r, w, False)
            else:
                for r in range(NP2):
                    for w in range(2):
                        body(r, w, r == NP2 - 1 and w == 1)

        @block.tensor
        def _(pe):
            pe.sem_inc(page_used, RING)
            pe.sem_inc(quad_scored, 2)
            pe.wait_ge(zeroed, 1)

            def gates(c):
                if c:
                    pe.wait_ge(summed, c)
                for j in range(4):
                    mm = pe.transpose(ov[0][0:NB * H, j * P:(j + 1) * P], lf[:, 4 * c + j].rearrange("p b h -> p (b h)"), e.c("ident"))
                mm.then_inc(lf_turned, 1)

            def turn(g, b, r, u):
                pe.wait_ge(page_loaded[u], 16 * (r + 1 + (2 * g * BG + b) * NP2))
                for p in range(HP):
                    mm = pe.transpose(ktp[u % 2][:, p, :], page[:, u, p * P:(p + 1) * P], e.c("ident"))
                mm.then_inc(page_used, 1)

            def turn_out(s):
                pe.wait_ge(o_out, s + 1)
                if s:
                    pe.wait_ge(o_kept, s)
                for p in range(HP):
                    mm = pe.transpose(o_cols[:, p * NS:(p + 1) * NS], o_rows[:, s % 2, p * P:(p + 1) * P],
                                      e.c("ident")[0:NS, 0:NS])
                mm.then_inc(o_turned, 1)

            for g in range(NG):
                if g:
                    pe.wait_ge(exped, g)
                for c in range(4):
                    pe.matmul(score[:, c * 512:(c + 1) * 512], e.identb[:], zero[:], start=True, stop=False)
                pe.matmul(score[:, PAST:KEYS], e.identb[:], e.own_pastb[:, g * NS:(g + 1) * NS], start=True, stop=False)
                for b in range(BG):
                    for p in range(HP):
                        pe.matmul(score[:, PAST:KEYS], qs[:, g * BG + b, p, :], e.qkv[:, HP + p, SEQ:NT], start=False, stop=False)
                for u in range(4):
                    if u >= 2:
                        pe.wait_ge(kt_out[u % 2], g * BG * NPG // 2 + 1)
                    turn(g, 0, 0, u)
                for b in range(BG):
                    if g == 0:
                        gates(b)

                    def quad(r, w, last):
                        out = (g * BG + b) * NPG // 2 + 4 * r + 2 * w
                        for x in range(4):
                            if not last:
                                pe.wait_ge(kt_out[x % 2], out + 1 + (x + 2) // 2)
                                turn(g, b, r + w, 4 * (1 - w) + x)
                            if x == 0:
                                for z in range(2):
                                    pe.wait_ge(kt_out[z], out + 2)
                            mm = pe.matmul(score[:, ds(r * (RING * P) + 4 * w * P, 4 * P)], qs[:, g * BG + b, x, :],
                                           kt[:, w, x, :], start=False, stop=False)
                        mm.then_inc(quad_scored, 1)
                    key_pages(pe, b, quad)
                pe.wait_ge(prepared, 1)
                for c in range(4):
                    pe.matmul(score[:, c * 512:(c + 1) * 512], row[:, g * BG:(g + 1) * BG].rearrange("p b h t -> p (b h t)"),
                              ck[:, c * 512:(c + 1) * 512], start=False, stop=True)
                pe.matmul(score[:, PAST:KEYS], row[:, g * BG:(g + 1) * BG].rearrange("p b h t -> p (b h t)"),
                          ck_new[:].rearrange("p b t -> p (b t)"), start=False, stop=True).then_inc(scored, 1)
                pe.wait_ge(prob_ready, g + 1)
                for x in range(5):
                    m = 5 * g + x
                    if x >= 2:
                        pe.wait_ge(p_kept, m - 1)
                    for y in range(4 if x < 4 else 1):
                        j = 4 * x + y
                        n = P if x < 4 else NS
                        mm = pe.transpose(ktp[x % 2][0:n, y, :], prob[:, j * P:j * P + n], e.c("ident"))
                    mm.then_inc(p_turned, 1)
                pe.wait_ge(p_kept, 5 * g + 5)
                for b in range(BG):
                    s = g * BG + b
                    if s >= 2:
                        pe.wait_ge(o_out, s - 1)
                    for n in range(NPG):
                        pe.wait_ge(page_loaded[n % RING], 16 * (n // RING + 1 + ((2 * g + 1) * BG + b) * NP2))
                        pe.matmul(ov[s % 2][0:NS, :], probT[:, n, b * NS:(b + 1) * NS], page[:, n % RING, :],
                                  start=(n == 0), stop=False).then_inc(page_used, 1)
                    pe.matmul(ov[s % 2][0:NS, :], probT[0:NS, NPG, b * NS:(b + 1) * NS], e.v_tok[0:NS, TT, :],
                              start=False, stop=True).then_inc(mixed, 1)
                    if b:
                        turn_out(s - 1)
                turn_out(s)
                pe.wait_ge(o_kept, s + 1)

        def keys_out(eng, copy, z, g, b):
            with eng.Fori(0, NP2) as r:
                for w in range(2):
                    eng.wait_ge(quad_scored, 4 * (g * BG + b) + 2 * r + w + 1)
                    for x in (z, z + 2):
                        eng.wait_ge(page_used, used_before(g, 0, b, RING * r + 4 * w + x + 1))
                        copy(kt[:, w, :, x * P:(x + 1) * P], ktp[z][:]).then_inc(kt_out[z], 1)

        @block.scalar
        def _(act):
            for g in range(NG):
                for b in range(BG):
                    keys_out(act, act.copy, 0, g, b)
                act.wait_ge(biased, g + 1)
                if g:
                    act.wait_ge(p_turned, 5 * g)
                act.activation(prob[:], score[:, 0:KEYS], ACT.Exp, scale=0.125, bias=stat[:, 1:2],
                               accum_out=stat[:, 2:3]).then_inc(exped, 1)

        @block.vector
        def _(dve):
            dve.wait_ge(ones_set, 2)

            def sum_gates(c):
                dve.wait_ge(lf_turned, c + 1)
                dve.tensor_tensor_scan(
                    ck[0:64, c * 512:(c + 1) * 512], e.ones[0:64, 0:512], ov[0][0:64, 0:512],
                    0.0 if c == 0 else ck[0:64, c * 512 - 1:c * 512], ALU.mult, ALU.add).then_inc(summed, 1)
                dve.wait_ge(summed, c + 1)

            def sum_new_gates():
                dve.wait_ge(new_loaded, 16 * NB)
                steps.then(dve, dve.tensor_tensor_scan(ck[0:64, PAST:PAST + TS], e.ones[0:64, 0:TS], lf_new[:],
                                                       ck[0:64, PAST - 1:PAST], ALU.mult, ALU.add))
                cq = ck[0:64, PAST:PAST + TS]
                steps.done(dve.tensor_copy(ck_new[0:64], cq.unsqueeze(1).to_broadcast([64, NB, TS])))
                steps.done(dve.tensor_copy(stat[64:P, 0:4], cq))
                steps.done(dve.tensor_copy(row[:].rearrange("p b h t -> p (b h t)"), e.c("row_sel")))
                steps.settle(dve)
                rows = row[64:P].rearrange("p b h t -> p (b h) t")
                dve.tensor_tensor(rows, rows, stat[64:P, 0:4].unsqueeze(1).to_broadcast([64, NB * H, TS]),
                                  ALU.mult).then_inc(prepared, 1)

            for g in range(NG):
                for b in range(BG):
                    keys_out(dve, dve.tensor_copy, 1, g, b)
                    if g == 0:
                        sum_gates(b)
                if g == 0:
                    sum_new_gates()
                dve.wait_ge(scored, g + 1)
                dve.wait_ge(prepared, 1)
                dve.reduce_max(stat[:, 0:1], score[:, 0:KEYS], X).then_inc(maxed, 1)
                dve.wait_ge(maxed, g + 1)
                dve.tensor_scalar(stat[:, 1:2], stat[:, 0:1], -0.125, None, ALU.mult).then_inc(biased, 1)
                dve.wait_ge(exped, g + 1)
                dve.reciprocal(stat[:, 3:4], stat[:, 2:3]).then_inc(recip, 1)
                dve.wait_ge(recip, g + 1)
                dve.tensor_scalar(prob[:], prob[:], stat[:, 3:4], None, ALU.mult).then_inc(prob_ready, 1)
                for x in range(5):
                    dve.wait_ge(p_turned, 5 * g + x + 1)
                    if g:
                        dve.wait_ge(mixed, g * BG)
                    if x < 4:
                        dve.tensor_copy(probT[:, 4 * x:4 * x + 4, :], ktp[x % 2][:]).then_inc(p_kept, 1)
                    else:
                        dve.tensor_copy(probT[0:NS, NPG, :], ktp[x % 2][0:NS, 0, :]).then_inc(p_kept, 1)
                def keep(s):
                    dve.wait_ge(o_turned, s + 1)
                    for z in range(2):
                        half = slice(64 * z, 64 * z + 64)
                        own = o_cols[half, 0:HP * (NS + 2 * TS)].rearrange("p (j x) -> p j x", j=HP)[:, :, z * TS:(z + 1) * TS]
                        ins = dve.tensor_copy(e.oaT[half, :, SEQ + s * TS:SEQ + (s + 1) * TS], own)
                    ins.then_inc(o_kept, 1)

                for b in range(BG):
                    s = g * BG + b
                    dve.wait_ge(mixed, s + 1)
                    if s >= 2:
                        dve.wait_ge(o_turned, s - 1)
                    dve.tensor_copy(o_rows[:, s % 2], ov[s % 2][0:NS, :]).then_inc(o_out, 1)
                    if b:
                        keep(s - 1)
                keep(s)


def stage_rwkv_project(e):
    e.fox_mem.close()
    e.obT = e.sb("obT", [P, HP, NT])
    e.rw_mem = e.ctx.enter_context(ExitStack())
    e.u = e.rw_mem.enter_context(e.nc.sbuf_tensor("u_rw", [P, 14, NT], F32))
    with memory(e) as (sb, ps), e.nc.Block() as block:
        project_tiles(e, "rw", sb, ps, block, 12, 14, e.u)


def stage_rwkv_prepare(e):
    nc, a, sem = e.nc, e.a, e.sem
    rw = lambda name, shape: e.rw_mem.enter_context(nc.sbuf_tensor(name, shape, F32))
    e.alpha, e.beta = rw("alpha", [P, HP, NT]), rw("beta", [P, HP, NT])
    e.rho, e.gamma, e.val = e.u[:, 0:4], e.u[:, 4:8], e.u[:, 8:12]
    e.chunk_decay = rw("chunk_decay", [P, HP, NCH])
    e.dec_s = rw("dec_s", [P, HP, NS])
    loaded, shifted, stored = sem("lora_loaded"), sem("rw_shifted"), sem("shift_stored")
    shift_kept = sem("shift_kept")
    tanh_done, sg, sa = sem("rw_tanh"), sem("rw_sig_z"), sem("rw_sig_a")
    made_z, made_a, sq_done, made_s = sem("rw_made_z"), sem("rw_made_a"), sem("rw_sq"), sem("rw_made_s")
    ss_max, rt, exps, rk_ready, made_b, bonus_done = (sem("rw_ss_max"), sem("rw_root"), sem("rw_exps"),
                                                      sem("rw_rk"), sem("rw_made_b"), sem("rw_bonus"))
    cum_ready, pair_done = sem("rw_cum"), sem("rw_pair_done")
    st = e.steps["dve"]
    with memory(e) as (sb, ps), nc.Block() as block:
        lora = sb("lora_w", [P, W])
        old = sb("shift_old", [P, 14, NB])
        last = sb("shift_last", [P, 14, NB + 1])
        t2, t3, t4 = (sb(f"rw_t{n}", [P, NT]) for n in range(2, 5))
        t01 = [[sb(f"rw_t{n}_{b}", [P, NT]) for n in range(2)] for b in range(2)]
        moved = e.alpha[:, HP - 1], e.beta[:, HP - 1]
        keep = sb("keep", [P, SEQ])
        zp, ap_ = ps("rw_zp", [P, 3, 512]), ps("rw_ap", [P, 3, 512])

        @block.sync
        def _(sp):
            sp.dma_start(old[:], a["shiftT"]).then_inc(loaded, 16)
            sp.dma_start(lora[0:64, :], a["w2"]).then_inc(loaded, 16)
            sp.dma_start(lora[64:P, :], a["a2"]).then_inc(loaded, 16)
            sp.wait_ge(shift_kept, 1)
            sp.dma_start(a["shift_out"], last[:]).then_inc(stored, 16)
            sp.wait_ge(stored, 16)

        @block.tensor
        def _(pe):
            pe.wait_ge(tanh_done, 1)
            for p in range(HP):
                if p:
                    pe.wait_ge(ss_max, p)
                for c, (at, n) in enumerate(COLS):
                    mm = pe.matmul(zp[:, c, 0:n], lora[0:64, p * P:(p + 1) * P], e.u[0:64, 12, at:at + n],
                                   start=True, stop=True)
                mm.then_inc(made_z, 1)
                if p:
                    pe.wait_ge(bonus_done, p)
                for c, (at, n) in enumerate(COLS):
                    mm = pe.matmul(ap_[:, c, 0:n], lora[64:P, p * P:(p + 1) * P], e.u[64:P, 12, at:at + n],
                                   start=True, stop=True)
                mm.then_inc(made_a, 1)
                pe.wait_ge(sq_done, p + 1)
                pe.wait_ge(sg, p + 1)
                for c, (at, n) in enumerate(COLS):
                    mm = pe.matmul(zp[:, c, 0:n], e.c("head_ones"), t2[:, at:at + n], start=True, stop=True)
                mm.then_inc(made_s, 1)
                pe.wait_ge(rk_ready, p + 1)
                pe.wait_ge(sa, p + 1)
                for c, (at, n) in enumerate(COLS):
                    mm = pe.matmul(ap_[:, c, 0:n], e.c("head_ones"), t4[:, at:at + n], start=True, stop=True)
                mm.then_inc(made_b, 1)

        def cols(out, banks):
            yield out[:, 0:SEQ].rearrange("p (c n) -> p c n", c=2), banks[:, 0:2, :]
            yield out[:, SEQ:NT], banks[:, 2, 0:NS]

        @block.scalar
        def _(act):
            act.wait_ge(shifted, 1)
            act.activation(e.u[0:64, 12, :], e.u[0:64, 12, :], ACT.Tanh).then_inc(tanh_done, 1)
            act.wait_ge(shifted, 2)
            act.activation(e.u[:, 13, :], e.u[:, 13, :], ACT.Sigmoid)
            for p in range(HP):
                t0, t1 = t01[p % 2]
                act.wait_ge(made_z, p + 1)
                for out, banks in cols(t0[:], zp):
                    ins = act.activation(out, banks, ACT.Sigmoid, bias=e.v("w0")[:, p:p + 1])
                ins.then_inc(sg, 1)
                act.wait_ge(made_a, p + 1)
                for out, banks in cols(t1[:], ap_):
                    ins = act.activation(out, banks, ACT.Sigmoid, bias=e.v("a0")[:, p:p + 1])
                ins.then_inc(sa, 1)
                if p:
                    act.wait_ge(pair_done, p)
                act.wait_ge(shifted, 5 + 3 * p)
                act.activation(t2[:], e.gamma[:, p], ACT.Square, scale=e.v("k_k")[:, p:p + 1]).then_inc(sq_done, 1)
                act.wait_ge(ss_max, p + 1)
                act.activation(t2[:], t2[:], ACT.Sqrt).then_inc(rt, 1)
                act.wait_ge(cum_ready, p + 1)
                act.activation(t1[:, 0:SEQ], t1[:, 0:SEQ], ACT.Exp)
                act.activation(e.dec_s[:, p], t0[:, SEQ:NT], ACT.Exp)
                act.activation(t2[:, 0:SEQ], t3[:, 0:SEQ], ACT.Exp, scale=-1.0).then_inc(exps, 1)
                act.wait_ge(exps, 2 * p + 1)
                act.activation(t3[:, 0:SEQ], t3[:, 0:SEQ], ACT.Exp).then_inc(exps, 1)

        @block.vector
        def _(dve):
            st.then(dve, dve.memset(keep[:], 1.0))
            st.then(dve, dve.memset(keep[:, 0:SEQ:C], 0.0))
            dve.wait_ge(loaded, 48)
            dve.tensor_copy(last[:, :, 0:1], e.u[:, :, SEQ - 1:SEQ])
            dve.tensor_copy(last[:, :, 1:], e.u[:, :, SEQ + TS - 1:NT:TS]).then_inc(shift_kept, 1)
            samples = lambda x: x.rearrange("p (b t) -> p b t", t=TS)

            def shift(n, j):
                d, u = moved[n % 2], e.u[:, j]
                if n >= 2:
                    dve.wait_ge(shifted, n - 1)
                dve.tensor_tensor(d[:, 1:SEQ], u[:, 0:SEQ - 1], u[:, 1:SEQ], ALU.subtract)
                dve.tensor_scalar(d[:, 0:1], u[:, 0:1], -1.0, None, ALU.mult)
                ds_, us = samples(d[:, SEQ:NT]), samples(u[:, SEQ:NT])
                dve.tensor_tensor(ds_[:, :, 1:], us[:, :, 0:TS - 1], us[:, :, 1:], ALU.subtract)
                st.then(dve, dve.tensor_tensor(ds_[:, :, 0], old[:, j], us[:, :, 0], ALU.subtract))
                dve.scalar_tensor_tensor(u, d, e.v("mu")[:, j:j + 1], u, ALU.mult, ALU.add).then_inc(shifted, 1)

            def shift_pair(p):
                for n in range(3):
                    shift(2 + 3 * p + n, HP * n + p)
            shift(0, 12)
            shift(1, 13)
            shift_pair(0)
            for p in range(HP):
                r, k, v = e.rho[:, p], e.gamma[:, p], e.val[:, p]
                t0, t1 = t01[p % 2]
                dve.wait_ge(shifted, 5 + 3 * p)
                dve.wait_ge(sg, p + 1)
                st.then(dve, dve.tensor_scalar(t0[:], t0[:], -EXP_HALF, None, ALU.mult))
                st.then(dve, dve.tensor_tensor_scan(t3[:, 0:SEQ], keep[:], t0[:, 0:SEQ], 0.0, ALU.mult, ALU.add))
                if p + 1 < HP:
                    shift_pair(p + 1)
                dve.wait_ge(made_s, p + 1)
                for out, banks in cols(t2[:], zp):
                    ins = dve.tensor_scalar(out, banks, 1e-24, None, ALU.max)
                ins.then_inc(ss_max, 1)
                dve.wait_ge(rt, p + 1)
                st.then(dve, dve.reciprocal(t2[:], t2[:]))
                st.then(dve, dve.scalar_tensor_tensor(e.alpha[:, p], k, e.v("k_k")[:, p:p + 1], t2[:], ALU.mult, ALU.mult))
                st.then(dve, dve.tensor_tensor(e.beta[:, p], e.alpha[:, p], t1[:], ALU.mult))
                st.then(dve, dve.tensor_scalar(t1[:], t1[:], 1.0, e.v("k_a")[:, p:p + 1], ALU.subtract, ALU.mult))
                st.then(dve, dve.scalar_tensor_tensor(k, t1[:], 1.0, k, ALU.add, ALU.mult))
                dve.scalar_tensor_tensor(t4[:], r, e.v("r_k")[:, p:p + 1], k, ALU.mult, ALU.mult).then_inc(rk_ready, 1)
                dve.tensor_tensor(t1[:, 0:SEQ], t3[:, 0:SEQ], t0[:, 0:SEQ], ALU.subtract).then_inc(cum_ready, 1)
                dve.wait_ge(made_b, p + 1)
                vb = dict(zip("ab", [v[:, 0:SEQ].rearrange("p (c n) -> p c n", c=2), v[:, SEQ:NT]]))
                for (out, banks), vv in zip(cols(e.obT[:, p], ap_), vb.values()):
                    ins = dve.tensor_tensor(out, banks, vv, ALU.mult)
                ins.then_inc(bonus_done, 1)
                dve.wait_ge(exps, 2 * p + 1)
                m = slice(0, SEQ)
                dve.tensor_tensor(e.alpha[:, p, m], e.alpha[:, p, m], t1[:, m], ALU.mult)
                dve.tensor_tensor(e.beta[:, p, m], e.beta[:, p, m], t2[:, m], ALU.mult)
                dve.tensor_tensor(k[:, m], k[:, m], t2[:, m], ALU.mult)
                dve.wait_ge(exps, 2 * p + 2)
                dve.tensor_copy(e.chunk_decay[:, p], t3[:, C - 1:SEQ:C])
                dve.tensor_tensor(r[:, m], r[:, m], t3[:, m], ALU.mult).then_inc(pair_done, 1)


def stage_rwkv_scan(e):
    nc, a, sem = e.nc, e.a, e.sem
    stored = sem("scan_stored")
    names = ("staged made_g kept_g l_masked lt_ready masked t_ready made_tok kept_tok kept_v made_y kept_y made_z "
             "t_upd made_x kept_x made_u kept_u made_o made_s state_add state_ready gn_sum gn_cent gn_sq gn_var "
             "gn_root gn_rec gn_out o_turned o_stored go").split()
    q = {n: sem(f"scan_{n}") for n in names}
    NL = len(LEVELS) - 1
    with memory(e) as (sb, ps), nc.Block() as block:
        two = lambda name: sb(name, [P, 2, HP, C])
        ar = sb("ar", [P, 2, HP, 2, C])
        be, ga, va = two("be"), two("ga"), two("va")
        rbt, mt, rgt = two("rbt"), two("mt"), two("rgt")
        btok, gtok, vtok = two("btok"), two("gtok"), two("vtok")
        tt = two("tt")
        lt, ltm = sb("lt", [P, HP, C]), sb("ltm", [P, NL, HP, C])
        tl, ys = sb("tl", [P, HP, C]), sb("ys", [P, HP, C])
        xs, un = sb("xs", [P, HP, C]), sb("un", [P, HP, C])
        state, grown = sb("state_t", [P, HP, C]), sb("state_grown", [P, HP, C])
        cent, sqr = sb("gn_cent_t", [P, HP, C]), sb("gn_sqr", [P, HP, C])
        stat = sb("gn_stat", [P, 4, HP])
        g1, g2 = ps("g1", [P, HP, 2, C]), ps("g2", [P, HP, 2, C])
        g3, tk = ps("g3", [P, 2, HP, C]), ps("tk", [P, 2, HP, C])
        yp, zp = ps("yp", [P, 512]), ps("zp", [P, HP, 2, C])
        xp, op = ps("xp", [P, 2, HP, C]), ps("scan_op", [P, 2, HP, C])

        heads = [(p, slice(64 * s, 64 * s + 64)) for p in range(HP) for s in range(2)]
        bc = lambda x: x.unsqueeze(1).to_broadcast([P, HP, C])
        flat = lambda x: x.rearrange("p a n -> p (a n)")
        ypv = yp[:, 0:HP * C].rearrange("p (h n) -> p h n", h=HP)

        def schedule(eng, body):
            body(0, 0, True, False)
            with eng.Fori(0, NCH // 2 - 1) as i:
                body(2 * i + 1, 1, True, True)
                body(2 * i + 2, 0, True, True)
            body(NCH - 1, 1, True, True)
            body(NCH, 0, False, True)

        @block.gpsimd
        def _(pool):
            def stage(c, b):
                at = ds(c * C, C)
                pool.tensor_copy(ar[:, b, :, 0, :], e.alpha[:, :, at]).then_inc(q["staged"], 1)
                pool.tensor_copy(ar[:, b, :, 1, :], e.rho[:, :, at]).then_inc(q["staged"], 1)
                pool.tensor_copy(be[:, b], e.beta[:, :, at]).then_inc(q["staged"], 1)
                pool.tensor_copy(ga[:, b], e.gamma[:, :, at]).then_inc(q["staged"], 1)
                pool.tensor_copy(va[:, b], e.val[:, :, at]).then_inc(q["staged"], 1)
            stage(0, 0)
            stage(1, 1)
            with pool.Fori(1, NCH // 2) as i:
                for b in range(2):
                    pool.wait_ge(q["made_o"], 2 * i + b - 1)
                    stage(2 * i + b, b)

        @block.tensor
        def _(pe):
            ident = e.c("ident")

            def each(out, lhsT, rhs, start=True, stop=True):
                for p, hs in heads:
                    mm = pe.matmul(out(p, hs), lhsT(p, hs), rhs(p, hs), start=start, stop=stop)
                return mm

            def go():
                pe.sem_inc(q["go"], 1)

            def grams(c, b):
                pe.wait_ge(q["staged"], 5 * c + 5)
                pe.wait_ge(q["kept_g"], 3 * c)
                pe.wait_ge(q["kept_v"], c)
                pe.wait_ge(q["kept_tok"], 2 * c)
                go()
                both = lambda p, hs: flat(ar[hs, b, p])
                each(lambda p, hs: flat(g1[hs, p]), lambda p, hs: be[hs, b, p], both)
                each(lambda p, hs: flat(g2[hs, p]), lambda p, hs: ga[hs, b, p], both)
                each(lambda p, hs: g3[hs, 0, p], lambda p, hs: ar[hs, b, p, 0], lambda p, hs: be[hs, b, p])
                each(lambda p, hs: g3[hs, 1, p], lambda p, hs: va[hs, b, p], lambda p, hs: ident[hs, hs]).then_inc(q["made_g"], 1)
                each(lambda p, hs: tk[hs, 0, p], lambda p, hs: be[hs, b, p], lambda p, hs: ident[hs, hs])
                each(lambda p, hs: tk[hs, 1, p], lambda p, hs: ga[hs, b, p], lambda p, hs: ident[hs, hs]).then_inc(q["made_tok"], 1)

            def level_y(c, b, l):
                if l == 0:
                    pe.wait_ge(q["t_ready"], 2 * c + 2)
                    pe.wait_ge(q["masked"], c + 1)
                pe.wait_ge(q["t_upd"], c * NL + l)
                go()
                each(lambda p, hs: ypv[hs, p], lambda p, hs: ltm[hs, l, p], lambda p, hs: tl[hs, p]).then_inc(q["made_y"], 1)

            def level_z(c, b, l):
                pe.wait_ge(q["kept_y"], c * NL + l + 1)
                go()
                if l < NL - 1:
                    each(lambda p, hs: zp[hs, p, 0], lambda p, hs: tt[hs, b, p], lambda p, hs: ys[hs, p])
                each(lambda p, hs: zp[hs, p, 1], lambda p, hs: ys[hs, p], lambda p, hs: tt[hs, b, p]).then_inc(q["made_z"], 1)

            def x(c, b):
                pe.wait_ge(q["kept_tok"], 2 * c + 2)
                pe.wait_ge(q["kept_v"], c + 1)
                pe.wait_ge(q["kept_g"], 3 * c + 3)
                pe.wait_ge(q["state_ready"], c + 1)
                go()
                for p, hs in heads:
                    pe.matmul(xp[hs, 0, p], ar[hs, b, p, 0], state[hs, p], start=True, stop=False)
                    mm = pe.matmul(xp[hs, 0, p], mt[hs, b, p], vtok[hs, b, p], start=False, stop=True)
                mm.then_inc(q["made_x"], 1)

            def u(c, b):
                pe.wait_ge(q["kept_x"], c + 1)
                pe.wait_ge(q["t_upd"], NL * (c + 1))
                pe.wait_ge(q["o_stored"], c + 1)
                go()
                each(lambda p, hs: op[hs, 1, p], lambda p, hs: tt[hs, b, p], lambda p, hs: xs[hs, p]).then_inc(q["made_u"], 1)

            def s_and_o(c, b):
                pe.wait_ge(q["kept_u"], c + 1)
                go()
                for p, hs in heads:
                    pe.matmul(xp[hs, 1, p], btok[hs, b, p], un[hs, p], start=True, stop=False)
                    mm = pe.matmul(xp[hs, 1, p], gtok[hs, b, p], vtok[hs, b, p], start=False, stop=True)
                mm.then_inc(q["made_s"], 1)
                for p, hs in heads:
                    pe.matmul(op[hs, 0, p], ar[hs, b, p, 1], state[hs, p], start=True, stop=False)
                    pe.matmul(op[hs, 0, p], rbt[hs, b, p], un[hs, p], start=False, stop=False)
                    mm = pe.matmul(op[hs, 0, p], rgt[hs, b, p], vtok[hs, b, p], start=False, stop=True)
                mm.then_inc(q["made_o"], 1)

            def turn(c):
                pe.wait_ge(q["gn_out"], c + 1)
                go()
                each(lambda p, hs: op[hs, 1, p], lambda p, hs: sqr[hs, p], lambda p, hs: ident[hs, hs]).then_inc(q["o_turned"], 1)

            def body(c, b, A, B):
                d = 1 - b
                if B:
                    x(c - 1, d)
                if A:
                    grams(c, b)
                if B:
                    u(c - 1, d)
                if A:
                    level_y(c, b, 0)
                if B:
                    s_and_o(c - 1, d)
                if A:
                    level_z(c, b, 0)
                    for l in (1, 2):
                        level_y(c, b, l)
                        level_z(c, b, l)
                if B:
                    turn(c - 1)
                if A:
                    for l in range(3, NL):
                        level_y(c, b, l)
                        level_z(c, b, l)
            schedule(pe, body)

        @block.scalar
        def _(act):
            def body(c, b, A, B):
                m = c - 1

                def keep_y(l):
                    act.wait_ge(q["made_y"], c * NL + l + 1)
                    act.copy(ys[:], ypv).then_inc(q["kept_y"], 1)
                if B:
                    act.wait_ge(q["made_x"], m + 1)
                    act.copy(xs[:], xp[:, 0]).then_inc(q["kept_x"], 1)
                if A:
                    act.wait_ge(q["made_tok"], c + 1)
                    act.copy(btok[:, b], tk[:, 0]).then_inc(q["kept_tok"], 1)
                    act.copy(gtok[:, b], tk[:, 1]).then_inc(q["kept_tok"], 1)
                if B:
                    act.wait_ge(q["made_u"], m + 1)
                    act.mul(un[:], op[:, 1], -1.0).then_inc(q["kept_u"], 1)
                if A:
                    act.wait_ge(q["l_masked"], c + 1)
                    act.copy(vtok[:, b], g3[:, 1]).then_inc(q["kept_v"], 1)
                    keep_y(0)
                    keep_y(1)
                if B:
                    act.wait_ge(q["gn_var"], m + 1)
                    act.activation(stat[:, 2], stat[:, 1], ACT.Sqrt, scale=1.0 / DH, bias=e.eps[:, 1:2]).then_inc(q["gn_root"], 1)
                if A:
                    keep_y(2)
                if B:
                    act.wait_ge(q["o_turned"], m + 1)
                    act.copy(e.alpha[:, :, ds(m * C, C)], op[:, 1]).then_inc(q["o_stored"], 1)
                if A:
                    for l in range(3, NL):
                        keep_y(l)
            act.sem_inc(q["o_stored"], 1)
            schedule(act, body)

        @block.vector
        def _(dve):
            dve.memset(state[:], 0.0).then_inc(q["state_ready"], 1)

            def prepare(c, b):
                dve.wait_ge(q["made_g"], c + 1)
                dve.tensor_copy(lt[:], g1[:, :, 0, :]).then_inc(q["lt_ready"], 1)
                dve.tensor_tensor(tl[:], g3[:, 0], bc(e.c("level0")), ALU.mult).then_inc(q["l_masked"], 1)
                dve.wait_ge(q["lt_ready"], 2 * c + 1)
                dve.tensor_tensor(tt[:, b], lt[:], bc(e.c("levels_t")[:, 0:C]), ALU.mult).then_inc(q["lt_ready"], 1)
                dve.wait_ge(q["l_masked"], c + 1)
                dve.tensor_tensor(tl[:], tl[:], bc(e.c("lower_eye")), ALU.add).then_inc(q["t_ready"], 1)
                dve.wait_ge(q["lt_ready"], 2 * c + 2)
                dve.tensor_tensor(tt[:, b], tt[:, b], bc(e.c("lower_eye")), ALU.add).then_inc(q["t_ready"], 1)
                for l in range(NL):
                    ins = dve.tensor_tensor(ltm[:, l], lt[:], bc(e.c("levels_t")[:, (l + 1) * C:(l + 2) * C]), ALU.mult)
                ins.then_inc(q["masked"], 1)
                dve.tensor_tensor(rbt[:, b], g1[:, :, 1, :], bc(e.c("upper_diag")), ALU.mult).then_inc(q["kept_g"], 1)
                dve.tensor_tensor(mt[:, b], g2[:, :, 0, :], bc(e.c("upper")), ALU.mult).then_inc(q["kept_g"], 1)
                dve.tensor_tensor(rgt[:, b], g2[:, :, 1, :], bc(e.c("upper_diag")), ALU.mult).then_inc(q["kept_g"], 1)

            def update(c, b, l):
                n = c * NL + l
                dve.wait_ge(q["made_z"], n + 1)
                dve.wait_ge(q["t_ready"], 2 * c + 2)
                dve.wait_ge(q["t_upd"], n)
                if l < NL - 1:
                    dve.tensor_tensor(tl[:], tl[:], zp[:, :, 0, :], ALU.subtract)
                dve.tensor_tensor(tt[:, b], tt[:, b], zp[:, :, 1, :], ALU.subtract).then_inc(q["t_upd"], 1)

            def new_state(c):
                dve.wait_ge(q["made_o"], c + 1)
                dve.tensor_tensor(grown[:], state[:], xp[:, 1], ALU.add).then_inc(q["state_add"], 1)
                dve.wait_ge(q["state_add"], c + 1)
                dve.tensor_tensor(state[:], grown[:], e.chunk_decay[:, :, ds(c, 1)].to_broadcast([P, HP, C]),
                                  ALU.mult).then_inc(q["state_ready"], 1)

            def centre(c):
                dve.reduce_sum(stat[:, 0], op[:, 0], X).then_inc(q["gn_sum"], 1)
                dve.wait_ge(q["gn_sum"], c + 1)
                dve.scalar_tensor_tensor(cent[:], stat[:, 0].unsqueeze(2).to_broadcast([P, HP, C]), -1.0 / DH, op[:, 0],
                                         ALU.mult, ALU.add).then_inc(q["gn_cent"], 1)
                dve.wait_ge(q["gn_cent"], c + 1)
                dve.tensor_tensor(sqr[:], cent[:], cent[:], ALU.mult).then_inc(q["gn_sq"], 1)
                dve.wait_ge(q["gn_sq"], c + 1)
                dve.reduce_sum(stat[:, 1], sqr[:], X).then_inc(q["gn_var"], 1)

            def normalise(c):
                dve.wait_ge(q["gn_root"], c + 1)
                dve.reciprocal(stat[:, 3], stat[:, 2]).then_inc(q["gn_rec"], 1)
                dve.wait_ge(q["gn_rec"], c + 1)
                dve.tensor_tensor(sqr[:], cent[:], stat[:, 3].unsqueeze(2).to_broadcast([P, HP, C]),
                                  ALU.mult).then_inc(q["gn_out"], 1)

            def body(c, b, A, B):
                if A:
                    prepare(c, b)
                if B:
                    new_state(c - 1)
                if A:
                    update(c, b, 0)
                if B:
                    centre(c - 1)
                if A:
                    update(c, b, 1)
                if B:
                    normalise(c - 1)
                if A:
                    for l in range(2, NL):
                        update(c, b, l)
            schedule(dve, body)

        @block.sync
        def _(sp):
            sp.wait_ge(q["state_ready"], NCH + 1)
            sp.dma_start(a["wkv_prompt"], state[:]).then_inc(stored, 16)
            sp.wait_ge(stored, 16)


def stage_rwkv_sample(e):
    nc, a, sem = e.nc, e.a, e.sem
    st = e.steps["dve"]
    turned, kept, sent, back, loaded = sem("rs_turned"), sem("rs_kept"), [sem(f"rs_sent{z}") for z in range(2)], sem("rs_back"), sem("rs_loaded")
    outer, o_ready, o_sent, o_back = sem("rs_outer"), sem("rs_o_ready"), sem("rs_o_sent"), sem("rs_o_back")
    var, root, oh_ready, o_turned = sem("rs_var"), sem("rs_root"), sem("rs_oh"), sem("rs_o_turned")
    gained, gate_kept, bonused = sem("rs_gained"), sem("rs_gate_kept"), sem("rs_bonused")
    gate_made, gate_used, ready = sem("rs_gate_made"), sem("rs_gate_used"), sem("rs_v_ready")
    state_done, stored, used = sem("rs_state_done"), sem("rs_stored"), sem("rs_outer_used")
    NV = 6
    with memory(e) as (sb, ps), nc.Block() as block:
        g2w = sb("g2w", [P, W])
        vec = sb("rs_vec", [P, NV, TS, DH])
        vz = sb("rs_vz", [P, TS, DH // 2])
        o = sb("rs_o", [P, TS, DH // 2])
        nsk = sb("rs_nsk", [P, DH // 2])
        stat = sb("rs_stat", [NS, 4, H])
        ot, cent, sq = (sb(f"rs_tok{n}", [NS, H, DH]) for n in range(3))
        flat = lambda x: x.rearrange("p h n -> p (h n)")
        cube = lambda x: flat(x)[:, 0:2048].rearrange("p (v k) -> p v k", k=DH)
        vt = flat(e.gamma)[0:NS, 0:NV * W].rearrange("p (v c) -> p v c", v=NV)
        state, tmp = cube(e.beta), flat(e.beta)[:, 2048:4096].rearrange("p (v k) -> p v k", k=DH)
        prod = cube(e.gamma)
        scr, gate, last = sb("rs_scr", [P, SEQ]), sb("rs_gate", [P, SEQ]), sb("rs_last", [P, HP, NS])
        tp = ps("rs_t", [NS, NV, W])
        gp = ps("rs_g", [P, 2, 512])

        def send(eng, z):
            eng.wait_ge(kept, 1)
            for b in range(NB):
                for v in range(z, NV, 2):
                    eng.dma_start(e.sv_d[v, b].rearrange("h t d -> t h d"),
                                  vt[b * TS:(b + 1) * TS, v].rearrange("t (h d) -> t h d", h=H)).then_inc(sent[z], 16)

        @block.sync
        def _(sp):
            sp.dma_start(g2w[:], a["g2"]).then_inc(loaded, 16)
            send(sp, 0)
            for z in range(2):
                sp.dma_start(flat(e.beta)[64 * z:64 * z + 64, 0:2048],
                             a["state"].rearrange("b h (z v) k -> z (b h) (v k)", z=2)[z]).then_inc(back, 16)
            for z in range(2):
                sp.wait_ge(sent[z], 16 * NB * NV // 2)
            for z in range(2):
                sp.dma_start(vec[64 * z:64 * z + 64].rearrange("p v t d -> p v (t d)"),
                             e.sv_d.rearrange("v b h t d -> (b h) v (t d)")).then_inc(back, 16)
            sp.wait_ge(o_ready, TS)
            for z in range(2):
                for b in range(NB):
                    sp.dma_start(e.so_d[b * TS:(b + 1) * TS, :].rearrange("t (h z v) -> z h t v", h=H, z=2)[z],
                                 o[64 * z + 8 * b:64 * z + 8 * b + 8]).then_inc(o_sent, 16)
            sp.wait_ge(o_sent, 16 * 2 * NB)
            sp.dma_start(ot[:].rearrange("p h d -> p (h d)"), e.so_d).then_inc(o_back, 16)
            for z in range(2):
                sp.dma_start(a["wkv_sample"].rearrange("b h (z v) k -> z (b h) (v k)", z=2)[z],
                             flat(e.beta)[64 * z:64 * z + 64, 0:2048]).then_inc(stored, 16)
            sp.wait_ge(stored, 32)

        @block.tensor
        def _(pe):
            for v, src in enumerate((e.alpha, e.beta, e.gamma, e.rho, e.val, e.dec_s)):
                for p in range(HP):
                    col = src[:, p, SEQ:NT] if v < 5 else src[:, p]
                    mm = pe.transpose(tp[:, v, p * P:(p + 1) * P], col, e.c("ident"))
            mm.then_inc(turned, 1)
            pe.wait_ge(loaded, 16)
            pe.wait_ge(kept, 1)
            for p in range(HP):
                for c in range(2):
                    n = 2 * p + c
                    if n >= 2:
                        pe.wait_ge(gate_kept, n - 1)
                    pe.matmul(gp[:, n % 2], g2w[:, p * P:(p + 1) * P], e.u[:, 13, c * 512:(c + 1) * 512],
                              start=True, stop=True).then_inc(gate_made, 1)
            pe.wait_ge(gate_kept, 2 * HP)
            pe.wait_ge(oh_ready, 1)
            for p in range(HP):
                mm = pe.transpose(gp[:, 0, p * NS:(p + 1) * NS], sq[:].rearrange("p h d -> p (h d)")[:, p * P:(p + 1) * P],
                                  e.c("ident")[0:NS, 0:NS])
            mm.then_inc(o_turned, 1)
            for p in range(HP):
                mm = pe.matmul(gp[:, 1, p * NS:(p + 1) * NS], g2w[:, p * P:(p + 1) * P], e.u[:, 13, SEQ:NT],
                               start=True, stop=True)
            mm.then_inc(gate_made, 1)

        @block.gpsimd
        def _(pool):
            pool.wait_ge(ready, 1)
            for t in range(TS):
                if t:
                    pool.wait_ge(used, t)
                pool.tensor_tensor(prod, vz[:, t].unsqueeze(2).to_broadcast([P, DH // 2, DH]),
                                   vec[:, 2, t].unsqueeze(1).to_broadcast([P, DH // 2, DH]), ALU.mult).then_inc(outer, 1)
                pool.wait_ge(gained, t + 1)
                pool.wait_ge(gate_kept, 2 * t + 2)
                ob = e.obT[:, t, 0:SEQ]
                pool.tensor_tensor(ob, ob, scr[:, 0:SEQ], ALU.add).then_inc(bonused, 1)
                pool.wait_ge(bonused, t + 1)
                pool.tensor_tensor(ob, ob, gate[:], ALU.mult).then_inc(gate_used, 1)

        @block.scalar
        def _(act):
            send(act, 1)
            for p in range(HP):
                if p:
                    act.wait_ge(gate_used, p)
                act.activation(scr[:, 0:SEQ], e.alpha[:, p, 0:SEQ], ACT.Identity, scale=e.v("lnx_w")[:, p:p + 1],
                               bias=e.v("lnx_b")[:, p:p + 1]).then_inc(gained, 1)
                for c in range(2):
                    n = 2 * p + c
                    act.wait_ge(gate_made, n + 1)
                    act.copy(gate[:, c * 512:(c + 1) * 512], gp[:, n % 2]).then_inc(gate_kept, 1)
            act.wait_ge(var, 1)
            act.activation(stat[:, 2], stat[:, 1], ACT.Sqrt, scale=1.0 / DH, bias=e.eps[0:NS, 1:2]).then_inc(root, 1)

        @block.vector
        def _(dve):
            dve.wait_ge(turned, 1)
            dve.tensor_copy(vt, tp[:]).then_inc(kept, 1)
            dve.wait_ge(back, 16 * 4)
            for z in range(2):
                h = slice(64 * z, 64 * z + 64)
                ins = dve.tensor_copy(vz[h], vec[h, 4, :, 32 * z:32 * z + 32])
                st.done(ins)
            st.settle(dve)
            dve.sem_inc(ready, 1)
            row = lambda v, t: vec[:, v, t].unsqueeze(1).to_broadcast([P, DH // 2, DH])
            for t in range(TS):
                if t:
                    dve.wait_ge(o_ready, t)
                st.then(dve, dve.tensor_tensor(tmp, state, row(0, t), ALU.mult))
                st.done(dve.tensor_reduce(nsk[:], tmp, X, ALU.add, negate=True))
                st.then(dve, dve.tensor_tensor(state, state, row(5, t), ALU.mult))
                st.then(dve, dve.tensor_tensor(tmp, nsk[:].unsqueeze(2).to_broadcast([P, DH // 2, DH]), row(1, t), ALU.mult))
                st.then(dve, dve.tensor_tensor(state, state, tmp, ALU.add))
                dve.wait_ge(outer, t + 1)
                dve.tensor_tensor(state, state, prod, ALU.add).then_inc(used, 1)
                dve.wait_ge(used, t + 1)
                st.then(dve, dve.tensor_tensor(tmp, state, row(3, t), ALU.mult))
                dve.tensor_reduce(o[:, t], tmp, X, ALU.add).then_inc(o_ready, 1)
            dve.wait_ge(o_back, 16)
            st.then(dve, dve.reduce_sum(stat[:, 0], ot[:], X))
            wide = lambda x: x.unsqueeze(2).to_broadcast([NS, H, DH])
            st.then(dve, dve.scalar_tensor_tensor(cent[:], wide(stat[:, 0]), -1.0 / DH, ot[:], ALU.mult, ALU.add))
            st.then(dve, dve.tensor_tensor(sq[:], cent[:], cent[:], ALU.mult))
            dve.reduce_sum(stat[:, 1], sq[:], X).then_inc(var, 1)
            dve.wait_ge(root, 1)
            st.then(dve, dve.reciprocal(stat[:, 3], stat[:, 2]))
            dve.tensor_tensor(sq[:], cent[:], wide(stat[:, 3]), ALU.mult).then_inc(oh_ready, 1)
            dve.wait_ge(o_turned, 1)
            st.then(dve, dve.tensor_copy(last[:], gp[:, 0, 0:HP * NS].rearrange("p (h n) -> p h n", h=HP)))
            for p in range(HP):
                st.then(dve, dve.tensor_scalar(last[:, p], last[:, p], e.v("lnx_w")[:, p:p + 1], e.v("lnx_b")[:, p:p + 1],
                                               ALU.mult, ALU.add))
            ob = e.obT[:, :, SEQ:NT]
            st.then(dve, dve.tensor_tensor(ob, ob, last[:], ALU.add))
            dve.wait_ge(gate_made, 2 * HP + 1)
            dve.tensor_tensor(ob, ob, gp[:, 1, 0:HP * NS].rearrange("p (h n) -> p h n", h=HP), ALU.mult)


def stage_mix(e):
    nc, a, sem = e.nc, e.a, e.sem
    e.rw_mem.close()
    e.count = e.sb("count", [1, NE + 1], I32)
    e.mix_mem = e.ctx.enter_context(ExitStack())
    e.mixedT = e.mix_mem.enter_context(nc.sbuf_tensor("mixedT", [P, KD, NT], F32))
    loaded = [sem(f"mix_w_loaded{b}") for b in range(2)]
    made, gated, summed, prods = sem("mix_made"), sem("mix_gated"), sem("mix_summed"), sem("mix_prods")
    with memory(e) as (sb, ps), nc.Block() as block:
        w = sb("mix_w", [P, 2, 24, P])
        banks = [ps(f"mix_b{b}", [P, 4, 512]) for b in range(2)]
        gate = sb("mix_gate", [P, 2, 2, 512])
        part = sb("mix_part", [P, 2, 512])
        items = [(c, at, m) for c, (at, m) in enumerate(COLS)]

        @block.sync
        def _(sp):
            def load(j, b):
                sp.dma_start(w[:, b, 0:8], a["w_in"][ds(j + 26, 1)].squeeze(0)).then_inc(loaded[b], 16)
                sp.dma_start(w[:, b, 8:16], a["w_in"][ds(j + 34, 1)].squeeze(0)).then_inc(loaded[b], 16)
                sp.dma_start(w[:, b, 16:24], a["p_ab"][ds(j, 1)].squeeze(0)).then_inc(loaded[b], 16)
            load(0, 0)
            load(1, 1)
            with sp.Fori(0, KD // 2 - 1) as i:
                for b in range(2):
                    sp.wait_ge(made, 3 * (2 * i + b + 1))
                    load(2 * i + b + 2, b)

        def loop(eng, body):
            with eng.Fori(0, KD // 2) as i:
                for b in range(2):
                    for c, at, m in items:
                        body(2 * i + b, b, i, (3 * b + c) % 2, c, at, m, 6 * i + 3 * b + c)

        @block.tensor
        def _(pe):
            pe.sem_inc(summed, 2)

            def body(j, b, i, x, c, at, m, n):
                if c == 0:
                    pe.wait_ge(loaded[b], 48 * (i + 1))
                pe.wait_ge(summed, n + 1)
                for g in range(2):
                    for k in range(KD):
                        pe.matmul(banks[x][:, g, 0:m], w[:, b, 8 * g + k, :], e.xnT[:, k, at:at + m], start=(k == 0), stop=(k == KD - 1))
                for g, src in enumerate((e.oaT, e.obT)):
                    for k in range(HP):
                        mm = pe.matmul(banks[x][:, 2 + g, 0:m], w[:, b, 16 + 4 * g + k, :], src[:, k, at:at + m],
                                       start=(k == 0), stop=(k == HP - 1))
                mm.then_inc(made, 1)
            loop(pe, body)

        @block.scalar
        def _(act):
            def body(j, b, i, x, c, at, m, n):
                act.wait_ge(made, n + 1)
                act.wait_ge(summed, n + 1)
                act.activation(gate[:, x, :, 0:m], banks[x][:, 0:2, 0:m], ACT.Sigmoid).then_inc(gated, 1)
            loop(act, body)

        @block.vector
        def _(dve):
            def body(j, b, i, x, c, at, m, n):
                dve.wait_ge(gated, n + 1)
                dve.wait_ge(made, n + 1)
                dve.wait_ge(summed, n + 2)
                dve.tensor_tensor(part[:, :, 0:m], gate[:, x, :, 0:m], banks[x][:, 2:4, 0:m], ALU.mult).then_inc(prods, 1)
                dve.wait_ge(prods, n + 1)
                dve.tensor_tensor(e.mixedT[:, ds(j, 1), at:at + m].squeeze(1), part[:, 0, 0:m], part[:, 1, 0:m],
                                  ALU.add).then_inc(summed, 1)
            loop(dve, body)


def stage_out_and_route(e):
    nc, a, sem = e.nc, e.a, e.sem
    st = e.steps["dve"]
    w_loaded = sem("wo_loaded")
    x_loaded, made, added, sq, std, rstd = sem("xr_loaded"), sem("wo_made"), sem("x1_added"), sem("x1_sq"), sem("x1_std"), sem("x1_rstd")
    h_ready, h_stored, h_turned, hT_ready, logits_made, logits_kept = (
        sem("h_ready"), [sem(f"h_stored{b}") for b in range(2)], sem("h_turned"), sem("hT_ready"), sem("logits_made"), sem("logits_kept"))
    r_exp_in, r_exped, r_exp2_in, r_exped2, m_ready, ranked = (sem("r_exp_in"), sem("r_exped"), sem("r_exp2_in"),
                                                              sem("r_exped2"), sem("r_m_ready"), sem("r_ranked"))
    ent_ready, table_set, scattered, table_zero = sem("ent_ready"), sem("table_set"), sem("scattered"), sem("table_zero")
    with memory(e) as (sb, ps), nc.Block() as block:
        wo, wr = sb("wo", [P, KD, D]), sb("wr", [P, KD, GR + NE])
        xt = e.x1
        hx = sb("hx_t", [P, 2, D])
        hT = sb("hT", [P, 2, KD, P])
        junk = sb("h_junk", [P, D])
        stat = sb("h_stat", [P, 3, NTT])
        lg = sb("logits", [P, NTT, GR + NE])
        n9 = lambda name, k=NE: sb(f"r_{name}", [P, NTT, k])
        gd, eq, ohg, bias4 = n9("gd", GR), n9("eq", GR), n9("ohg", GR), n9("bias4", GR)
        el, cand, o1, o2, both, prev, tmp = (n9(x) for x in "el cand o1 o2 both prev tmp".split())
        s = sb("r_small", [P, 16, NTT])
        slot = sb("slot", [P, NTT, 2], I32)
        ent = sb("ent", [P, NTT, 2, 4], I32)
        total = sb("r_total", [P, NE + 1])
        empty = sb("empty", [P, NE * e.CAP // P * 4], I32)
        xp = [ps(f"x1_p{b}", [P, 2, 512]) for b in range(2)]
        hp = ps("h_p", [P, KD, P])
        lp = ps("lg_p", [P, 512])
        rp = ps("rank_p", [P, 512])

        @block.sync
        def _(sp):
            sp.dma_start(wo[:], a["w_o"].rearrange("(k p) n -> p k n", p=P)).then_inc(w_loaded, 16)
            sp.dma_start(wr[:], a["w_route"]).then_inc(w_loaded, 16)
            sp.dma_start(xt[:], a["x"].rearrange("(t p) d -> p t d", p=P)).then_inc(x_loaded, 16)
            sp.wait_ge(table_zero, 1)
            sp.dma_start(e.table_d.rearrange("(p n) c -> p (n c)", p=P), empty[:]).then_inc(table_set, 16)
            for t in range(NTT):
                sp.wait_ge(h_ready, t + 1)
                sp.dma_start(e.h_d[t * P:(t + 1) * P, :], hx[:, t % 2]).then_inc(h_stored[t % 2], 16)

        @block.tensor
        def _(pe):
            pe.wait_ge(w_loaded, 32)

            def out(t):
                n = min(P, NT - t * P)
                if t >= 2:
                    pe.wait_ge(added, t - 1)
                for k in range(KD):
                    for c in range(2):
                        mm = pe.matmul(xp[t % 2][0:n, c], e.mixedT[:, k, t * P:t * P + n], wo[:, k, c * 512:(c + 1) * 512],
                                       start=(k == 0), stop=(k == KD - 1))
                mm.then_inc(made, 1)

            def route(t):
                pe.wait_ge(h_ready, t + 1)
                if t:
                    pe.wait_ge(hT_ready, t)
                for k in range(KD):
                    mm = pe.transpose(hp[:, k], hx[:, t % 2, k * P:(k + 1) * P], e.c("ident"))
                mm.then_inc(h_turned, 1)
                pe.wait_ge(hT_ready, t + 1)
                if t:
                    pe.wait_ge(logits_kept, t)
                for k in range(KD):
                    mm = pe.matmul(lp[:, 0:GR + NE], hT[:, t % 2, k], wr[:, k], start=(k == 0), stop=(k == KD - 1))
                mm.then_inc(logits_made, 1)
            out(0)
            for t in range(NTT):
                if t + 1 < NTT:
                    out(t + 1)
                route(t)
            pe.wait_ge(m_ready, 1)
            pe.matmul(rp[:, 0:NTT * NE], e.c("before"), both[:].rearrange("p t e -> p (t e)"), start=True, stop=False)
            pe.matmul(rp[:, 0:NTT * NE], e.ones[:, 0:P], prev[:].rearrange("p t e -> p (t e)"), start=False, stop=True)
            pe.matmul(rp[:, 480:480 + NE], e.ones[:, 0:P], total[:, 0:NE], start=True, stop=True).then_inc(ranked, 1)

        @block.scalar
        def _(act):
            for t in range(NTT):
                act.wait_ge(added, t + 1)
                act.activation(junk[:], e.x1[:, t], ACT.Square, accum_out=stat[:, 0, t:t + 1]).then_inc(sq, 1)
                act.wait_ge(sq, t + 1)
                act.activation(stat[:, 1, t:t + 1], stat[:, 0, t:t + 1], ACT.Sqrt, scale=1.0 / D,
                               bias=e.eps[:, 0:1]).then_inc(std, 1)
            act.wait_ge(r_exp_in, 1)
            act.activation(gd[:], gd[:], ACT.Exp).then_inc(r_exped, 1)
            act.wait_ge(r_exp2_in, 1)
            act.activation(s[:, 8], s[:, 7], ACT.Exp).then_inc(r_exped2, 1)

        @block.gpsimd
        def _(pool):
            pool.memset(empty[:], 1 << 24).then_inc(table_zero, 1)
            pool.wait_ge(ent_ready, 1)
            pool.wait_ge(table_set, 16)
            for t in range(NTT):
                for j in range(2):
                    pool.indirect_dma_start(out=e.table_d, out_offset=bass.IndirectOffsetOnAxis(ap=slot[:, t, j:j + 1], axis=0),
                                            in_=ent[:, t, j], in_offset=None, bounds_check=NE * e.CAP - 1,
                                            oob_is_err=False).then_inc(scattered, 16)
            pool.wait_ge(scattered, 16 * 2 * NTT)
            for b in range(2):
                pool.wait_ge(h_stored[b], 16 * ((NTT + 1 - b) // 2))

        @block.vector
        def _(dve):
            dve.wait_ge(x_loaded, 16)

            def add(t):
                n = min(P, NT - t * P)
                dve.wait_ge(made, t + 1)
                dve.tensor_tensor(e.x1[0:n, t], e.x1[0:n, t], xp[t % 2][0:n].rearrange("p c n -> p (c n)"),
                                  ALU.add).then_inc(added, 1)

            def norm(t):
                dve.wait_ge(std, t + 1)
                dve.reciprocal(stat[:, 2, t:t + 1], stat[:, 1, t:t + 1]).then_inc(rstd, 1)
                dve.wait_ge(rstd, t + 1)
                if t >= 2:
                    dve.wait_ge(h_stored[t % 2], 16 * (t // 2))
                dve.tensor_scalar(hx[:, t % 2], e.x1[:, t], stat[:, 2, t:t + 1], None, ALU.mult).then_inc(h_ready, 1)
                dve.wait_ge(h_turned, t + 1)
                dve.tensor_tensor(hT[:, t % 2], hp[:], e.v("norm_ffn").unsqueeze(2).to_broadcast([P, KD, P]),
                                  ALU.mult).then_inc(hT_ready, 1)
                dve.wait_ge(logits_made, t + 1)
                dve.tensor_copy(lg[:, t], lp[:, 0:GR + NE]).then_inc(logits_kept, 1)
            add(0)
            for t in range(NTT):
                if t + 1 < NTT:
                    add(t + 1)
                norm(t)
            dve.wait_ge(logits_kept, NTT)
            G, E = lg[:, :, 0:GR], lg[:, :, GR:]
            w4 = lambda x: x.unsqueeze(2).to_broadcast([P, NTT, GR])
            w32 = lambda x: x.unsqueeze(2).to_broadcast([P, NTT, NE])
            iota = lambda k: e.c("expert_id")[:, 0:k].unsqueeze(1).to_broadcast([P, NTT, k])
            by_group = lambda x: x.rearrange("p t (g k) -> p (t g) k", g=GR)
            do = lambda ins: st.then(dve, ins)
            do(dve.reduce_max(s[:, 0], G, X))
            dve.tensor_tensor(gd[:], G, w4(s[:, 0]), ALU.subtract).then_inc(r_exp_in, 1)
            do(dve.tensor_tensor(eq[:], G, w4(s[:, 0]), ALU.is_equal))
            do(dve.scalar_tensor_tensor(eq[:], eq[:], -99.0, iota(GR), ALU.mult, ALU.add))
            do(dve.tensor_reduce(s[:, 1], eq[:], X, ALU.min))
            do(dve.tensor_tensor(ohg[:], eq[:], w4(s[:, 1]), ALU.is_equal))
            dve.wait_ge(r_exped, 1)
            do(dve.reduce_sum(s[:, 2], gd[:], X))
            do(dve.reciprocal(s[:, 2], s[:, 2]))
            do(dve.tensor_scalar(bias4[:], ohg[:], -NEG, NEG, ALU.mult, ALU.add))
            wide = lambda x: x.rearrange("p t g -> p (t g)").unsqueeze(2).to_broadcast([P, NTT * GR, EPG])
            do(dve.tensor_copy(el[:], E))
            do(dve.tensor_tensor(by_group(el[:]), by_group(el[:]), wide(ohg[:]), ALU.mult))
            do(dve.tensor_tensor(by_group(el[:]), by_group(el[:]), wide(bias4[:]), ALU.add))

            def first_largest(at, onehot):
                do(dve.reduce_max(s[:, at], el[:], X))
                do(dve.tensor_tensor(cand[:], el[:], w32(s[:, at]), ALU.is_equal))
                do(dve.scalar_tensor_tensor(cand[:], cand[:], -99.0, iota(NE), ALU.mult, ALU.add))
                do(dve.tensor_reduce(s[:, at + 1], cand[:], X, ALU.min))
                do(dve.tensor_tensor(onehot[:], cand[:], w32(s[:, at + 1]), ALU.is_equal))
            first_largest(3, o1)
            do(dve.scalar_tensor_tensor(el[:], o1[:], 3 * NEG, el[:], ALU.mult, ALU.add))
            first_largest(5, o2)
            dve.tensor_tensor(s[:, 7], s[:, 5], s[:, 3], ALU.subtract).then_inc(r_exp2_in, 1)
            dve.wait_ge(r_exped2, 1)
            do(dve.tensor_scalar(s[:, 9], s[:, 8], 1.0, None, ALU.add))
            do(dve.reciprocal(s[:, 9], s[:, 9]))
            do(dve.tensor_tensor(s[:, 9], s[:, 9], s[:, 2], ALU.mult))
            do(dve.tensor_tensor(s[:, 10], s[:, 9], s[:, 8], ALU.mult))
            last = slice(NTT - 1, NTT)
            for o in (o1, o2):
                do(dve.tensor_scalar(o[:, NTT - 1], o[:, NTT - 1], e.c("is_sample"), None, ALU.mult))
            do(dve.tensor_tensor(both[:], o1[:], o2[:], ALU.add))
            do(dve.memset(prev[:, 0], 0.0))
            for t in range(NTT - 1):
                do(dve.tensor_tensor(prev[:, t + 1], prev[:, t], both[:, t], ALU.add))
            dve.tensor_tensor(total[:, 0:NE], prev[:, NTT - 1], both[:, NTT - 1], ALU.add).then_inc(m_ready, 1)
            dve.wait_ge(ranked, 1)
            rank = rp[:, 0:NTT * NE].rearrange("p (t e) -> p t e", t=NTT)
            for j, (o, at) in enumerate(((o1, 4), (o2, 6))):
                do(dve.tensor_tensor(tmp[:], o[:], rank, ALU.mult))
                do(dve.reduce_sum(s[:, 11 + j], tmp[:], X))
                do(dve.tensor_scalar(s[:, at], s[:, at], 99.0, float(e.CAP), ALU.add, ALU.mult))
                do(dve.tensor_tensor(s[:, 11 + j], s[:, 11 + j], s[:, at], ALU.add))
                do(dve.scalar_tensor_tensor(s[:, 11 + j, last], s[:, 11 + j, last], e.c("is_sample"), e.c("beyond"), ALU.mult, ALU.add))
                do(dve.tensor_copy(slot[:, :, j], s[:, 11 + j]))
                do(dve.tensor_copy(ent[:, :, j, 0], e.c("token")))
                do(dve.tensor_scalar(s[:, 13], e.c("token"), 2.0, float(j), ALU.mult, ALU.add))
                do(dve.tensor_copy(ent[:, :, j, 1], s[:, 13]))
                do(dve.tensor_copy(ent[:, :, j, 2].bitcast(F32), s[:, 9 + j]))
                do(dve.tensor_copy(ent[:, :, j, 3], e.c("token")))
            do(dve.tensor_copy(total[:, 0:NE], rp[:, 480:480 + NE]))
            do(dve.reduce_max(total[:, NE:NE + 1], total[:, 0:NE], X))
            dve.tensor_copy(e.count[:], total[0:1, :]).then_inc(ent_ready, 1)


def stage_moe(e):
    nc, a, sem = e.nc, e.a, e.sem
    e.mix_mem.close()
    NW = 4
    w_loaded, gathered, scattered = ([sem(f"moe_{n}{b}") for b in range(NW)] for n in ("w_loaded", "gathered", "scattered"))
    names = "ent_loaded more_loaded turned hT_act hT_dve made_gu silu acted made_y y_dve y_act zero go placed0 placed1"
    q = {n: sem(f"moe_{n}") for n in names.split()}
    with memory(e) as (sb, ps), nc.Block() as block:
        wgu, wd = sb("wgu", [P, NW, KD, 2 * DE]), sb("wd", [P, NW, 2, D])
        ent = sb("moe_ent", [R, NE, 4], I32)
        more_ent, place = sb("moe_more_ent", [R, 4], I32), sb("moe_place", [R, NW, 2], I32)
        hx, y = sb("moe_hx", [R, NW, D]), sb("moe_y", [R, NW, D])
        hT = e.beside_x1[:, 0:2 * KD * R].rearrange("p (d k n) -> p d k n", d=2, k=KD)
        act_g, aT = (e.beside_x1[:, (2 * KD + 4 * x) * R:(2 * KD + 4 * x + 4) * R].rearrange("p (d k n) -> p d k n", d=2, k=2)
                     for x in range(2))
        hp = ps("moe_hp", [P, 2, 512])
        gu = [ps(f"moe_gu{b}", [P, 512]) for b in range(2)]
        yp = [ps(f"moe_yp{b}", [R, 2, 512]) for b in range(2)]
        gut = [g[:, 0:4 * R].rearrange("p (t n) -> p t n", t=4) for g in gu]
        hpt = hp[:, :, 0:KD // 2 * R].rearrange("p c (k n) -> p c k n", n=R)
        half = KD // 2

        def after(eng, s, v):
            if not isinstance(v, int) or v > 0:
                eng.wait_ge(s, v)

        def load_weights(sp, u, ex):
            sp.dma_start(wgu[:, u], a["we_gu"][ds(ex, 1)].squeeze(0)).then_inc(w_loaded[u], 16)
            sp.dma_start(wd[:, u], a["we_down"][ds(ex, 1)].squeeze(0)).then_inc(w_loaded[u], 16)

        def go(pool):
            pool.sem_inc(q["go"], 1)

        def at_fixed_place(pool, n, u, c):
            if c:
                pool.wait_ge(q["y_dve"], n + 1)
                go(pool)
            pool.tensor_copy(place[:, u, c:c + 1], index(n, c)).then_inc(q[f"placed{c}"], 1)
            pool.wait_ge(q[f"placed{c}"], n + 1)
            go(pool)
            return place[:, u, c:c + 1]

        def gather(pool, u, token):
            pool.indirect_dma_start(out=hx[:, u], out_offset=None, in_=e.h_d,
                                    in_offset=bass.IndirectOffsetOnAxis(ap=token, axis=0),
                                    bounds_check=NT - 1, oob_is_err=False).then_inc(gathered[u], 16)

        def scatter(pool, n, u, row):
            pool.wait_ge(q["y_dve"], n + 1)
            pool.wait_ge(q["y_act"], n + 1)
            go(pool)
            pool.indirect_dma_start(out=e.y2_d, out_offset=bass.IndirectOffsetOnAxis(ap=row, axis=0),
                                    in_=y[:, u], in_offset=None, bounds_check=2 * NT - 1,
                                    oob_is_err=False).then_inc(scattered[u], 16)

        def pe_turn(pe, n, i, u):
            pe.wait_ge(gathered[u], 16 * (i + 1))
            after(pe, q["hT_act"], n)
            after(pe, q["hT_dve"], n)
            for k in range(KD):
                mm = pe.transpose(hpt[:, k // half, k % half], hx[:, u, k * P:(k + 1) * P], e.c("ident")[0:R, 0:R])
            mm.then_inc(q["turned"], 1)

        def pe_gate_up(pe, n, i, u, d):
            pe.wait_ge(w_loaded[u], 32 * (i + 1))
            pe.wait_ge(q["hT_act"], n + 1)
            pe.wait_ge(q["hT_dve"], n + 1)
            after(pe, q["acted"], n - 1)
            for t in range(4):
                for k in range(KD):
                    mm = pe.matmul(gut[d][:, t], wgu[:, u, k, t * P:(t + 1) * P], hT[:, d, k], start=(k == 0), stop=(k == KD - 1))
            mm.then_inc(q["made_gu"], 1)

        def pe_down(pe, n, u, d):
            pe.wait_ge(q["acted"], n + 1)
            after(pe, q["y_act"], n - 1)
            after(pe, q["y_dve"], n - 1)
            for c in range(2):
                for k in range(2):
                    mm = pe.matmul(yp[d][:, c], aT[:, d, k], wd[:, u, k, c * 512:(c + 1) * 512], start=(k == 0), stop=(k == 1))
            mm.then_inc(q["made_y"], 1)

        def gain(c):
            return e.v("norm_ffn")[:, c * half:(c + 1) * half].unsqueeze(2).to_broadcast([P, half, R])

        def hT_half(eng, n, d, c, done):
            eng.wait_ge(q["turned"], n + 1)
            after(eng, q["made_gu"], n - 1)
            if c:
                eng.tensor_tensor(hT[:, d, half:], hpt[:, 1], gain(1), ALU.mult).then_inc(done, 1)
            else:
                for k in range(half):
                    ins = eng.activation(hT[:, d, k], hpt[:, 0, k], ACT.Copy, scale=e.v("norm_ffn")[:, k:k + 1])
                ins.then_inc(done, 1)

        def act_silu(act, n, d):
            act.wait_ge(q["made_gu"], n + 1)
            after(act, q["acted"], n - 1)
            act.activation(act_g[:, d], gut[d][:, 0:2], ACT.Silu).then_inc(q["silu"], 1)

        def act_y(act, n, i, u, d, weight):
            act.wait_ge(q["made_y"], n + 1)
            after(act, scattered[u], 16 * i)
            act.activation(y[:, u, 0:512], yp[d][:, 0], ACT.Copy, scale=weight).then_inc(q["y_act"], 1)

        def dve_act(dve, n, d):
            dve.wait_ge(q["silu"], n + 1)
            after(dve, q["made_y"], n - 1)
            dve.tensor_tensor(aT[:, d], act_g[:, d], gut[d][:, 2:4], ALU.mult).then_inc(q["acted"], 1)

        def dve_y(dve, n, i, u, d, weight):
            dve.wait_ge(q["made_y"], n + 1)
            after(dve, scattered[u], 16 * i)
            dve.tensor_scalar(y[:, u, 512:D], yp[d][:, 1], weight, None, ALU.mult).then_inc(q["y_dve"], 1)

        def first_round(eng, body):
            for u in range(NW):
                body(u, 0, u, u % 2)
            with eng.Fori(1, NE // NW - 1) as i:
                for u in range(NW):
                    body(i * NW + u, i, u, u % 2)
            for u in range(NW):
                body(NE - NW + u, NE // NW - 1, u, u % 2)

        def more_rounds(eng, body):
            longest = eng.value_load(e.count[0:1, NE:NE + 1], min_val=0, max_val=NT)
            with eng.Fori(1, e.CAP // R) as r:
                with eng.If(longest > r * R):
                    with eng.Fori(0, NE) as ex:
                        body(r * NE + ex, r * NE + ex + (NE // NW - NE), ex, r)

        index = lambda n, c: ent[:, ds(n, 1), c:c + 1].squeeze(1)
        weight = lambda n: index(n, 2).bitcast(F32)
        more_weight = more_ent[:, 2:3].bitcast(F32)

        @block.sync
        def _(sp):
            sp.dma_start(ent[:], e.table_d.rearrange("(e c) k -> c e k", e=NE)[0:R]).then_inc(q["ent_loaded"], 16)
            for u in range(NW):
                load_weights(sp, u, u)
            with sp.Fori(0, NE // NW - 1) as i:
                for u in range(NW):
                    sp.wait_ge(q["made_y"], i * NW + u + 1)
                    load_weights(sp, u, i * NW + u + NW)

            def more(n, i, ex, r):
                sp.wait_ge(q["made_y"], n)
                load_weights(sp, 0, ex)
            more_rounds(sp, more)

        @block.gpsimd
        def _(pool):
            pool.memset(hx[:], 0.0).then_inc(q["zero"], 1)
            pool.wait_ge(q["zero"], 1)
            pool.wait_ge(q["ent_loaded"], 16)
            for u in range(NW):
                gather(pool, u, at_fixed_place(pool, u, u, 0))

            def first(n, i, u, d):
                if not isinstance(n, int) or n + NW < NE:
                    pool.wait_ge(q["turned"], n + 1)
                    go(pool)
                    gather(pool, u, at_fixed_place(pool, n + NW, u, 0))
                scatter(pool, n, u, at_fixed_place(pool, n, u, 1))
            first_round(pool, first)
            for u in range(NW):
                pool.wait_ge(scattered[u], 16 * (NE // NW))

            def more(n, i, ex, r):
                pool.dma_start(more_ent[:], e.table_d[ds(ex * e.CAP + r * R, R), :]).then_inc(q["more_loaded"], 16)
                pool.wait_ge(q["more_loaded"], 16 * (n - NE + 1))
                go(pool)
                gather(pool, 0, more_ent[:, 0:1])
                scatter(pool, n, 0, more_ent[:, 1:2])
                pool.wait_ge(scattered[0], 16 * (i + 1))
                go(pool)
            more_rounds(pool, more)

        @block.tensor
        def _(pe):
            pe_turn(pe, 0, 0, 0)

            def first(n, i, u, d):
                pe_gate_up(pe, n, i, u, d)
                if not isinstance(n, int) or n + 1 < NE:
                    pe_turn(pe, n + 1, i + (u + 1) // NW, (u + 1) % NW)
                pe_down(pe, n, u, d)
            first_round(pe, first)

            def more(n, i, ex, r):
                pe_turn(pe, n, i, 0)
                pe_gate_up(pe, n, i, 0, 0)
                pe_down(pe, n, 0, 0)
            more_rounds(pe, more)

        @block.scalar
        def _(act):
            hT_half(act, 0, 0, 0, q["hT_act"])

            def first(n, i, u, d):
                act_silu(act, n, d)
                if not isinstance(n, int) or n + 1 < NE:
                    hT_half(act, n + 1, 1 - d, 0, q["hT_act"])
                act_y(act, n, i, u, d, weight(n))
            first_round(act, first)

            def more(n, i, ex, r):
                hT_half(act, n, 0, 0, q["hT_act"])
                act_silu(act, n, 0)
                act_y(act, n, i, 0, 0, more_weight)
            more_rounds(act, more)

        @block.vector
        def _(dve):
            hT_half(dve, 0, 0, 1, q["hT_dve"])

            def first(n, i, u, d):
                dve_act(dve, n, d)
                if not isinstance(n, int) or n + 1 < NE:
                    hT_half(dve, n + 1, 1 - d, 1, q["hT_dve"])
                dve_y(dve, n, i, u, d, weight(n))
            first_round(dve, first)

            def more(n, i, ex, r):
                hT_half(dve, n, 0, 1, q["hT_dve"])
                dve_act(dve, n, 0)
                dve_y(dve, n, i, 0, 0, more_weight)
            more_rounds(dve, more)


def stage_final(e):
    nc, a, sem = e.nc, e.a, e.sem
    NBUF = 4
    loaded = [sem(f"y2_loaded{b}") for b in range(NBUF)]
    stored = [sem(f"y_stored{b}") for b in range(2)]
    gain_loaded, sum1, sum2, sq, std, rstd, out_ready = (
        sem("gain_loaded"), sem("f_sum1"), sem("f_sum2"), sem("f_sq"), sem("f_std"), sem("f_rstd"), sem("f_out"))
    with memory(e) as (sb, ps), nc.Block() as block:
        y2 = sb("y2_tile", [P, NBUF, 2 * D])
        gain, junk = sb("gain", [P, D]), sb("f_junk", [P, D])
        out = sb("y_out", [P, 2, D])
        stat = sb("f_stat", [P, 3, NTT])

        @block.sync
        def _(sp):
            sp.dma_start(gain[:], a["norm_final"].to_broadcast([P, D])).then_inc(gain_loaded, 16)
            for t in range(NTT):
                n = min(P, NT - t * P)
                if t >= NBUF:
                    sp.wait_ge(sum2, t - NBUF + 1)
                sp.dma_start(y2[0:n, t % NBUF, :], e.y2_d.rearrange("(t j) d -> t (j d)", j=2)[t * P:t * P + n, :]).then_inc(loaded[t % NBUF], 16)

        @block.gpsimd
        def _(pool):
            for t in range(NTT):
                n = min(P, NT - t * P)
                pool.wait_ge(out_ready, t + 1)
                pool.dma_start(a["y"][t * P:t * P + n, :], out[0:n, t % 2]).then_inc(stored[t % 2], 16)
            for b in range(2):
                pool.wait_ge(stored[b], 16 * ((NTT + 1 - b) // 2))

        @block.scalar
        def _(act):
            for t in range(NTT):
                n = min(P, NT - t * P)
                act.wait_ge(sum2, t + 1)
                act.activation(junk[0:n], e.x1[0:n, t], ACT.Square, accum_out=stat[0:n, 0, t:t + 1]).then_inc(sq, 1)
                act.wait_ge(sq, t + 1)
                act.activation(stat[0:n, 1, t:t + 1], stat[0:n, 0, t:t + 1], ACT.Sqrt, scale=1.0 / D,
                               bias=e.eps[0:n, 0:1]).then_inc(std, 1)

        @block.vector
        def _(dve):
            dve.wait_ge(gain_loaded, 16)

            def add(t):
                n = min(P, NT - t * P)
                dve.wait_ge(loaded[t % NBUF], 16 * (t // NBUF + 1))
                dve.tensor_tensor(e.x1[0:n, t], e.x1[0:n, t], y2[0:n, t % NBUF, 0:D], ALU.add).then_inc(sum1, 1)
                dve.wait_ge(sum1, t + 1)
                dve.tensor_tensor(e.x1[0:n, t], e.x1[0:n, t], y2[0:n, t % NBUF, D:], ALU.add).then_inc(sum2, 1)

            add(0)
            for t in range(NTT):
                n = min(P, NT - t * P)
                if t + 1 < NTT:
                    add(t + 1)
                dve.wait_ge(std, t + 1)
                dve.reciprocal(stat[0:n, 2, t:t + 1], stat[0:n, 1, t:t + 1]).then_inc(rstd, 1)
                dve.wait_ge(rstd, t + 1)
                if t >= 2:
                    dve.wait_ge(stored[t % 2], 16 * (t // 2))
                dve.scalar_tensor_tensor(out[0:n, t % 2], e.x1[0:n, t], stat[0:n, 2, t:t + 1], gain[0:n], ALU.mult,
                                         ALU.mult).then_inc(out_ready, 1)


STAGES = [stage_norm, stage_fox_project, stage_fox_prepare, stage_fox_prompt, stage_fox_sample,
          stage_rwkv_project, stage_rwkv_prepare, stage_rwkv_scan, stage_rwkv_sample,
          stage_mix, stage_out_and_route, stage_moe, stage_final]


def layout(inputs):
    f = {n: np.asarray(v) for n, v in inputs.items()}
    a = {}
    a["x"] = np.concatenate([f["x_prompt"].reshape(SEQ, D), f["x_sample"].reshape(NS, D),
                             np.zeros((P - NS, D), np.float32)])
    w = f["w_in"][0]
    order = np.concatenate([w[:, 0:3 * W], w[:, FOX:]], 1)
    a["w_in"] = np.ascontiguousarray(order.reshape(KD, P, -1, P).transpose(2, 1, 0, 3))
    a["w_f"] = np.ascontiguousarray(w[:, 3 * W:FOX].reshape(KD, P, H).transpose(1, 0, 2))
    vec = np.zeros((P, NVEC), np.float32)
    for name, n in VEC_FIELDS:
        src = f[{"mu": "mu_rw"}.get(name, name)].reshape(-1)
        at = VEC_AT[name][0]
        if name == "b_f":
            vec[:H, at] = src
        else:
            vec[:, at:at + n] = src.reshape(n, P).T
    a["vec"] = vec
    a["consts"] = np.ascontiguousarray(np.concatenate([CONSTS[n] for n in CONST_AT], 1))
    for name in ("cache_k", "cache_v", "cache_logf", "w2", "a2", "g2", "w_o"):
        a[name] = f[name][0]
    pab = np.stack([f["p_a"][0], f["p_b"][0]]).reshape(2, HP, P, KD, P)
    a["p_ab"] = np.ascontiguousarray(pab.transpose(3, 2, 0, 1, 4).reshape(KD, P, 2 * HP, P))
    a["page_table"] = f["page_table"].reshape(1, NB * NPG)
    a["state"] = f["state_wkv"][0]
    a["shiftT"] = np.ascontiguousarray(f["state_shift"][0].reshape(NB, RW // P, P).transpose(2, 1, 0))
    a["norm_final"] = f["norm_final"].reshape(1, D)
    a["w_route"] = np.ascontiguousarray(np.concatenate([f["w_grp"][0], f["w_exp"][0]], 1)
                                        .reshape(KD, P, GR + NE).transpose(1, 0, 2))
    gu = np.concatenate([f["we_gate"][0], f["we_up"][0]], 2)
    a["we_gu"] = np.ascontiguousarray(gu.reshape(NE, KD, P, 2 * DE).transpose(0, 2, 1, 3))
    a["we_down"] = np.ascontiguousarray(f["we_down"][0].reshape(NE, 2, P, D).transpose(0, 2, 1, 3))
    return a


OUTS = {
    "y": [NTT * P, D], "k_out": [NT, W], "v_out": [NT, W], "logf_out": [NT, H],
    "wkv_prompt": [P, HP, DH], "wkv_sample": [NB, H, DH, DH],
    "shift_out": [P, RW // P, NB + 1],
}


def program(nc, arrays, upto=99):
    a = {}
    for n, v in arrays.items():
        a[n] = nc.dram_tensor(f"in_{n}", v.shape, mybir.dt.from_np(v.dtype), kind="ExternalInput").ap()
    for n, shape in OUTS.items():
        a[n] = nc.dram_tensor(f"out_{n}", shape, F32, kind="ExternalOutput").ap()
    build(nc, a, upto)


def kernel(**inputs):
    import concourse.bacc as bacc
    from concourse.bass_utils import run_bass_kernel_spmd

    arrays = layout(inputs)
    nc = bacc.Bacc("TRN2", target_bir_lowering=False, num_devices=1)
    program(nc, arrays)
    r = run_bass_kernel_spmd(nc, [{f"in_{n}": v for n, v in arrays.items()}], core_ids=[0]).results[0]
    o = {n: r[f"out_{n}"] for n in OUTS}
    split = lambda x, *tail: (x[:SEQ].reshape(1, 1, SEQ, *tail), x[SEQ:NT].reshape(1, NB, TS, *tail))
    kp, ks = split(o["k_out"], H, DH)
    vp, vs = split(o["v_out"], H, DH)
    fp, fs = split(o["logf_out"], H)
    y = o["y"]
    state = o["wkv_prompt"].reshape(2, DH, HP, DH).transpose(2, 0, 3, 1).reshape(1, 1, H, DH, DH)
    shift = o["shift_out"].transpose(2, 1, 0).reshape(NB + 1, RW)
    return (y[:SEQ].reshape(1, SEQ, D), y[SEQ:NT].reshape(NB, TS, D), kp, vp, fp,
            state, shift[0].reshape(1, 1, RW), ks, vs, fs,
            o["wkv_sample"].reshape(1, NB, H, DH, DH), shift[1:].reshape(1, NB, RW))
```
